# Optimizing a Trainium2 kernel written in Bass

```python
import jax, jax.numpy as jnp
from jax import lax
import numpy as np

D_MODEL = 1024
BATCH = 1
SEQ = 1024
DEPTH = 1

HEAD_DIM = 64
N_ATT_HEADS = 6
N_KV_GROUPS = 2
ATT_WIDTH = N_ATT_HEADS * HEAD_DIM
KV_WIDTH = N_KV_GROUPS * HEAD_DIM
N_IDX_HEADS = 8
IDX_DIM = 32
TOPK_MAX = 256
Q_BLOCK = 128
CONV_CHANNELS = 384
SHORT_CONV_K = 3
N_CROSS_HEADS = 4
CROSS_WIDTH = N_CROSS_HEADS * HEAD_DIM
MEM_LEN = 256
N_BRANCHES = 3
D_FF = 2816
FFN_CONV_K = 3
ROPE_THETA = 500000.0
ROPE_FRACTION = 4
NORM_EPS = 1e-6

PROJ_SIZES = (ATT_WIDTH, KV_WIDTH, KV_WIDTH, N_IDX_HEADS * IDX_DIM, IDX_DIM, N_IDX_HEADS,
              3 * CONV_CHANNELS, CROSS_WIDTH, N_BRANCHES * D_MODEL)
PROJ_WIDTH = sum(PROJ_SIZES)


def rms_norm(x, g):
    xf = x.astype(jnp.float32)
    y = xf * lax.rsqrt(jnp.mean(xf * xf, axis=-1, keepdims=True) + NORM_EPS)
    return (y * g.astype(jnp.float32)).astype(x.dtype)

def split_cols(a, sizes):
    out, off = [], 0
    for n in sizes:
        out.append(a[..., off:off + n])
        off += n
    return out

def rope_tables(positions, rot_dim, dtype):
    half = rot_dim // 2
    inv_freq = ROPE_THETA ** (-jnp.arange(half, dtype=jnp.float32) / half)
    ang = positions.astype(jnp.float32)[:, None] * inv_freq[None, :]
    return jnp.cos(ang).astype(dtype), jnp.sin(ang).astype(dtype)

def partial_rope(x, cos, sin):
    half = cos.shape[-1]
    shape = (1, cos.shape[0]) + (1,) * (x.ndim - 3) + (half,)
    c, s = cos.reshape(shape), sin.reshape(shape)
    x1, x2, rest = x[..., :half], x[..., half:2 * half], x[..., 2 * half:]
    return jnp.concatenate([x1 * c - x2 * s, x2 * c + x1 * s, rest], axis=-1)

def causal_dwconv(u, w):
    k, c = w.shape
    return lax.conv_general_dilated(u, w[:, None, :].astype(u.dtype), window_strides=(1,),
                                    padding=[(k - 1, 0)],
                                    dimension_numbers=("NWC", "WIO", "NWC"),
                                    feature_group_count=c)

def dsa_attention(q, k, v, qi, ki, wi):
    b, s = q.shape[:2]
    topk = min(TOPK_MAX, s // 4)
    blk = min(Q_BLOCK, s)
    nb = s // blk
    rep = N_ATT_HEADS // N_KV_GROUPS
    idx_scale = (N_IDX_HEADS * IDX_DIM) ** -0.5
    att_scale = HEAD_DIM ** -0.5
    key_pos = jnp.arange(s)
    gather = jax.vmap(lambda a, i: a[i])

    def to_blocks(a):
        return jnp.moveaxis(a.reshape((b, nb, blk) + a.shape[2:]), 1, 0)

    def one_block(args):
        q_b, qi_b, wi_b, start = args
        qpos = start + jnp.arange(blk)
        causal = key_pos[None, :] <= qpos[:, None]
        rel = jax.nn.relu(jnp.einsum('bqhd,bsd->bqhs', qi_b, ki).astype(jnp.float32))
        score = jnp.einsum('bqh,bqhs->bqs', wi_b.astype(jnp.float32), rel) * idx_scale
        score = jnp.where(causal[None], score, -jnp.inf)
        _, sel = lax.top_k(score, topk)
        k_sel = gather(k, sel)
        v_sel = gather(v, sel)
        qg = q_b.reshape(b, blk, N_KV_GROUPS, rep, HEAD_DIM)
        logits = jnp.einsum('bqgrd,bqkgd->bqgrk', qg, k_sel).astype(jnp.float32) * att_scale
        valid = sel <= qpos[None, :, None]
        logits = jnp.where(valid[:, :, None, None, :], logits, -jnp.inf)
        p = jax.nn.softmax(logits, axis=-1).astype(v.dtype)
        o = jnp.einsum('bqgrk,bqkgd->bqgrd', p, v_sel)
        return o.reshape(b, blk, N_ATT_HEADS * HEAD_DIM)

    starts = jnp.arange(nb) * blk
    out = lax.map(one_block, (to_blocks(q), to_blocks(qi), to_blocks(wi), starts))
    return jnp.moveaxis(out, 0, 1).reshape(b, s, N_ATT_HEADS * HEAD_DIM)

def memory_attention(qc, km, vm):
    b, s = qc.shape[:2]
    logits = jnp.einsum('bshd,bmhd->bhsm', qc, km).astype(jnp.float32) * HEAD_DIM ** -0.5
    p = jax.nn.softmax(logits, axis=-1).astype(vm.dtype)
    return jnp.einsum('bhsm,bmhd->bshd', p, vm).reshape(b, s, CROSS_WIDTH)

def first_inputs(seed: int = 0) -> dict:
    key = jax.random.key(seed)
    ks = jax.random.split(key, 20)

    def w(k, shape, fan_in):
        return jax.random.normal(k, shape, jnp.float32) * fan_in ** -0.5

    def gain(k, shape):
        return 1.0 + 0.02 * jax.random.normal(k, shape, jnp.float32)

    return {
        "x": jax.random.normal(ks[0], (BATCH, SEQ, D_MODEL), jnp.float32),
        "mem": jax.random.normal(ks[1], (BATCH, MEM_LEN, D_MODEL), jnp.float32),
        "g_mix": gain(ks[2], (DEPTH, D_MODEL)),
        "w_in": w(ks[3], (DEPTH, D_MODEL, PROJ_WIDTH), D_MODEL),
        "b_gate": 0.02 * jax.random.normal(ks[4], (DEPTH, N_BRANCHES * D_MODEL), jnp.float32),
        "conv_w_short": w(ks[5], (DEPTH, SHORT_CONV_K, CONV_CHANNELS), SHORT_CONV_K),
        "w_att_out": w(ks[6], (DEPTH, ATT_WIDTH, D_MODEL), ATT_WIDTH),
        "w_conv_out": w(ks[7], (DEPTH, CONV_CHANNELS, D_MODEL), CONV_CHANNELS),
        "w_mem_out": w(ks[8], (DEPTH, CROSS_WIDTH, D_MODEL), CROSS_WIDTH),
        "w_o": w(ks[9], (DEPTH, D_MODEL, D_MODEL), D_MODEL),
        "g_mem": gain(ks[10], (DEPTH, D_MODEL)),
        "w_mem_kv": w(ks[11], (DEPTH, D_MODEL, 2 * CROSS_WIDTH), D_MODEL),
        "g_ffn": gain(ks[12], (DEPTH, D_MODEL)),
        "w_up": w(ks[13], (DEPTH, D_MODEL, 2 * D_FF), D_MODEL),
        "conv_w_ffn": w(ks[14], (DEPTH, FFN_CONV_K, 2 * D_FF), FFN_CONV_K),
        "w_down": w(ks[15], (DEPTH, D_FF, D_MODEL), D_FF),
        "g_final": gain(ks[16], (D_MODEL,)),
    }

def first_block(x, mem, g_mix, w_in, b_gate, conv_w_short, w_att_out, w_conv_out, w_mem_out,
              w_o, g_mem, w_mem_kv, g_ffn, w_up, conv_w_ffn, w_down, g_final):
    b, s, d = x.shape
    m = mem.shape[1]
    positions = jnp.arange(s)
    cos_a, sin_a = rope_tables(positions, HEAD_DIM // ROPE_FRACTION, x.dtype)
    cos_i, sin_i = rope_tables(positions, IDX_DIM // ROPE_FRACTION, x.dtype)

    for l in range(DEPTH):
        h = rms_norm(x, g_mix[l])
        proj = h @ w_in[l]
        q, k, v, qi, ki, wi, conv_in, qc, gate_pre = split_cols(proj, PROJ_SIZES)

        q = partial_rope(q.reshape(b, s, N_ATT_HEADS, HEAD_DIM), cos_a, sin_a)
        k = partial_rope(k.reshape(b, s, N_KV_GROUPS, HEAD_DIM), cos_a, sin_a)
        v = v.reshape(b, s, N_KV_GROUPS, HEAD_DIM)
        qi = partial_rope(qi.reshape(b, s, N_IDX_HEADS, IDX_DIM), cos_i, sin_i)
        ki = partial_rope(ki, cos_i, sin_i)
        y_att = dsa_attention(q, k, v, qi, ki, wi) @ w_att_out[l]

        bg, cg, u = jnp.split(conv_in, 3, axis=-1)
        y_conv = (bg * causal_dwconv(cg * u, conv_w_short[l])) @ w_conv_out[l]

        mem_kv = (rms_norm(mem, g_mem[l]) @ w_mem_kv[l]).reshape(b, m, 2, N_CROSS_HEADS, HEAD_DIM)
        y_mem = memory_attention(qc.reshape(b, s, N_CROSS_HEADS, HEAD_DIM),
                                 mem_kv[:, :, 0], mem_kv[:, :, 1]) @ w_mem_out[l]

        gates = jax.nn.sigmoid(gate_pre + b_gate[l]).reshape(b, s, N_BRANCHES, d)
        merged = gates[:, :, 0] * y_att + gates[:, :, 1] * y_conv + gates[:, :, 2] * y_mem
        x = x + merged @ w_o[l]

        h = rms_norm(x, g_ffn[l])
        up = causal_dwconv(h @ w_up[l], conv_w_ffn[l])
        gate, val = jnp.split(up, 2, axis=-1)
        x = x + (jax.nn.silu(gate) * val) @ w_down[l]

    return rms_norm(x, g_final)


N_MIXERS = 2
N_MEM = 256
MEM_HEADS = 4
MEM_HD = 64
SB_HEADS = 12
SB_HD = 64
SB_BLOCK = 128
HG_HEADS = 6
HG_DK = 128
HG_DV = 128
HG_CHUNK = 64
D_FF_2 = 4 * D_MODEL
D_MIX = SB_HEADS * SB_HD + MEM_HEADS * MEM_HD
SB_PROJ = 3 * SB_HEADS * SB_HD + MEM_HEADS * MEM_HD
HG_PROJ = 2 * HG_HEADS * HG_DK + 2 * HG_HEADS * HG_DV + MEM_HEADS * MEM_HD
N_LAYERS_A = (DEPTH + N_MIXERS - 1) // N_MIXERS
N_LAYERS_B = (DEPTH + N_MIXERS - 2) // N_MIXERS
DN_ALPHA = (2 * DEPTH) ** 0.25
DN_BETA = (8 * DEPTH) ** -0.25
LN_EPS = 1e-5
RMS_EPS = 1e-6


def layer_norm(x, g, b):
    xf = x.astype(jnp.float32)
    mu = jnp.mean(xf, axis=-1, keepdims=True)
    var = jnp.mean(jnp.square(xf - mu), axis=-1, keepdims=True)
    return ((xf - mu) * lax.rsqrt(var + LN_EPS) * g + b).astype(x.dtype)

def split_heads(t, h):
    b, s, _ = t.shape
    return t.reshape(b, s, h, -1).transpose(0, 2, 1, 3)

def merge_heads(t):
    b, h, s, d = t.shape
    return t.transpose(0, 2, 1, 3).reshape(b, s, h * d)

def memory_attention_2(q_mem, mem, w_mem_kv):
    k, v = jnp.split(mem @ w_mem_kv, 2, axis=-1)
    q = split_heads(q_mem, MEM_HEADS)
    k = split_heads(k, MEM_HEADS)
    v = split_heads(v, MEM_HEADS)
    s = jnp.einsum('bhtd,bhmd->bhtm', q, k).astype(jnp.float32) * (MEM_HD ** -0.5)
    p = jax.nn.softmax(s, axis=-1).astype(v.dtype)
    return merge_heads(jnp.einsum('bhtm,bhmd->bhtd', p, v))

def stick_breaking_attention(q, k, v):
    seq = q.shape[2]
    scale = SB_HD ** -0.5
    outs = []
    for blk in range(seq // SB_BLOCK):
        t0 = blk * SB_BLOCK
        t1 = t0 + SB_BLOCK
        qb = q[:, :, t0:t1]
        kb = k[:, :, :t1]
        vb = v[:, :, :t1]
        z = jnp.einsum('bhtd,bhsd->bhts', qb, kb).astype(jnp.float32) * scale
        strict = jnp.arange(t1)[None, :] < jnp.arange(t0, t1)[:, None]
        log_stay = jnp.where(strict, jax.nn.log_sigmoid(-z), 0.0)
        later = lax.cumsum(log_stay, axis=3, reverse=True) - log_stay
        w = jnp.where(strict, jnp.exp(jax.nn.log_sigmoid(z) + later), 0.0)
        outs.append(jnp.einsum('bhts,bhsd->bhtd', w.astype(vb.dtype), vb))
    return jnp.concatenate(outs, axis=2)

def hgrn2_recurrence(q, k, v, log_f):
    b, h, s, dk = q.shape
    dv = v.shape[-1]
    nc = s // HG_CHUNK

    def chunks(t):
        return t.reshape(b, h, nc, HG_CHUNK, t.shape[-1]).transpose(2, 0, 1, 3, 4)

    causal = jnp.tril(jnp.ones((HG_CHUNK, HG_CHUNK), dtype=bool))[:, :, None]

    def step(state, inp):
        qc, kc, vc, gc = inp
        G = jnp.cumsum(gc.astype(jnp.float32), axis=2)
        G_last = G[:, :, -1:]
        o_inter = jnp.einsum('bhck,bhkv->bhcv', qc * jnp.exp(G), state)
        decay = jnp.exp(jnp.where(causal, G[:, :, :, None, :] - G[:, :, None, :, :], -jnp.inf))
        scores = jnp.einsum('bhtk,bhsk,bhtsk->bhts', qc, kc, decay)
        o_intra = jnp.einsum('bhts,bhsv->bhtv', scores, vc)
        k_dec = kc * jnp.exp(G_last - G)
        new_state = jnp.exp(G_last[:, :, 0])[..., None] * state + jnp.einsum('bhck,bhcv->bhkv', k_dec, vc)
        return new_state, o_inter + o_intra

    state0 = jnp.zeros((b, h, dk, dv), jnp.float32)
    _, o = lax.scan(step, state0, (chunks(q), chunks(k), chunks(v), chunks(log_f)))
    return o.transpose(1, 2, 0, 3, 4).reshape(b, h, s, dv)

def hgrn2_mixer(proj, lb, gnorm_g):
    wk = HG_HEADS * HG_DK
    wv = HG_HEADS * HG_DV
    q = proj[..., :wk]
    f_pre = proj[..., wk:2 * wk].astype(jnp.float32)
    i = proj[..., 2 * wk:2 * wk + wv]
    gate = proj[..., 2 * wk + wv:]
    log_f = jnp.logaddexp(jnp.log(lb), jnp.log1p(-lb) + jax.nn.log_sigmoid(f_pre))
    k = ((1.0 - lb) * jax.nn.sigmoid(-f_pre)).astype(q.dtype)
    o = hgrn2_recurrence(split_heads(q, HG_HEADS), split_heads(k, HG_HEADS),
                         split_heads(i, HG_HEADS), split_heads(log_f, HG_HEADS))
    of = o.astype(jnp.float32)
    of = of * lax.rsqrt(jnp.mean(jnp.square(of), axis=-1, keepdims=True) + RMS_EPS)
    o = merge_heads(of) * gnorm_g
    return (o * jax.nn.silu(gate.astype(jnp.float32))).astype(proj.dtype)

def hgrn2_lower_bounds(lower_bounds):
    p = jax.nn.softmax(lower_bounds.astype(jnp.float32), axis=0)
    return jnp.cumsum(p, axis=0) - p[0:1]

def second_inputs(seed: int = 0) -> dict:
    key = jax.random.key(seed)
    ks = jax.random.split(key, 16)
    d_hg = HG_HEADS * HG_DK
    nrm = jax.random.normal
    return {
        "x": nrm(ks[0], (BATCH, SEQ, D_MODEL), jnp.float32),
        "mem": nrm(ks[1], (BATCH, N_MEM, D_MODEL), jnp.float32),
        "w_in_sb": nrm(ks[2], (N_LAYERS_A, D_MODEL, SB_PROJ), jnp.float32) * D_MODEL ** -0.5,
        "w_in_hg": nrm(ks[3], (N_LAYERS_B, D_MODEL, HG_PROJ), jnp.float32) * D_MODEL ** -0.5,
        "w_mem_kv": nrm(ks[4], (DEPTH, D_MODEL, 2 * MEM_HEADS * MEM_HD), jnp.float32) * D_MODEL ** -0.5,
        "lower_bounds": 1.0 + 0.1 * nrm(ks[5], (DEPTH, d_hg), jnp.float32),
        "hg_norm_g": 1.0 + 0.05 * nrm(ks[6], (N_LAYERS_B, HG_HEADS * HG_DV), jnp.float32),
        "w_out": nrm(ks[7], (DEPTH, D_MIX, D_MODEL), jnp.float32) * (D_MIX ** -0.5 * DN_BETA),
        "ln_mix_g": 1.0 + 0.05 * nrm(ks[8], (DEPTH, D_MODEL), jnp.float32),
        "ln_mix_b": 0.02 * nrm(ks[9], (DEPTH, D_MODEL), jnp.float32),
        "w_up": nrm(ks[10], (DEPTH, D_MODEL, D_FF_2), jnp.float32) * D_MODEL ** -0.5,
        "w_down": nrm(ks[11], (DEPTH, D_FF_2, D_MODEL), jnp.float32) * (D_FF_2 ** -0.5 * DN_BETA),
        "ln_ffn_g": 1.0 + 0.05 * nrm(ks[12], (DEPTH, D_MODEL), jnp.float32),
        "ln_ffn_b": 0.02 * nrm(ks[13], (DEPTH, D_MODEL), jnp.float32),
    }

def second_block(x, mem, w_in_sb, w_in_hg, w_mem_kv, lower_bounds, hg_norm_g, w_out,
              ln_mix_g, ln_mix_b, w_up, w_down, ln_ffn_g, ln_ffn_b):
    lbs = hgrn2_lower_bounds(lower_bounds)
    w_sb = SB_HEADS * SB_HD
    for layer in range(DEPTH):
        slot = layer // N_MIXERS
        if layer % N_MIXERS == 0:
            proj = x @ w_in_sb[slot]
            q = split_heads(proj[..., :w_sb], SB_HEADS)
            k = split_heads(proj[..., w_sb:2 * w_sb], SB_HEADS)
            v = split_heads(proj[..., 2 * w_sb:3 * w_sb], SB_HEADS)
            q_mem = proj[..., 3 * w_sb:]
            mix = merge_heads(stick_breaking_attention(q, k, v))
        else:
            proj = x @ w_in_hg[slot]
            split = 2 * HG_HEADS * HG_DK + 2 * HG_HEADS * HG_DV
            q_mem = proj[..., split:]
            mix = hgrn2_mixer(proj[..., :split], lbs[layer], hg_norm_g[slot])
        mem_out = memory_attention_2(q_mem, mem, w_mem_kv[layer])
        y = jnp.concatenate([mix, mem_out.astype(mix.dtype)], axis=-1) @ w_out[layer]
        x = layer_norm(DN_ALPHA * x + y, ln_mix_g[layer], ln_mix_b[layer])
        h = jnp.square(jax.nn.relu(x @ w_up[layer]))
        x = layer_norm(DN_ALPHA * x + h @ w_down[layer], ln_ffn_g[layer], ln_ffn_b[layer])
    return x


def setup_inputs(seed=0):
    out = dict(first_inputs(seed))
    for name, value in second_inputs(seed + 1).items():
        if name != "x":
            out[name + "_2"] = value
    return out


def reference(
    x, mem, g_mix, w_in, b_gate, conv_w_short, w_att_out, w_conv_out, w_mem_out, w_o, g_mem,
    w_mem_kv, g_ffn, w_up, conv_w_ffn, w_down, g_final, mem_2, w_in_sb_2, w_in_hg_2, w_mem_kv_2,
    lower_bounds_2, hg_norm_g_2, w_out_2, ln_mix_g_2, ln_mix_b_2, w_up_2, w_down_2, ln_ffn_g_2,
    ln_ffn_b_2,
):
    x = first_block(
        x, mem, g_mix, w_in, b_gate, conv_w_short, w_att_out, w_conv_out, w_mem_out, w_o, g_mem,
        w_mem_kv, g_ffn, w_up, conv_w_ffn, w_down, g_final,
    )
    return second_block(
        x, mem_2, w_in_sb_2, w_in_hg_2, w_mem_kv_2, lower_bounds_2, hg_norm_g_2, w_out_2,
        ln_mix_g_2, ln_mix_b_2, w_up_2, w_down_2, ln_ffn_g_2, ln_ffn_b_2,
    )


_drawn_inputs = setup_inputs


def setup_inputs(seed=0):
    import zlib

    import numpy as np

    out = dict(_drawn_inputs(seed))
    spreads = {}
    factors = {'b_gate': 8.0, 'g_mem': 8.0, 'g_ffn': 4.074, 'g_final': 2.702, 'ln_ffn_b_2': 2.782}
    for name, (base, spread) in spreads.items():
        noise = np.random.default_rng([zlib.crc32(name.encode()), seed]).standard_normal(out[name].shape)
        drawn = base * np.exp(spread * noise) if base else spread * noise
        out[name] = __import__('jax').numpy.asarray(drawn.astype(out[name].dtype))
    for name, factor in factors.items():
        out[name] = (out[name] * factor).astype(out[name].dtype)
    return out
```

```python
from contextlib import ExitStack

import numpy as np

import concourse.bass as bass
from concourse import mybir

F32 = mybir.dt.float32
F32R = mybir.dt.float32r
ACT = mybir.ActivationFunctionType
ALU = mybir.AluOpType
AX = mybir.AxisListType

P = 128
S = 1024
D = 1024
KB = D // P
TB = S // P
MEM = 256
HD = 64
ATT_H, GROUPS = 6, 2
IDX_H, IDX_D = 8, 32
TOPK = 256
CONV = 384
FF, FF2 = 2816, 4096
SB_H = 12
FB, FB2 = FF // P, FF2 // P
FG = 4
EPS_RMS, EPS_LN = 1e-6, 1e-5
ALPHA = 2.0 ** 0.25
SCALE = HD ** -0.5
IDX_SCALE = (IDX_H * IDX_D) ** -0.5
NEG = -1e30
TAKEN = -3e38
BIG_E = 2.0 ** 60
RAW = 4

T_KI = 0
T_QI = 1
T_K = 3
T_Q = 4
T_V = 7
T_MEM = 8
T_CONV = 14
T_GATE = 23
T_ATT = T_GATE + 4 * KB
T_WO = T_ATT + KB // 2
T_FF = T_WO + KB
FULL, REST = FB // FG, FB % FG
FF_TILES = 2 * FG + KB // 2
T_REST = T_FF + FULL * FF_TILES
T_MEM2 = T_REST + 2 * REST + KB // 2
T_SB = T_MEM2 + 6
T_OUT2 = T_SB + 3 * SB_H // 2
T_FF2 = T_OUT2 + KB
FF2_GROUPS = FB2 // FG
FF2_TILES = FG + KB // 2
TILES = T_FF2 + FF2_GROUPS * FF2_TILES
FF_USES = 2 * FG + KB
U_REST = T_FF + FULL * FF_USES
U_MEM2 = U_REST + 2 * REST + KB
U_SB = U_MEM2 + 6
U_OUT2 = U_SB + 3 * SB_H // 2
U_FF2 = U_OUT2 + KB
FF2_USES = FG + KB

SMALL, _at = {}, 0
for _name, _n in (("inv_d", 1), ("g_mix", KB), ("g_mem", KB), ("g_ffn", KB), ("g_final", KB), ("ln1_g", KB),
                  ("ln1_b", KB), ("ln2_g", KB), ("ln2_b", KB), ("b_gate", 3 * KB), ("taps_short", 9),
                  ("pick_wi", IDX_H), ("taps_ff", 6 * FB)):
    SMALL[_name] = _at
    _at += _n
SMALL_N = _at
ROUNDS = TOPK // 8
IDX_STEPS = (TB - TOPK // P) * IDX_H
DSA_STEPS = TB * ATT_H
MATRICES = ("ident", "ones", "swap_att", "swap_idx", "rep_ki", "rep_swap_ki", "causal_q", "strict_mul", "strict_add",
            "neg_later", "neg_ones")


def stick_plan():
    return [(hh, th, a, max(0, a * P - 512 * th)) for th in range(2) for hh in range(2)
            for a in range(4 * th + 3, -1, -1)]


PLAN = stick_plan()
NS = len(PLAN)


def score_at(i):
    return P * (i * (i + 1) // 2)


def repeat(eng, n, body):
    body(0)
    with eng.Fori(1, n) as i:
        body(i)


def build(nc, io, out):
    with ExitStack() as ctx:
        base = (nc.sbuf_base + 31) // 32 * 32

        def at(name, shape, dtype, kib):
            return nc.alloc_sbuf_tensor_at(name, shape, dtype, offset=base + int(kib * 1024))

        def sem(name):
            return ctx.enter_context(nc.semaphore(name))

        def pair(name):
            return [sem(f"{name}{s}") for s in range(2)]

        raw = at("raw", [P, RAW, D], F32, 0)
        w_hi = at("w_hi", [P, 2, D], F32R, 16)
        w_lo = at("w_lo", [P, 2, D], F32R, 24)
        a_hi = at("a_hi", [P, KB, S], F32R, 32)
        a_lo = at("a_lo", [P, KB, S], F32R, 64)
        T = at("T", [P, 4, S], F32, 96)
        mats = {name: at(name, [P, P], F32, 112 + 0.5 * n) for n, name in enumerate(MATRICES)}
        ident, ones = mats["ident"], mats["ones"]
        small = at("small", [P, SMALL_N], F32, 117.5)
        tiny = at("tiny", [P, 256], F32, 118.75)
        bias_now = tiny[:, 224:225]
        zero = at("zero", [P, 8], F32, 119.75)
        Y0 = 120
        k_f = at("k_f", [P, S], F32, Y0)
        q_f = at("q_f", [P, 3, S], F32, Y0 + 4)
        v_f = at("v_f", [P, TB, P], F32, Y0 + 16)
        score = at("score", [P, score_at(TB)], F32, Y0 + 20)
        rope_tab = at("rope_tab", [P, 4, S], F32, Y0 + 20)
        x_in = at("x_in", [P, KB, S], F32, Y0 + 38)
        qi_f = at("qi_f", [P, 2, S], F32, Y0 + 38)
        ki_f = at("ki_f", [P, S], F32, Y0 + 46)
        qc_f = at("qc_f", [P, 2, S], F32, Y0 + 50)
        m_hi = at("m_hi", [P, KB, MEM], F32R, Y0 + 70)
        m_lo = at("m_lo", [P, KB, MEM], F32R, Y0 + 78)
        ym_f = at("ym_f", [P, 2, S], F32, Y0 + 74)
        ym_hi = at("ym_hi", [P, 2, S], F32R, Y0 + 58)
        ym_lo = at("ym_lo", [P, 2, S], F32R, Y0 + 66)
        km_f = at("km_f", [P, 2, MEM], F32, Y0 + 86)
        vm_f = at("vm_f", [P, 2, MEM], F32, Y0 + 88)
        vm_t = at("vm_t", [P, 2, MEM], F32, Y0 + 90)
        m_in = at("m_in", [P, KB, MEM], F32, Y0 + 94)
        yc_hi = at("yc_hi", [P, 3, S], F32R, Y0 + 74)
        yc_lo = at("yc_lo", [P, 3, S], F32R, Y0 + 86)
        gates = at("gates", [P, 4, S], F32, Y0 + 38)
        ya_f = at("ya_f", [P, 3, S], F32, Y0 + 38)
        ya_hi = at("ya_hi", [P, 3, S], F32R, Y0 + 50)
        ya_lo = at("ya_lo", [P, 3, S], F32R, Y0 + 62)
        back = at("back", [P, 4, S], F32, Y0 + 74)
        x_res = at("x_res", [P, KB, S], F32, Y0)
        b_hi = at("b_hi", [P, FG, S], F32R, Y0 + 38)
        b_lo = at("b_lo", [P, FG, S], F32R, Y0 + 54)
        qc2_f = at("qc2_f", [P, 2, S], F32, Y0 + 38)
        y2_f = at("y2_f", [P, KB, S], F32, Y0 + 38)
        sq_hi = at("sq_hi", [P, S], F32R, Y0 + 70)
        sq_lo = at("sq_lo", [P, S], F32R, Y0 + 74)
        sk_hi = at("sk_hi", [P, S], F32R, Y0 + 78)
        sk_lo = at("sk_lo", [P, S], F32R, Y0 + 82)
        sv_t = at("sv_t", [P, S], F32, Y0 + 86)
        sv_f = at("sv_f", [P, TB, P], F32, Y0 + 90)
        stick_w = at("stick_w", [P, 4, 512], F32, Y0 + 94)

        def par(name, k=0):
            return small[:, SMALL[name] + k:SMALL[name] + k + 1]

        row_max, neg_max = tiny[:, 0:8], tiny[:, 8:16]
        row_sum, inv_sum = tiny[:, 16:24], tiny[:, 24:32]
        std, rstd = tiny[:, 32:40], tiny[:, 40:48]
        best = tiny[:, 48:96].rearrange("p (b e) -> p b e", e=8)
        taps_act, taps_dve = tiny[:, 96:96 + 6 * FG], tiny[:, 128:128 + 6 * FG]
        wi_f = tiny[:, 160:160 + TB * IDX_H].rearrange("p (i h) -> p i h", h=IDX_H)

        dense = ctx.enter_context(nc.psum_tensor("dense", [P, 2, S], F32))
        side = ctx.enter_context(nc.psum_tensor("side", [P, 2, S], F32))

        weights_loaded = [sem(f"weights_loaded{r}") for r in range(RAW)]
        weights_rounded, weights_split = sem("weights_rounded"), sem("weights_split")
        tile_done, first_done = sem("tile_done"), sem("first_of_two_done")
        sums_free = pair("sums_free")
        consts_in, x_loaded, x_back, out_stored = sem("consts_in"), sem("x_loaded"), sem("x_back"), sem("out_stored")
        mem_loaded, mem2_loaded = sem("mem_loaded"), sem("mem2_loaded")
        met = {e: sem(f"met_{e}") for e in ("pe", "act", "dve")}
        squares, squares_used = sem("squares_ready"), sem("squares_used")
        mean_ready, std_ready, diag_ready, spread_ready = (sem("mean_ready"), sem("std_ready"), sem("diagonals_ready"),
                                                           sem("spread_ready"))
        scaled, shifted = sem("scaled_ready"), sem("shifted_ready")
        centred = sem("centred_ready")
        parts = {n: (sem(n + "_rounded"), sem(n + "_split")) for n in (
            "h", "mem", "ym", "yc", "ya", "merged", "h2", "hidden", "x2", "mem2", "y2", "x3", "hidden2")}
        yc_ready = sem("conv_out_ready")
        turned, roped, turn_free = sem("proj_turned"), sem("proj_rotated"), pair("turn_free")
        idx_ready, rel_ready, rel_used = sem("index_products"), sem("relu_ready"), sem("relu_used")
        mturned = sem("mem_values_turned")
        lg_ready, lg_max, lg_exp, lg_p = sem("logits_ready"), sem("row_max_ready"), sem("exp_ready"), sem("probs_ready")
        lg_t, lg_tc, lg_o, lg_oc = (sem("probs_turned"), sem("probs_copied"), sem("heads_ready"), sem("heads_copied"))
        conv_used = sem("conv_gate_used")
        part_ready, branch_free = sem("partial_ready"), pair("branch_free")
        gate_spilled, part_spilled, fetched = pair("gate_spilled"), pair("partial_spilled"), pair("fetched")
        att_sums, att_free, merged_sum = sem("att_out_ready"), pair("att_out_free"), sem("merged_ready")
        tap_ready, taps_done, acted = sem("first_tap_ready"), sem("taps_done"), sem("hidden_gate_ready")
        product_ready, squared = sem("hidden_product_ready"), sem("hidden_squared")
        sb_round, sb_vturned, sb_v = (sem("stick_rounded"), sem("stick_values_turned"),
                                               sem("stick_values_ready"))
        z_ready, e_ready, e_clip, ln_ready, sp_ready = (sem("z_ready"), sem("exp_z_ready"), sem("exp_z_clipped"),
                                                        sem("log_ready"), sem("softplus_ready"))
        arg_ready, w_ready, pv_done, y_copied = (sem("exponent_ready"), sem("stick_weights_ready"), sem("stick_pv_done"),
                                                 sem("stick_heads_copied"))

        spill_gate = nc.dram_tensor("spill_gate", [KB, P, S], F32).ap()
        spill_part = nc.dram_tensor("spill_part", [KB, P, S], F32).ap()

        block = ctx.enter_context(nc.Block())

        def emptied(eng, u, i=0, per=0):
            eng.wait_ge(sums_free[u % 2], i * (per // 2) + (u // 2 + 1))

        def meet(eng, me, count):
            count[0] += 1
            eng.drain().then_inc(met[me], 1)
            for other in met:
                if other != me:
                    eng.wait_ge(met[other], count[0])

        @block.sync
        def _(sp):
            sp.dma_start(x_in[:, :, :], io["x_t"]).then_inc(x_loaded, 16)
            sp.dma_start(small[:, :], io["small"]).then_inc(consts_in, 16)
            for r in range(RAW):
                sp.dma_start(raw[:, r, :], io["w_stream"][r]).then_inc(weights_loaded[r], 16)
            for name in MATRICES:
                sp.dma_start(mats[name][:, :], io[name]).then_inc(consts_in, 16)
            sp.dma_start(m_in[:, :, :], io["mem_t"]).then_inc(mem_loaded, 16)
            sp.dma_start(rope_tab[:, :, :], io["rope_tab"]).then_inc(consts_in, 16)
            with sp.Fori(1, TILES // RAW) as i:
                for r in range(RAW):
                    sp.wait_ge(weights_split, i * RAW + (r - RAW + 1))
                    sp.dma_start(raw[:, r, :], io["w_stream"][bass.ds(i * RAW + r, 1)].rearrange("a p k -> p (a k)")
                                 ).then_inc(weights_loaded[r], 16)
            for r in range(TILES % RAW):
                t = TILES // RAW * RAW + r
                sp.wait_ge(weights_split, t - RAW + 1)
                sp.dma_start(raw[:, r, :], io["w_stream"][t]).then_inc(weights_loaded[r], 16)

        CONSTS = 16 * (len(MATRICES) + 2)

        @block.gpsimd
        def _(pool):
            def split(t, r, loads):
                pool.wait_ge(weights_loaded[r], loads)
                pool.tensor_tensor(w_hi[:, r % 2, :], raw[:, r, :], zero[:, 0:1].broadcast_to([P, D]), ALU.add).then_inc(weights_rounded, 1)
                pool.wait_ge(weights_rounded, t + 1)
                pool.tensor_tensor(w_lo[:, r % 2, :], raw[:, r, :], w_hi[:, r % 2, :].bitcast(F32), ALU.subtract
                                   ).then_inc(weights_split, 1)

            pool.memset(zero[:, :], 0.0)
            pool.drain()
            for r in range(RAW):
                if r >= 2:
                    pool.wait_ge(tile_done, r - 1)
                split(r, r, 16)
            with pool.Fori(1, TILES // RAW) as i:
                for r in range(RAW):
                    pool.wait_ge(tile_done, i * RAW + (r - 1))
                    split(i * RAW + r, r, i * 16 + 16)
            for r in range(TILES % RAW):
                t = TILES // RAW * RAW + r
                pool.wait_ge(tile_done, t - 1)
                split(t, r, 16 * (TILES // RAW) + 16)

        @block.tensor
        def _(pe):
            met_n, norm_n = [0], {"sq": 0, "mean": 0, "diag": 0}

            def halves(psum, s, width=S):
                return [psum[:, s, c:min(c + 512, width)] for c in range(0, width, 512)]

            def product(slot, outs, hi, lo, blocks, at_block=0, ready=None, begin=0, end=True):
                for b in range(begin, blocks):
                    w = slice(P * (at_block + b), P * (at_block + b) + P)
                    stop = end and b == blocks - 1
                    if ready is not None:
                        pe.wait_ge(ready, b + 1)
                    for c, o in enumerate(outs):
                        x = slice(c * 512, c * 512 + o.shape[-1])
                        pe.matmul(o, w_hi[:, slot, w], hi[:, b, x], start=b == 0, stop=False)
                        pe.matmul(o, w_hi[:, slot, w], lo[:, b, x], start=False, stop=False)
                    for c, o in enumerate(outs):
                        x = slice(c * 512, c * 512 + o.shape[-1])
                        last = pe.matmul(o, w_lo[:, slot, w], hi[:, b, x], start=False, stop=stop)
                return last

            def tile(t, u, hi=a_hi, lo=a_lo, blocks=KB, width=S, at_block=0, ready=None, i=0, per=(0, 0),
                     done=tile_done):
                s = u % 2
                if u >= 2:
                    pe.wait_ge(sums_free[s], i * (per[1] // 2) + u // 2)
                pe.wait_ge(weights_split, i * per[0] + (t + 1))
                product(t % 2, halves(dense, s, width), hi, lo, blocks, at_block, ready).then_inc(done, 1)

            def means(src, blocks, sem_ready):
                for k in range(KB):
                    pe.wait_ge(sem_ready, norm_n["sq"] + k + 1)
                    for b in range(blocks):
                        last = pe.matmul(side[:, 0, b:b + 1], src(k)[:, b * P:b * P + P], par("inv_d"),
                                         start=k == 0 and b == 0, stop=k == KB - 1, skip_group_check=True)
                    last.then_inc(squares_used if k < KB - 1 else mean_ready, 1)

            def spread(blocks):
                pe.wait_ge(diag_ready, norm_n["diag"] + 1)
                norm_n["diag"] += 1
                for b in range(blocks):
                    last = pe.matmul(side[:, 1, b * P:b * P + P], ones[:, :], T[:, 2, b * P:b * P + P], start=True,
                                     stop=True, skip_group_check=True)
                last.then_inc(spread_ready, 1)

            def rms(blocks):
                means(lambda k: T[:, k % 2, :], blocks, squares)
                norm_n["sq"] += KB
                spread(blocks)

            def layer_norm():
                pe.wait_ge(centred, norm_n["mean"] + 1)
                norm_n["mean"] += 1
                for k in range(KB):
                    for b in range(TB):
                        last = pe.matmul(side[:, 0, b:b + 1], x_res[:, k, b * P:b * P + P], par("inv_d"),
                                         start=k == 0 and b == 0, stop=k == KB - 1, skip_group_check=True)
                last.then_inc(mean_ready, 1)
                spread(TB)
                rms(TB)

            pe.wait_ge(consts_in, CONSTS)
            rms(TB)
            rms(MEM // P)
            meet(pe, "pe", met_n)

            def turn(n, src, matrices):
                for m, (v, matrix) in enumerate(matrices):
                    if m == 0:
                        emptied(pe, n)
                    if v >= 2:
                        pe.wait_ge(turn_free[v % 2], v // 2)
                    for c in range(0, S, 512):
                        last = pe.matmul(side[:, v % 2, c:c + 512], matrix[:, :], src[:, c:c + 512], start=True, stop=True)
                    last.then_inc(turned, 1)

            for t in range(T_KI, T_MEM):
                tile(t, t, ready=parts["h"][1] if t == 0 else None)
                if t == 1:
                    turn(0, T[:, 0, :], [(0, mats["rep_ki"]), (1, mats["rep_swap_ki"])])
                    pe.wait_ge(turn_free[0], 1)
                    for b in range(TB):
                        last = pe.matmul(side[:, 0, b * IDX_H:b * IDX_H + IDX_H], T[:, 0, b * P:b * P + P],
                                         small[:, SMALL["pick_wi"]:SMALL["pick_wi"] + IDX_H], start=True, stop=True,
                                         skip_group_check=True)
                    last.then_inc(turned, 1)
                elif t >= 2:
                    turn(t - 1, T[:, (t - 1) % 2, :], [(t + 1, mats["swap_idx" if t - 1 < T_K else "swap_att"])])
            emptied(pe, T_V)
            pe.wait_ge(turn_free[1], 4)
            for b in range(TB):
                last = pe.transpose(side[:, 1, b * P:b * P + P], T[:, T_V % 2, b * P:b * P + P], ident[:, :])
            last.then_inc(turned, 1)
            meet(pe, "pe", met_n)

            for n in range(IDX_STEPS):
                i, h = TOPK // P + n // IDX_H, n % IDX_H
                rows = slice(IDX_D * (h % 4), IDX_D * (h % 4) + IDX_D)
                if n >= 2:
                    pe.wait_ge(rel_ready, n - 1)
                for c in range(0, P * (i + 1), 512):
                    e = min(P * (i + 1), c + 512)
                    last = pe.matmul(side[:, n % 2, c:e], qi_f[rows, h // 4, i * P:i * P + P], ki_f[rows, c:e], start=True,
                                     stop=True)
                last.then_inc(idx_ready, 1)
            meet(pe, "pe", met_n)

            def probs_turn(n, n0, blocks):
                pe.wait_ge(lg_p, n0 + n + 1)
                if n >= 2:
                    pe.wait_ge(lg_oc, n0 + n - 1)
                for b in range(blocks):
                    last = pe.transpose(dense[:, n % 2, b * P:b * P + P], T[:, n % 2, b * P:b * P + P], ident[:, :])
                last.then_inc(lg_t, 1)

            def memory(t0, u0, hi, lo, ready, qc, n0, layer):
                for n in range(4):
                    tile(t0 + n, u0 + n, hi=hi, lo=lo, width=MEM, ready=ready if n == 0 else None)
                for n in range(4, 6):
                    tile(t0 + n, u0 + n)
                emptied(pe, u0 + 2)
                emptied(pe, u0 + 3)
                for mt in range(2):
                    for j in range(2):
                        last = pe.transpose(side[:, 0, mt * MEM + j * P:mt * MEM + j * P + P],
                                            vm_t[:, j, mt * P:mt * P + P], ident[:, :])
                last.then_inc(mturned, 1)
                meet(pe, "pe", met_n)
                for n in range(TB + 2):
                    if n < TB:
                        if n >= 2:
                            pe.wait_ge(lg_exp, n0 + n - 1)
                        for h in range(4):
                            o = 512 * (h % 2) + MEM * (h // 2)
                            r = slice(HD * (h % 2), HD * (h % 2) + HD)
                            last = pe.matmul(side[:, n % 2, o:o + MEM], qc[r, h // 2, n * P:n * P + P], km_f[r, h // 2, :],
                                             start=h < 2, stop=True, skip_group_check=True)
                        last.then_inc(lg_ready, 1)
                    if 1 <= n <= TB:
                        probs_turn(n - 1, n0, KB)
                    if n >= 2:
                        b = n - 2
                        pe.wait_ge(lg_tc, n0 + b + 1)
                        for h in range(4):
                            q = 2 * (h % 2) + h // 2
                            for mt in range(2):
                                last = pe.matmul(dense[:, b % 2, h * P:h * P + P], vm_f[:, mt, h // 2 * P:h // 2 * P + P],
                                                 T[:, 2 + b % 2, (2 * q + mt) * P:(2 * q + mt) * P + P],
                                                 start=h == 0 and mt == 0, stop=mt == 1, skip_group_check=True)
                        last.then_inc(lg_o, 1)
                meet(pe, "pe", met_n)

            memory(T_MEM, T_MEM, m_hi, m_lo, parts["mem"][1], qc_f, 0, 0)

            for t in range(T_CONV, T_GATE):
                tile(t, t)

            pe.wait_ge(parts["yc"][1], 3)
            pe.wait_ge(parts["ym"][1], 2)

            def gate_blocks(i):
                for j in range(2):
                    for c in range(4):
                        t = T_GATE + 4 * j + c
                        if c < 3:
                            tile(t, t, i=i, per=(8, 8))
                        else:
                            tile(t, t, hi=yc_hi, lo=yc_lo, blocks=3, i=i, per=(8, 8), done=first_done)
                            if not isinstance(i, int):
                                pe.wait_ge(branch_free[j], i)
                            product(t % 2, halves(side, j), ym_hi, ym_lo, 2, at_block=3).then_inc(tile_done, 1)

            repeat(pe, 4, gate_blocks)
            meet(pe, "pe", met_n)

            for n in range(DSA_STEPS + 2):
                if n < DSA_STEPS:
                    i, h = divmod(n, ATT_H)
                    r = slice(HD * (h // 3), HD * (h // 3) + HD)
                    if n >= 2:
                        pe.wait_ge(lg_max, TB + n - 1)
                    for c in range(0, P * (i + 1), 512):
                        e = min(P * (i + 1), c + 512)
                        last = pe.matmul(side[:, n % 2, c:e], q_f[r, h % 3, i * P:i * P + P], k_f[r, c:e], start=True,
                                         stop=True)
                    last.then_inc(lg_ready, 1)
                if 1 <= n <= DSA_STEPS:
                    probs_turn(n - 1, TB, (n - 1) // ATT_H + 1)
                if n >= 2:
                    b = n - 2
                    i = b // ATT_H
                    pe.wait_ge(lg_tc, TB + b + 1)
                    for kb in range(i + 1):
                        last = pe.matmul(dense[:, b % 2, 0:P], v_f[:, kb, :], T[:, 2 + b % 2, kb * P:kb * P + P],
                                         start=kb == 0, stop=kb == i)
                    last.then_inc(lg_o, 1)
            meet(pe, "pe", met_n)

            for n in range(KB // 2):
                t = T_ATT + n
                tile(t, t, hi=ya_hi, lo=ya_lo, blocks=3, ready=parts["ya"][1] if n == 0 else None, done=first_done)
                if n >= 2:
                    pe.wait_ge(att_free[n % 2], n // 2)
                product(t % 2, halves(side, n % 2), ya_hi, ya_lo, 3, at_block=3).then_inc(tile_done, 1)
            for n in range(KB):
                tile(T_WO + n, T_WO + n, ready=parts["merged"][1] if n == 0 else None)
            meet(pe, "pe", met_n)
            rms(TB)

            def feed(t0, u0, ups, hidden, blocks, per, ready, n0):
                def group(i):
                    for c in range(ups):
                        tile(t0 + c, u0 + c, i=i, per=per,
                             ready=ready if isinstance(i, int) and c == 0 else None)
                    t = t0 + ups
                    pe.wait_ge(weights_split, i * per[0] + (t + 1))
                    for m in range(2):
                        u = u0 + ups + m
                        pe.wait_ge(sums_free[u % 2], i * (per[1] // 2) + u // 2)
                        if m == 0:
                            pe.wait_ge(hidden, i * blocks + (n0 + blocks - 1))
                        product(t % 2, halves(dense, u % 2), b_hi, b_lo, blocks - 1, m * blocks, end=False)
                    pe.wait_ge(hidden, i * blocks + (n0 + blocks))
                    for m in range(2):
                        product(t % 2, halves(dense, (u0 + ups + m) % 2), b_hi, b_lo, blocks, m * blocks, begin=blocks - 1
                                ).then_inc(tile_done if m else first_done, 1)
                    for c in range(1, KB // 2):
                        for m in range(2):
                            tile(t + c, u0 + ups + 2 * c + m, hi=b_hi, lo=b_lo, blocks=blocks, at_block=m * blocks, i=i,
                                 per=per, done=tile_done if m else first_done)
                return group

            h2 = parts["h2"][1]
            hidden = parts["hidden"][1]
            repeat(pe, FULL, feed(T_FF, T_FF, 2 * FG, hidden, FG, (FF_TILES, FF_USES), h2, 0))
            feed(T_REST, U_REST, 2 * REST, hidden, REST, (0, 0), None, FULL * FG)(0)
            meet(pe, "pe", met_n)
            rms(TB)

            pe.wait_ge(parts["x2"][1], KB)
            memory(T_MEM2, U_MEM2, m_hi, m_lo, parts["mem2"][1], qc2_f, TB + DSA_STEPS, 1)

            def zbank(n, c0=0):
                return side[:, (n % 4) // 2, (n % 2) * 512 + c0:(n % 2) * 512 + 512]

            def strip(t, n, c0):
                return t[:, (n % 4) // 2, (n % 2) * 512 + c0:(n % 2) * 512 + 512]

            def stick_pairs(i):
                for pr in range(2):
                    for c in range(3):
                        tile(T_SB + 3 * pr + c, U_SB + 3 * pr + c, i=i, per=(6, 6))
                    n0 = NS * pr
                    emptied(pe, U_SB + 3 * pr + 2, i, 6)
                    for b in range(TB):
                        last = pe.transpose(side[:, 0, b * P:b * P + P], sv_t[:, b * P:b * P + P], ident[:, :])
                    last.then_inc(sb_vturned, 1)
                    pe.wait_ge(sb_v, i * 2 + (pr + 1))
                    for n in range(NS + 4):
                        if n < NS:
                            hh, th, a, c0 = PLAN[n]
                            r = slice(HD * hh, HD * hh + HD)
                            kb, tk = slice(a * P, a * P + P), slice(512 * th + c0, 512 * th + 512)
                            if n >= 4:
                                pe.wait_ge(w_ready, i * (2 * NS) + (n0 + n - 3))
                            z = zbank(n, c0)
                            pe.matmul(z, sk_hi[r, kb], sq_hi[r, tk], start=True, stop=False, skip_group_check=True)
                            pe.matmul(z, sk_hi[r, kb], sq_lo[r, tk], start=False, stop=False, skip_group_check=True)
                            pe.matmul(z, sk_lo[r, kb], sq_hi[r, tk], start=False, stop=True, skip_group_check=True
                                      ).then_inc(z_ready, 1)
                        if 2 <= n < NS + 2:
                            m = n - 2
                            hh, th, a, c0 = PLAN[m]
                            pe.wait_ge(sp_ready, i * (2 * NS) + (n0 + m + 1))
                            if a >= 4 * th:
                                pe.matmul(zbank(m)[:, c0:c0 + P], ident[:, :], mats["strict_add"][:, :], start=False,
                                          stop=True, skip_group_check=True)
                            if a < 4 * th + 3:
                                c1 = PLAN[m - 1][3]
                                pe.matmul(zbank(m, c1), mats["neg_ones"][:, :], strip(T[:, 2:4, :], m, c1), start=False,
                                          stop=True, skip_group_check=True)
                            pe.matmul(zbank(m, c0), mats["neg_later"][:, :], strip(T[:, 0:2, :], m, c0), start=False,
                                      stop=True, skip_group_check=True).then_inc(arg_ready, 1)
                        if n >= 4:
                            m = n - 4
                            hh, th, a, c0 = PLAN[m]
                            pe.wait_ge(w_ready, i * (2 * NS) + (n0 + m + 1))
                            pe.matmul(dense[:, hh, 512 * th + c0:512 * th + 512], sv_f[:, a, :], stick_w[:, m % 4, c0:512],
                                      start=a == 4 * th + 3, stop=a == 0, skip_group_check=True).then_inc(pv_done, 1)
                    pe.wait_ge(y_copied, i * 8 + (4 * pr + 4))

            repeat(pe, SB_H // 4, stick_pairs)
            meet(pe, "pe", met_n)

            for n in range(KB):
                tile(T_OUT2 + n, U_OUT2 + n, ready=parts["y2"][1] if n == 0 else None)
            meet(pe, "pe", met_n)
            layer_norm()
            repeat(pe, FF2_GROUPS, feed(T_FF2, U_FF2, FG, parts["hidden2"][1], FG, (FF2_TILES, FF2_USES),
                                        parts["x3"][1], 0))
            meet(pe, "pe", met_n)
            layer_norm()
            meet(pe, "pe", met_n)

        @block.scalar
        def _(act):
            met_n, norm_n = [0], {"sq": 0, "used": 0, "mean": 0, "scaled": 0}

            def rms_squares(src, width):
                for k in range(KB):
                    if k >= 2:
                        act.wait_ge(squares_used, norm_n["used"] + k - 1)
                    act.activation(T[:, k % 2, 0:width], src(k), ACT.Square).then_inc(squares, 1)
                norm_n["used"] += KB - 1
                norm_n["mean"] += 1

            def root(blocks, eps):
                act.wait_ge(mean_ready, norm_n["mean"])
                act.activation(std[:, 0:blocks], side[:, 0, 0:blocks], ACT.Sqrt, bias=eps).then_inc(std_ready, 1)

            def round_scaled(dst, src, which, shift=None):
                for k in range(KB):
                    act.wait_ge(scaled, norm_n["scaled"] + k + 1)
                    if shift is not None:
                        act.activation(x_res[:, k, :], src(k), ACT.Identity, bias=par(shift, k)).then_inc(shifted, 1)
                        act.drain()
                        if dst is not None:
                            act.activation(dst[:, k, :], x_res[:, k, :], ACT.Copy).then_inc(parts[which][0], 1)
                    else:
                        act.activation(dst[:, k, :], src(k), ACT.Copy).then_inc(parts[which][0], 1)
                norm_n["scaled"] += KB

            act.wait_ge(consts_in, CONSTS)
            act.wait_ge(x_loaded, 16)
            rms_squares(lambda k: x_in[:, k, :], S)
            root(TB, EPS_RMS)
            round_scaled(a_hi, lambda k: x_in[:, k, :], "h")
            act.wait_ge(mem_loaded, 16)
            rms_squares(lambda k: m_in[:, k, :], MEM)
            root(MEM // P, EPS_RMS)
            round_scaled(m_hi, lambda k: m_in[:, k, :], "mem")
            meet(act, "act", met_n)

            for t in range(T_KI, T_MEM):
                act.wait_ge(tile_done, t + 1)
                if t >= 2:
                    act.wait_ge(roped, t - 1)
                act.activation(T[:, t % 2, :], dense[:, t % 2, :], ACT.Copy).then_inc(sums_free[t % 2], 1)
            meet(act, "act", met_n)

            for n in range(IDX_STEPS):
                i = TOPK // P + n // IDX_H
                act.wait_ge(idx_ready, n + 1)
                if n >= 2:
                    act.wait_ge(rel_used, n - 1)
                act.activation(T[:, n % 2, 0:P * (i + 1)], side[:, n % 2, 0:P * (i + 1)], ACT.Relu).then_inc(rel_ready, 1)
            meet(act, "act", met_n)

            def memory(t0, u0, qc, yf, y0, n0, layer):
                for n in range(6):
                    act.wait_ge(tile_done, t0 + n + 1)
                    s = (u0 + n) % 2
                    if n < 4:
                        act.activation((km_f if n < 2 else vm_t)[:, n % 2, :], dense[:, s, 0:MEM], ACT.Copy
                                       ).then_inc(sums_free[s], 1)
                    else:
                        act.activation(qc[:, n % 2, :], dense[:, s, :], ACT.Copy).then_inc(sums_free[s], 1)
                meet(act, "act", met_n)
                for n in range(TB + 2):
                    if n < TB:
                        act.wait_ge(lg_max, n0 + n + 1)
                        if n >= 2:
                            act.wait_ge(lg_t, n0 + n - 1)
                        for q in range(4):
                            e = 4 * (n % 2) + q
                            last = act.activation(T[:, n % 2, q * MEM:q * MEM + MEM], side[:, n % 2, q * MEM:q * MEM + MEM],
                                                  ACT.Exp, bias=neg_max[:, e:e + 1], scale=SCALE,
                                                  accum_out=row_sum[:, e:e + 1])
                        last.then_inc(lg_exp, 1)
                    if 1 <= n <= TB:
                        copy_turned(n - 1, n0, S)
                    if n >= 2:
                        b = n - 2
                        act.wait_ge(lg_o, n0 + b + 1)
                        heads = dense[:, b % 2, 0:512].rearrange("p (j e q) -> p j e q", j=2, e=2)
                        for e in range(2):
                            r = slice(HD * e, HD * e + HD)
                            last = act.activation(yf[r, y0:y0 + 2, b * P:b * P + P], heads[r, :, e, :], ACT.Copy)
                        last.then_inc(lg_oc, 1)

            def copy_turned(n, n0, width):
                act.wait_ge(lg_t, n0 + n + 1)
                if n >= 2:
                    act.wait_ge(lg_o, n0 + n - 1)
                act.activation(T[:, 2 + n % 2, 0:width], dense[:, n % 2, 0:width], ACT.Copy).then_inc(lg_tc, 1)

            memory(T_MEM, T_MEM, qc_f, ym_f, 0, 0, 0)
            act.drain()
            for k in range(2):
                act.activation(ym_hi[:, k, :], ym_f[:, k, :], ACT.Copy).then_inc(parts["ym"][0], 1)
            meet(act, "act", met_n)

            for j in range(3):
                t = T_CONV + 3 * j
                act.wait_ge(tile_done, t + 1)
                if j:
                    act.wait_ge(conv_used, j)
                act.activation(T[:, 0, :], dense[:, t % 2, :], ACT.Copy).then_inc(sums_free[t % 2], 1)
                act.wait_ge(yc_ready, j + 1)
                act.activation(yc_hi[:, j, :], T[:, 2, :], ACT.Copy).then_inc(parts["yc"][0], 1)

            def gate_blocks(i):
                first = isinstance(i, int)
                for j in range(2):
                    t = T_GATE + 4 * j
                    for c in range(3):
                        b = SMALL["b_gate"] + 3 * j + c
                        act.activation(bias_now[:, :], small[:, b:b + 1] if first else small[:, bass.ds(i * 6 + b, 1)], ACT.Copy)
                        act.drain()
                        act.wait_ge(tile_done, i * 8 + (t + c + 1))
                        dst = T[:, j, :] if c == 0 else gates[:, 2 * j + c - 1, :]
                        if not first and c == 0:
                            act.wait_ge(gate_spilled[j], i * 16)
                        if not first and c == 1:
                            act.wait_ge(part_spilled[j], i * 16)
                        act.activation(dst, dense[:, (t + c) % 2, :], ACT.Sigmoid, bias=bias_now[:, :]
                                       ).then_inc(sums_free[(t + c) % 2], 1)
                        act.drain()
                        if c == 0:
                            act.dma_start(spill_gate[bass.ds(i * 2 + j, 1)].rearrange("a p s -> p (a s)")
                                          if not first else spill_gate[j], T[:, j, :]).then_inc(gate_spilled[j], 16)
                    act.wait_ge(part_ready, i * 2 + (j + 1))
                    act.dma_start(spill_part[bass.ds(i * 2 + j, 1)].rearrange("a p s -> p (a s)")
                                  if not first else spill_part[j], gates[:, 2 * j, :]).then_inc(part_spilled[j], 16)

            repeat(act, 4, gate_blocks)
            for j in range(2):
                act.wait_ge(gate_spilled[j], 64)
                act.wait_ge(part_spilled[j], 64)
            meet(act, "act", met_n)

            for n in range(DSA_STEPS + 2):
                if n < DSA_STEPS:
                    w, e = P * (n // ATT_H + 1), n % 8
                    act.wait_ge(lg_max, TB + n + 1)
                    act.activation(T[:, n % 2, 0:w], T[:, n % 2, 0:w], ACT.Exp, bias=neg_max[:, e:e + 1], scale=SCALE,
                                   accum_out=row_sum[:, e:e + 1]).then_inc(lg_exp, 1)
                if 1 <= n <= DSA_STEPS:
                    copy_turned(n - 1, TB, P * ((n - 1) // ATT_H + 1))
                if n >= 2:
                    i, h = divmod(n - 2, ATT_H)
                    r = slice(HD * (h // 3), HD * (h // 3) + HD)
                    act.wait_ge(lg_o, TB + n - 1)
                    act.activation(ya_f[r, h % 3, i * P:i * P + P], dense[r, n % 2, 0:P], ACT.Copy).then_inc(lg_oc, 1)
            meet(act, "act", met_n)

            act.dma_start(x_res[:, :, :], io["x_t"]).then_inc(x_back, 16)

            def fetch(j):
                act.dma_start(back[:, 2 * (j % 2), :], spill_gate[j]).then_inc(fetched[j % 2], 16)
                act.dma_start(back[:, 2 * (j % 2) + 1, :], spill_part[j]).then_inc(fetched[j % 2], 16)

            fetch(0)
            fetch(1)
            act.dma_start(m_in[:, :, :], io["mem2_t"]).then_inc(mem2_loaded, 16)
            for k in range(3):
                act.activation(ya_hi[:, k, :], ya_f[:, k, :], ACT.Copy).then_inc(parts["ya"][0], 1)
            for j in range(KB):
                act.wait_ge(merged_sum, j + 1)
                act.activation(a_hi[:, j, :], T[:, j % 2, :], ACT.Copy).then_inc(parts["merged"][0], 1)
                if j + 2 < KB:
                    fetch(j + 2)
            meet(act, "act", met_n)

            rms_squares(lambda k: x_res[:, k, :], S)
            root(TB, EPS_RMS)
            round_scaled(a_hi, lambda k: T[:, (0, 1, 3)[k % 3], :], "h2")
            act.wait_ge(mem2_loaded, 16)
            act.activation(m_hi[:, :, :], m_in[:, :, :], ACT.Copy).then_inc(parts["mem2"][0], 1)

            def gated(i, t0, n_f, f0, per):
                cols = SMALL["taps_ff"] + 6 * f0
                act.drain()
                act.activation(taps_act[:, 0:6 * n_f], small[:, bass.ds(i * (6 * FG) + cols, 6 * n_f)]
                               if not isinstance(i, int) else small[:, cols:cols + 6 * n_f], ACT.Copy)
                act.drain()
                for f in range(n_f):
                    for c in range(2):
                        t = t0 + 2 * f + c
                        u = gu[0] + 2 * f + c
                        act.wait_ge(tile_done, i * per + (t + 1))
                        slot = 2 * (f % 2) + c
                        if f >= 2 or not isinstance(i, int) or f0:
                            act.wait_ge(parts["hidden"][1] if c == 0 else product_ready, i * FG + (f0 + f - 1))
                        act.activation(T[:, slot, :], dense[:, u % 2, :], ACT.Copy,
                                       scale=taps_act[:, 6 * f + 3 * c + 2:6 * f + 3 * c + 3]).then_inc(tap_ready, 1)
                    act.wait_ge(taps_done, i * (2 * FG) + (2 * (f0 + f) + 1))
                    act.activation(T[:, 2 * (f % 2), :], T[:, 2 * (f % 2), :], ACT.Silu).then_inc(acted, 1)
                    act.wait_ge(product_ready, i * FG + (f0 + f + 1))
                    act.activation(b_hi[:, f, :], T[:, 2 * (f % 2), :], ACT.Copy).then_inc(parts["hidden"][0], 1)

            gu = [T_FF]
            repeat(act, FULL, lambda i: gated(i, T_FF, FG, 0, FF_TILES))
            gu[0] = U_REST
            gated(0, T_REST, REST, FULL * FG, 0)
            meet(act, "act", met_n)

            rms_squares(lambda k: x_res[:, k, :], S)
            root(TB, EPS_RMS)
            round_scaled(a_hi, lambda k: x_res[:, k, :], "x2")

            memory(T_MEM2, U_MEM2, qc2_f, y2_f, 6, TB + DSA_STEPS, 1)
            meet(act, "act", met_n)

            def stick_pairs(i):
                for pr in range(2):
                    for c in range(3):
                        u = U_SB + 3 * pr + c
                        act.wait_ge(tile_done, i * 6 + (T_SB + 3 * pr + c + 1))
                        if c == 0:
                            act.activation(sq_hi[:, :], dense[:, u % 2, :], ACT.Copy, scale=SCALE).then_inc(sb_round, 1)
                        elif c == 1:
                            act.activation(sk_hi[:, :], dense[:, u % 2, :], ACT.Copy).then_inc(sb_round, 1)
                        else:
                            act.activation(sv_t[:, :], dense[:, u % 2, :], ACT.Copy).then_inc(sums_free[u % 2], 1)
                    n0 = NS * pr
                    for n in range(NS + 3):
                        if n < NS:
                            c0 = PLAN[n][3]
                            act.wait_ge(z_ready, i * (2 * NS) + (n0 + n + 1))
                            act.activation(strip(T[:, 0:2, :], n, c0), zbank(n, c0), ACT.Exp).then_inc(e_ready, 1)
                        if 1 <= n <= NS:
                            m, c0 = n - 1, PLAN[n - 1][3]
                            act.wait_ge(e_clip, i * (2 * NS) + (n0 + m + 1))
                            act.activation(strip(T[:, 0:2, :], m, c0), strip(T[:, 0:2, :], m, c0), ACT.Ln, bias=1.0
                                           ).then_inc(ln_ready, 1)
                        if n >= 3:
                            m, c0 = n - 3, PLAN[n - 3][3]
                            if n0 + m - 3 > 0 or not isinstance(i, int):
                                act.wait_ge(pv_done, i * (2 * NS) + (n0 + m - 3))
                            act.wait_ge(arg_ready, i * (2 * NS) + (n0 + m + 1))
                            act.activation(stick_w[:, m % 4, c0:512], zbank(m, c0), ACT.Exp).then_inc(w_ready, 1)

            def zbank(n, c0=0):
                return side[:, (n % 4) // 2, (n % 2) * 512 + c0:(n % 2) * 512 + 512]

            def strip(t, n, c0):
                return t[:, (n % 4) // 2, (n % 2) * 512 + c0:(n % 2) * 512 + 512]

            act.preload_act_table_set("natural_log_exp_and_others")
            repeat(act, SB_H // 4, stick_pairs)
            meet(act, "act", met_n)

            for k in range(KB):
                act.activation(a_hi[:, k, :], y2_f[:, k, :], ACT.Copy).then_inc(parts["y2"][0], 1)
            meet(act, "act", met_n)

            def layer_norm(dst, which, shift):
                norm_n["mean"] += 1
                act.wait_ge(mean_ready, norm_n["mean"])
                for k in range(KB):
                    act.wait_ge(centred, cen[0] + k + 1)
                    if k >= 2:
                        act.wait_ge(squares_used, norm_n["used"] + k - 1)
                    act.activation(T[:, k % 2, :], x_res[:, k, :], ACT.Square).then_inc(squares, 1)
                cen[0] += KB + 1
                norm_n["used"] += KB - 1
                norm_n["mean"] += 1
                root(TB, EPS_LN)
                round_scaled(dst, lambda k: T[:, (0, 1, 3)[k % 3], :], which, shift)

            cen = [1]
            layer_norm(a_hi, "x3", "ln1_b")

            def squared_relu(i):
                for f in range(FG):
                    act.wait_ge(squared, i * FG + (f + 1))
                    act.activation(b_hi[:, f, :], T[:, f, :], ACT.Copy).then_inc(parts["hidden2"][0], 1)

            repeat(act, FF2_GROUPS, squared_relu)
            meet(act, "act", met_n)
            layer_norm(None, None, "ln2_b")
            act.drain()
            act.dma_start(out, x_res[:, :, :]).then_inc(out_stored, 16)
            act.wait_ge(out_stored, 16)
            meet(act, "act", met_n)

        @block.vector
        def _(dve):
            met_n, norm_n = [0], {"mean": 0, "std": 0, "spread": 0, "parts": 0, "shift": 0}

            def diagonals(values, blocks):
                for b in range(blocks):
                    last = dve.tensor_scalar(T[:, 2, b * P:b * P + P], ident[:, :], values[:, b:b + 1], None, ALU.mult)
                last.then_inc(diag_ready, 1)
                norm_n["spread"] += 1
                dve.wait_ge(spread_ready, norm_n["spread"])

            def inverse_std(blocks):
                norm_n["std"] += 1
                dve.wait_ge(std_ready, norm_n["std"])
                dve.reciprocal(rstd[:, 0:blocks], std[:, 0:blocks])
                dve.drain()
                diagonals(rstd, blocks)

            def low(dst, k, src, which, n):
                dve.wait_ge(parts[which][0], n)
                dve.tensor_tensor(dst[1], src, dst[0].bitcast(F32), ALU.subtract).then_inc(parts[which][1], 1)

            def scale_all(src, dst, gain, which, hi, lo, width, ring=0, lag=1):
                for k in range(KB + lag):
                    if k < KB:
                        if ring and k >= ring:
                            dve.wait_ge(parts[which][1], k - ring + 1)
                        dve.scalar_tensor_tensor(dst(k), src(k), par(gain, k), side[:, 1, 0:width], ALU.mult, ALU.mult
                                                 ).then_inc(scaled, 1)
                    if k >= lag and which is not None:
                        m = k - lag
                        low((hi[:, m, :], lo[:, m, :]), m, dst(m), which, m + 1)

            dve.wait_ge(consts_in, CONSTS)
            dve.wait_ge(x_loaded, 16)
            inverse_std(TB)
            scale_all(lambda k: x_in[:, k, :], lambda k: x_in[:, k, :], "g_mix", "h", a_hi, a_lo, S)
            dve.wait_ge(mem_loaded, 16)
            inverse_std(MEM // P)
            scale_all(lambda k: m_in[:, k, :], lambda k: m_in[:, k, :], "g_mem", "mem", m_hi, m_lo, MEM)
            meet(dve, "dve", met_n)

            def rotate(t, tab, dst, n_turned, v):
                dve.wait_ge(turned, n_turned)
                dve.tensor_tensor(T[:, 2 + t % 2, :], side[:, v % 2, :], rope_tab[:, tab + 1, :], ALU.mult
                                  ).then_inc(turn_free[v % 2], 1)
                dve.tensor_tensor(T[:, t % 2, :], T[:, t % 2, :], rope_tab[:, tab, :], ALU.mult)
                dve.drain()
                dve.tensor_tensor(dst, T[:, t % 2, :], T[:, 2 + t % 2, :], ALU.add).then_inc(roped, 1)

            dve.wait_ge(turned, 1)
            dve.tensor_tensor(T[:, 3, :], side[:, 0, :], rope_tab[:, 0, :], ALU.mult).then_inc(turn_free[0], 1)
            dve.wait_ge(turned, 2)
            dve.tensor_tensor(T[:, 2, :], side[:, 1, :], rope_tab[:, 1, :], ALU.mult).then_inc(turn_free[1], 1)
            dve.drain()
            dve.tensor_tensor(ki_f[:, :], T[:, 2, :], T[:, 3, :], ALU.add)
            dve.wait_ge(turned, 3)
            dve.tensor_copy(tiny[:, 160:160 + TB * IDX_H], side[:, 0, 0:TB * IDX_H]).then_inc(turn_free[0], 1)
            dve.drain().then_inc(roped, 1)
            for t in range(1, T_V):
                dst = qi_f[:, t - 1, :] if t < T_K else k_f[:, :] if t == T_K else q_f[:, t - T_Q, :]
                rotate(t, 0 if t < T_K else 2, dst, t + 3, t + 2)
            dve.wait_ge(turned, 10)
            dve.tensor_copy(v_f[:, :, :], side[:, 1, :].rearrange("p (b d) -> p b d", d=P)).then_inc(turn_free[1], 1)
            meet(dve, "dve", met_n)

            dve.memset(score[:, 0:score_at(2)], 0.0)
            for n in range(IDX_STEPS):
                i, h = TOPK // P + n // IDX_H, n % IDX_H
                w = P * (i + 1)
                sc = score[:, score_at(i):score_at(i) + w]
                dve.wait_ge(rel_ready, n + 1)
                if h == 0:
                    dve.tensor_scalar(sc, T[:, n % 2, 0:w], wi_f[:, i, h:h + 1], None, ALU.mult).then_inc(rel_used, 1)
                else:
                    dve.drain()
                    dve.scalar_tensor_tensor(sc, T[:, n % 2, 0:w], wi_f[:, i, h:h + 1], sc, ALU.mult, ALU.add
                                             ).then_inc(rel_used, 1)
            dve.drain()
            for i in range(TB):
                e = score_at(i + 1)
                dve.tensor_tensor(score[:, e - P:e], score[:, e - P:e], mats["causal_q"][:, :], ALU.add)
            dve.drain()
            meet(dve, "dve", met_n)

            def topk_round():
                for i in range(TOPK // P, TB):
                    dve.max(best[:, i - TOPK // P, :], score[:, score_at(i):score_at(i + 1)])
                dve.drain()
                for i in range(TOPK // P, TB):
                    sc = score[:, score_at(i):score_at(i + 1)]
                    dve.match_replace(sc, best[:, i - TOPK // P, :], sc, TAKEN)
                dve.drain()

            def memory(t0, u0, qc_n, n0, layer, rounds):
                dve.wait_ge(mturned, layer + 1)
                dve.tensor_copy(vm_f[:, :, :], side[:, 0, 0:512].rearrange("p (m d) -> p m d", m=2))
                meet(dve, "dve", met_n)
                for n in range(TB):
                    e = 4 * (n % 2)
                    dve.wait_ge(lg_ready, n0 + n + 1)
                    dve.tensor_reduce(row_max[:, e:e + 4], side[:, n % 2, :].rearrange("p (q m) -> p q m", q=4), AX.X,
                                      ALU.max)
                    dve.drain()
                    dve.tensor_scalar(neg_max[:, e:e + 4], row_max[:, e:e + 4], -SCALE, None, ALU.mult
                                      ).then_inc(lg_max, 1)
                    dve.wait_ge(lg_exp, n0 + n + 1)
                    dve.reciprocal(inv_sum[:, e:e + 4], row_sum[:, e:e + 4])
                    dve.drain()
                    for q in range(4):
                        pq = T[:, n % 2, q * MEM:q * MEM + MEM]
                        last = dve.tensor_scalar(pq, pq, inv_sum[:, e + q:e + q + 1], None, ALU.mult)
                    last.then_inc(lg_p, 1)

            memory(T_MEM, T_MEM, None, 0, 0, 0)
            for k in range(2):
                low((ym_hi[:, k, :], ym_lo[:, k, :]), k, ym_f[:, k, :], "ym", k + 1)
            meet(dve, "dve", met_n)

            for j in range(3):
                t = T_CONV + 3 * j
                with dve.Fori(0, 2):
                    topk_round()
                emptied(dve, t)
                dve.wait_ge(tile_done, t + 2)
                dve.tensor_tensor(T[:, 1, :], dense[:, (t + 1) % 2, :], T[:, 0, :], ALU.mult
                                  ).then_inc(sums_free[(t + 1) % 2], 1)
                dve.drain().then_inc(conv_used, 1)
                dve.tensor_scalar(T[:, 2, :], T[:, 1, :], par("taps_short", 3 * j + 2), None, ALU.mult)
                for d in (1, 2):
                    dve.drain()
                    dve.scalar_tensor_tensor(T[:, 2, d:S], T[:, 1, 0:S - d], par("taps_short", 3 * j + 2 - d), T[:, 2, d:S],
                                             ALU.mult, ALU.add)
                dve.drain()
                dve.wait_ge(tile_done, t + 3)
                dve.tensor_tensor(T[:, 2, :], dense[:, (t + 2) % 2, :], T[:, 2, :], ALU.mult
                                  ).then_inc(sums_free[(t + 2) % 2], 1)
                dve.drain().then_inc(yc_ready, 1)
                low((yc_hi[:, j, :], yc_lo[:, j, :]), j, T[:, 2, :], "yc", j + 1)

            def gate_blocks(i):
                for j in range(2):
                    t = T_GATE + 4 * j
                    for _ in range(3):
                        topk_round()
                    g1, g2 = gates[:, 2 * j, :], gates[:, 2 * j + 1, :]
                    dve.wait_ge(sums_free[(t + 2) % 2], i * 4 + ((t + 2) // 2 + 1))
                    dve.wait_ge(sums_free[(t + 1) % 2], i * 4 + ((t + 1) // 2 + 1))
                    dve.wait_ge(first_done, i * 2 + (j + 1))
                    dve.tensor_tensor(g1, dense[:, (t + 3) % 2, :], g1, ALU.mult).then_inc(sums_free[(t + 3) % 2], 1)
                    dve.wait_ge(tile_done, i * 8 + (t + 4))
                    dve.tensor_tensor(g2, side[:, j, :], g2, ALU.mult).then_inc(branch_free[j], 1)
                    dve.drain()
                    dve.tensor_tensor(g1, g1, g2, ALU.add).then_inc(part_ready, 1)

            repeat(dve, 4, gate_blocks)
            with dve.Fori(0, ROUNDS - 30):
                topk_round()
            sc = score[:, score_at(2):score_at(TB)]
            dve.tensor_scalar(sc, sc, TAKEN / 2, NEG, ALU.is_gt, ALU.mult)
            meet(dve, "dve", met_n)

            for n in range(DSA_STEPS):
                i, e = n // ATT_H, n % 8
                w = P * (i + 1)
                dve.wait_ge(lg_ready, TB + n + 1)
                if n >= 2:
                    dve.wait_ge(lg_t, TB + n - 1)
                dve.tensor_tensor_reduce(out=T[:, n % 2, 0:w], in0=side[:, n % 2, 0:w],
                                         in1=score[:, score_at(i):score_at(i) + w], scale=1.0, scalar=TAKEN, op0=ALU.add,
                                         op1=ALU.max, accum_out=row_max[:, e:e + 1])
                dve.drain()
                dve.tensor_scalar(neg_max[:, e:e + 1], row_max[:, e:e + 1], -SCALE, None, ALU.mult).then_inc(lg_max, 1)
                dve.wait_ge(lg_exp, TB + n + 1)
                dve.reciprocal(inv_sum[:, e:e + 1], row_sum[:, e:e + 1])
                dve.drain()
                dve.tensor_scalar(T[:, n % 2, 0:w], T[:, n % 2, 0:w], inv_sum[:, e:e + 1], None, ALU.mult
                                  ).then_inc(lg_p, 1)
            meet(dve, "dve", met_n)

            for k in range(3):
                low((ya_hi[:, k, :], ya_lo[:, k, :]), k, ya_f[:, k, :], "ya", k + 1)
            for j in range(KB):
                t, m = T_ATT + j // 2, j // 2
                src = dense[:, t % 2, :] if j % 2 == 0 else side[:, m % 2, :]
                dve.wait_ge(fetched[j % 2], 32 * (j // 2 + 1))
                if j % 2 == 0:
                    dve.wait_ge(first_done, 8 + m + 1)
                else:
                    dve.wait_ge(tile_done, t + 1)
                dve.tensor_tensor(T[:, j % 2, :], src, back[:, 2 * (j % 2), :], ALU.mult
                                  ).then_inc(sums_free[t % 2] if j % 2 == 0 else att_free[m % 2], 1)
                dve.drain()
                dve.tensor_tensor(T[:, j % 2, :], T[:, j % 2, :], back[:, 2 * (j % 2) + 1, :], ALU.add
                                  ).then_inc(merged_sum, 1)
                low((a_hi[:, j, :], a_lo[:, j, :]), j, T[:, j % 2, :], "merged", j + 1)
            dve.wait_ge(x_back, 16)
            for n in range(KB):
                u = T_WO + n
                dve.wait_ge(tile_done, T_WO + n + 1)
                dve.tensor_tensor(x_res[:, n, :], x_res[:, n, :], dense[:, u % 2, :], ALU.add
                                  ).then_inc(sums_free[u % 2], 1)
            meet(dve, "dve", met_n)

            def third(k):
                return T[:, (0, 1, 3)[k % 3], :]

            inverse_std(TB)
            scale_all(lambda k: x_res[:, k, :], third, "g_ffn", "h2", a_hi, a_lo, S, ring=3)
            dve.wait_ge(parts["mem2"][0], 1)
            for k in range(KB):
                dve.tensor_tensor(m_lo[:, k, :], m_in[:, k, :], m_hi[:, k, :].bitcast(F32), ALU.subtract
                                  ).then_inc(parts["mem2"][1], 1)

            def down(i, t0, u0, per, n0):
                for n in range(KB):
                    u = u0 + n
                    if n % 2 == 0:
                        dve.wait_ge(first_done, i * (KB // 2) + (n0 + n // 2 + 1))
                    else:
                        dve.wait_ge(tile_done, i * per + (t0 + n // 2 + 1))
                    dve.tensor_tensor(x_res[:, n, :], x_res[:, n, :], dense[:, u % 2, :], ALU.add
                                      ).then_inc(sums_free[u % 2], 1)

            def gated(i, t0, u0, n_f, f0, per, n0):
                cols = SMALL["taps_ff"] + 6 * f0
                dve.drain()
                dve.tensor_copy(taps_dve[:, 0:6 * n_f], small[:, bass.ds(i * (6 * FG) + cols, 6 * n_f)]
                                if not isinstance(i, int) else small[:, cols:cols + 6 * n_f])
                dve.drain()
                for f in range(n_f):
                    for c in range(2):
                        u, slot = u0 + 2 * f + c, 2 * (f % 2) + c
                        dve.wait_ge(tap_ready, i * (2 * FG) + (2 * (f0 + f) + c + 1))
                        for d in (1, 2):
                            tap = taps_dve[:, 6 * f + 3 * c + 2 - d:6 * f + 3 * c + 3 - d]
                            last = dve.scalar_tensor_tensor(T[:, slot, d:S], dense[:, u % 2, 0:S - d], tap, T[:, slot, d:S],
                                                            ALU.mult, ALU.add)
                            if d == 1:
                                dve.drain()
                        last.then_inc(sums_free[u % 2], 1)
                        dve.drain().then_inc(taps_done, 1)
                    g, v = T[:, 2 * (f % 2), :], T[:, 2 * (f % 2) + 1, :]
                    dve.wait_ge(acted, i * FG + (f0 + f + 1))
                    dve.tensor_tensor(g, g, v, ALU.mult).then_inc(product_ready, 1)
                    dve.wait_ge(parts["hidden"][0], i * FG + (f0 + f + 1))
                    dve.tensor_tensor(b_lo[:, f, :], g, b_hi[:, f, :].bitcast(F32), ALU.subtract
                                      ).then_inc(parts["hidden"][1], 1)
                down(i, t0 + 2 * n_f, u0 + 2 * n_f, per, n0)

            repeat(dve, FULL, lambda i: gated(i, T_FF, T_FF, FG, 0, FF_TILES, 12))
            gated(0, T_REST, U_REST, REST, FULL * FG, 0, 12 + FULL * KB // 2)
            meet(dve, "dve", met_n)

            inverse_std(TB)
            scale_all(lambda k: x_res[:, k, :], lambda k: x_res[:, k, :], "g_final", "x2", a_hi, a_lo, S)
            memory(T_MEM2, U_MEM2, None, TB + DSA_STEPS, 1, 0)
            meet(dve, "dve", met_n)

            def strip(t, n, c0):
                return t[:, (n % 4) // 2, (n % 2) * 512 + c0:(n % 2) * 512 + 512]

            def zbank(n, c0=0):
                return side[:, (n % 4) // 2, (n % 2) * 512 + c0:(n % 2) * 512 + 512]

            def stick_pairs(i):
                for pr in range(2):
                    u = U_SB + 3 * pr
                    dve.wait_ge(sb_round, i * 4 + (2 * pr + 1))
                    dve.scalar_tensor_tensor(sq_lo[:, :], dense[:, u % 2, :], SCALE, sq_hi[:, :].bitcast(F32), ALU.mult,
                                             ALU.subtract).then_inc(sums_free[u % 2], 1)
                    dve.wait_ge(sb_round, i * 4 + (2 * pr + 2))
                    dve.tensor_tensor(sk_lo[:, :], dense[:, (u + 1) % 2, :], sk_hi[:, :].bitcast(F32), ALU.subtract
                                      ).then_inc(sums_free[(u + 1) % 2], 1)
                    dve.wait_ge(sb_vturned, i * 2 + (pr + 1))
                    dve.tensor_copy(sv_f[:, :, :], side[:, 0, :].rearrange("p (b d) -> p b d", d=P)).then_inc(sb_v, 1)
                    n0 = NS * pr
                    for n in range(NS + 2):
                        if n < NS:
                            e = strip(T[:, 0:2, :], n, PLAN[n][3])
                            dve.wait_ge(e_ready, i * (2 * NS) + (n0 + n + 1))
                            dve.tensor_scalar(e, e, BIG_E, None, ALU.min).then_inc(e_clip, 1)
                        if 1 <= n <= NS:
                            m = n - 1
                            hh, th, a, c0 = PLAN[m]
                            sp = strip(T[:, 0:2, :], m, c0)
                            dve.wait_ge(ln_ready, i * (2 * NS) + (n0 + m + 1))
                            dve.tensor_tensor(sp, sp, zbank(m, c0), ALU.max)
                            dve.drain()
                            if a >= 4 * th:
                                dve.tensor_tensor(sp[:, 0:P], sp[:, 0:P], mats["strict_mul"][:, :], ALU.mult)
                                dve.drain()
                            dve.drain().then_inc(sp_ready, 1)
                            if a > 0:
                                to = T[:, 2:4, :]
                                if a == 4 * th + 3:
                                    dve.tensor_copy(strip(to, m + 1, c0), sp)
                                else:
                                    c1 = PLAN[m - 1][3]
                                    dve.tensor_tensor(strip(to, m + 1, c1), strip(to, m, c1), sp[:, c1 - c0:], ALU.add)
                                    if c1 > c0:
                                        dve.tensor_copy(strip(to, m + 1, c0)[:, 0:c1 - c0], sp[:, 0:c1 - c0])
                                dve.drain()
                    dve.wait_ge(pv_done, i * (2 * NS) + (n0 + NS))
                    for hh in range(2):
                        r = slice(HD * hh, HD * hh + HD)
                        for th in range(2):
                            tk = slice(512 * th, 512 * th + 512)
                            dst = (y2_f[r, bass.ds(i * 2 + pr, 1), tk].rearrange("p a s -> p (a s)")
                                   if not isinstance(i, int) else y2_f[r, pr, tk])
                            dve.tensor_scalar(dst, dense[r, hh, tk], 1.0, None, ALU.mult).then_inc(y_copied, 1)

            repeat(dve, SB_H // 4, stick_pairs)
            meet(dve, "dve", met_n)

            for k in range(KB):
                low((a_hi[:, k, :], a_lo[:, k, :]), k, y2_f[:, k, :], "y2", k + 1)
            for n in range(KB):
                u = U_OUT2 + n
                dve.wait_ge(tile_done, T_OUT2 + n + 1)
                dve.scalar_tensor_tensor(x_res[:, n, :], x_res[:, n, :], ALPHA, dense[:, u % 2, :], ALU.mult, ALU.add
                                         ).then_inc(sums_free[u % 2], 1)
            meet(dve, "dve", met_n)

            def layer_norm(gain, which):
                dve.drain().then_inc(centred, 1)
                norm_n["mean"] += 1
                dve.wait_ge(mean_ready, mean_at[norm_n["mean"] - 1])
                diagonals(side[:, 0, :], TB)
                for k in range(KB):
                    dve.tensor_tensor(x_res[:, k, :], x_res[:, k, :], side[:, 1, :], ALU.subtract).then_inc(centred, 1)
                inverse_std(TB)
                for k in range(KB + 1):
                    if k < KB:
                        if k >= 3:
                            dve.wait_ge(shifted, norm_n["shift"] + k - 2)
                        dve.scalar_tensor_tensor(third(k), x_res[:, k, :], par(gain, k), side[:, 1, :], ALU.mult, ALU.mult
                                                 ).then_inc(scaled, 1)
                    if k and which is not None:
                        m = k - 1
                        low((a_hi[:, m, :], a_lo[:, m, :]), m, x_res[:, m, :], which, m + 1)
                        dve.drain()
                        dve.tensor_scalar(x_res[:, m, :], x_res[:, m, :], ALPHA, None, ALU.mult)
                norm_n["shift"] += KB

            mean_at = [5, 7]
            layer_norm("ln1_g", "x3")

            def squared_relu(i):
                for f in range(FG):
                    u = U_FF2 + f
                    dve.wait_ge(tile_done, i * FF2_TILES + (T_FF2 + f + 1))
                    dve.tensor_scalar(T[:, f, :], dense[:, u % 2, :], 0.0, None, ALU.max)
                    dve.drain()
                    dve.tensor_tensor(T[:, f, :], dense[:, u % 2, :], T[:, f, :], ALU.mult).then_inc(squared, 1)
                    dve.drain().then_inc(sums_free[u % 2], 1)
                    dve.wait_ge(parts["hidden2"][0], i * FG + (f + 1))
                    dve.tensor_tensor(b_lo[:, f, :], T[:, f, :], b_hi[:, f, :].bitcast(F32), ALU.subtract
                                      ).then_inc(parts["hidden2"][1], 1)
                down(i, T_FF2 + FG, U_FF2 + FG, FF2_TILES, 12 + FULL * KB // 2 + KB // 2)

            repeat(dve, FF2_GROUPS, squared_relu)
            meet(dve, "dve", met_n)
            layer_norm("ln2_g", None)
            meet(dve, "dve", met_n)


def blocks_of(w, rows, cols):
    return np.stack([w[r][:, cols] for r in rows], axis=1)


def pack(x):
    tiles = np.zeros((TILES, P, KB, P), np.float32)
    n = [0]

    def put(*parts):
        at = 0
        for w, rows, cols in parts:
            b = blocks_of(w, rows, cols)
            tiles[n[0], :, at:at + b.shape[1], :b.shape[2]] = b
            at += b.shape[1]
        n[0] += 1

    def rows(*ks):
        return [slice(P * k, P * k + P) for k in ks]

    full = rows(*range(KB))
    w = x["w_in"][0]
    off = np.cumsum([0, 384, 128, 128, 256, 32, 8, CONV, CONV, CONV, 256])
    o_q, o_k, o_v, o_qi, o_ki, _, o_bg, o_cg, o_u, o_qc, o_gate = off

    def cols(o, j=0):
        return slice(o + P * j, o + P * j + P)

    put((w, full, slice(o_ki, o_ki + IDX_D + IDX_H)))
    for j in range(2):
        put((w, full, cols(o_qi, j)))
    put((w, full, cols(o_k)))
    two = [np.r_[HD * j:HD * j + HD, HD * (j + 3):HD * (j + 3) + HD] for j in range(3)]
    for j in range(3):
        put((w, full, o_q + two[j]))
    put((w, full, cols(o_v)))
    for j in range(4):
        put((x["w_mem_kv"][0], full, cols(0, j)))
    for j in range(2):
        put((w, full, cols(o_qc, j)))
    for j in range(3):
        for o in (o_cg, o_u, o_bg):
            put((w, full, cols(o, j)))
    for j in range(KB):
        for b in range(3):
            put((w, full, cols(o_gate + D * b, j)))
        put((x["w_conv_out"][0], rows(0, 1, 2), cols(0, j)), (x["w_mem_out"][0], rows(0, 1), cols(0, j)))
    for j in range(0, KB, 2):
        put((x["w_att_out"][0], two, cols(0, j)), (x["w_att_out"][0], two, cols(0, j + 1)))
    for j in range(KB):
        put((x["w_o"][0], full, cols(0, j)))
    for f0 in range(0, FB, FG):
        group = range(f0, min(FB, f0 + FG))
        for f in group:
            put((x["w_up"][0], full, cols(0, f)))
            put((x["w_up"][0], full, cols(FF, f)))
        for j in range(0, KB, 2):
            put((x["w_down"][0], rows(*group), cols(0, j)), (x["w_down"][0], rows(*group), cols(0, j + 1)))
    for j in range(4):
        put((x["w_mem_kv_2"][0], full, cols(0, j)))
    w = x["w_in_sb_2"][0]
    o_k, o_v, o_qc = SB_H * HD, 2 * SB_H * HD, 3 * SB_H * HD
    for j in range(2):
        put((w, full, cols(o_qc, j)))
    for j in range(SB_H // 2):
        for o in (0, o_k, o_v):
            put((w, full, cols(o, j)))
    for j in range(KB):
        put((x["w_out_2"][0], full, cols(0, j)))
    for f0 in range(0, FB2, FG):
        group = range(f0, f0 + FG)
        for f in group:
            put((x["w_up_2"][0], full, cols(0, f)))
        for j in range(0, KB, 2):
            put((x["w_down_2"][0], rows(*group), cols(0, j)), (x["w_down_2"][0], rows(*group), cols(0, j + 1)))
    assert n[0] == TILES
    return tiles.reshape(TILES, P, D)


def constants():
    r = np.arange(P)
    c = {"ident": np.eye(P), "ones": np.ones((P, P)), "neg_ones": -np.ones((P, P))}

    def partner(d, half):
        return np.where(d % (8 * half) < half, d + half, d - half)

    def swap(half):
        m = np.zeros((P, P))
        turn = r[r % (8 * half) < 2 * half]
        m[partner(turn, half), turn] = 1
        return m

    c["swap_att"], c["swap_idx"] = swap(8), swap(4)
    c["rep_ki"] = (r[:, None] == r[None, :] % IDX_D).astype(float)
    c["rep_swap_ki"] = c["swap_idx"][:, r % IDX_D] * (r[:, None] < IDX_D)
    c["causal_q"] = np.where(r[None, :] <= r[:, None], 0.0, NEG)
    c["strict_mul"] = (r[:, None] < r[None, :]).astype(float)
    c["strict_add"] = np.where(r[:, None] < r[None, :], 0.0, NEG)
    c["neg_later"] = -(r[:, None] >= r[None, :]).astype(float)
    tab = np.zeros((P, 4, S), np.float32)
    for n, half in ((0, 4), (2, 8)):
        freq = np.float32(500000.0) ** (-np.arange(half, dtype=np.float32) / np.float32(half))
        ang = np.arange(S, dtype=np.float32)[:, None] * freq.astype(np.float32)[None, :]
        d = r % (8 * half)
        on = d < 2 * half
        tab[:, n] = np.where(on[:, None], np.cos(ang).T[d % half], 1.0)
        tab[:, n + 1] = np.where(on[:, None], np.where(d < half, -1.0, 1.0)[:, None] * np.sin(ang).T[d % half], 0.0)
    c = {k: np.ascontiguousarray(v, np.float32) for k, v in c.items()}
    c["rope_tab"] = tab
    return c


def small_params(x):
    s = np.zeros((P, SMALL_N), np.float32)

    def put(name, a):
        s[:, SMALL[name]:SMALL[name] + a.shape[1]] = a

    def by_block(v):
        return v.reshape(-1, P).T

    s[:, SMALL["inv_d"]] = 1.0 / D
    for name, src in (("g_mix", "g_mix"), ("g_mem", "g_mem"), ("g_ffn", "g_ffn"), ("ln1_g", "ln_mix_g_2"),
                      ("ln1_b", "ln_mix_b_2"), ("ln2_g", "ln_ffn_g_2"), ("ln2_b", "ln_ffn_b_2")):
        put(name, by_block(x[src][0]))
    put("g_final", by_block(x["g_final"]))
    put("b_gate", x["b_gate"][0].reshape(3, KB, P).transpose(2, 1, 0).reshape(P, 3 * KB))
    put("taps_short", x["conv_w_short"][0].reshape(3, 3, P).transpose(2, 1, 0).reshape(P, 9))
    put("taps_ff", x["conv_w_ffn"][0].reshape(3, 2, FB, P).transpose(3, 2, 1, 0).reshape(P, 6 * FB))
    for h in range(IDX_H):
        s[IDX_D + h, SMALL["pick_wi"] + h] = IDX_SCALE
    return s


def kernel(**inputs):
    import concourse.bacc as bacc
    from concourse.bass_utils import run_bass_kernel_spmd

    x = {k: np.asarray(v) for k, v in inputs.items()}

    def turned(a):
        return np.ascontiguousarray(a[0].reshape(-1, KB, P).transpose(2, 1, 0))

    arrays = {"x_t": turned(x["x"]), "mem_t": turned(x["mem"]), "mem2_t": turned(x["mem_2"]), "w_stream": pack(x),
              "small": small_params(x), **constants()}
    nc = bacc.Bacc("TRN2", target_bir_lowering=False, num_devices=1, dynamic_dma_scratch_size=1024)
    io = {k: nc.dram_tensor("in_" + k, a.shape, F32, kind="ExternalInput").ap() for k, a in arrays.items()}
    out = nc.dram_tensor("out_t", (P, KB, S), F32, kind="ExternalOutput").ap()
    build(nc, io, out)
    r = run_bass_kernel_spmd(nc, [{"in_" + k: a for k, a in arrays.items()}], core_ids=[0])
    y = r.results[0]["out_t"]
    return np.ascontiguousarray(y.transpose(2, 1, 0).reshape(1, S, D))
```

```python
from contextlib import ExitStack

import numpy as np

import concourse.bass as bass
from concourse import mybir

F32 = mybir.dt.float32
F32R = mybir.dt.float32r
ACT = mybir.ActivationFunctionType
ALU = mybir.AluOpType
AX = mybir.AxisListType

P = 128
S = 1024
D = 1024
KB = D // P
TB = S // P
MEM = 256
HD = 64
ATT_H, GROUPS = 6, 2
IDX_H, IDX_D = 8, 32
TOPK = 256
CONV = 384
FF, FF2 = 2816, 4096
SB_H = 12
FB, FB2 = FF // P, FF2 // P
FG = 4
EPS_RMS, EPS_LN = 1e-6, 1e-5
ALPHA = 2.0 ** 0.25
SCALE = HD ** -0.5
IDX_SCALE = (IDX_H * IDX_D) ** -0.5
NEG = -1e30
TAKEN = -3e38
BIG_E = 2.0 ** 60
RAW = 2

T_KI = 0
T_QI = 1
T_K = 3
T_Q = 4
T_V = 7
T_MEM = 8
T_CONV = 14
T_GATE = 23
T_ATT = T_GATE + 4 * KB
T_WO = T_ATT + KB // 2
T_FF = T_WO + KB
FULL, REST = FB // FG, FB % FG
FF_TILES = 2 * FG + KB // 2
T_KV2 = T_FF + FULL * FF_TILES
T_REST = T_KV2 + 4
T_MEM2 = T_REST + 2 * REST + KB // 2
T_SB = T_MEM2 + 2
T_OUT2 = T_SB + 3 * SB_H // 2
T_FF2 = T_OUT2 + KB
FF2_GROUPS = FB2 // FG
FF2_TILES = FG + KB // 2
TILES = T_FF2 + FF2_GROUPS * FF2_TILES
FF_USES = 2 * FG + KB
U_KV2 = T_FF + FULL * FF_USES
U_REST = U_KV2 + 4
U_MEM2 = U_REST + 2 * REST + KB
U_SB = U_MEM2 + 2
U_OUT2 = U_SB
U_FF2 = U_OUT2 + KB
FF2_USES = FG + KB

SMALL, _at = {}, 0
for _name, _n in (("inv_d", 1), ("g_mix", KB), ("g_mem", KB), ("g_ffn", KB), ("g_final", KB), ("ln1_g", KB),
                  ("ln1_b", KB), ("ln2_g", KB), ("ln2_b", KB), ("b_gate", 3 * KB), ("taps_short", 9),
                  ("pick_wi", IDX_H), ("taps_ff", 6 * FB)):
    SMALL[_name] = _at
    _at += _n
SMALL_N = _at
ROUNDS = TOPK // 8
IDX_STEPS = (TB - TOPK // P) * IDX_H
DSA_STEPS = TB * ATT_H
IDX_S = S - TOPK
STACK = 3 * IDX_D
MATRICES = ("ident", "ones", "swap_att", "swap_idx", "rep_ki", "rep_swap_ki", "causal_q", "strict_add", "neg_later",
            "neg_earlier")


def stick_plan():
    return [(hh, th, a, max(0, a * P - 512 * th)) for th in range(2) for a in range(4 * th + 3, -1, -1)
            for hh in range(2)]


PLAN = stick_plan()
NS = len(PLAN)
BODY = 2 * NS
CARRIES = np.cumsum([PLAN[n % NS][2] > 0 for n in range(BODY)]).tolist()
BETWEEN = {0: (0, 0, 2), 1: (0, 2, 4), **{n: (0, n + 2, n + 3) for n in range(2, 6)},
           9: (1, 0, 2), 10: (1, 2, 4), 11: (1, 4, 6), 12: (1, 6, 7), 13: (1, 7, 8),
           15: (2, 0, 2), **{n: (2, n - 14, n - 13) for n in range(16, 22)}}
SPLIT_STEPS = (1, 7, 15)
SUM_LAG, PV_LAG = 3, 5
COPY_V, TURN_V, SPLIT_V, COPY_K, COPY_Q = 6, 7, 8, 14, 22


def score_at(i):
    return P * (i * (i + 1) // 2)


def repeat(eng, n, body):
    body(0)
    with eng.Fori(1, n) as i:
        body(i)


def build(nc, io, out):
    with ExitStack() as ctx:
        base = (nc.sbuf_base + 31) // 32 * 32

        def at(name, shape, dtype, kib):
            return nc.alloc_sbuf_tensor_at(name, shape, dtype, offset=base + int(kib * 1024))

        def sem(name):
            return ctx.enter_context(nc.semaphore(name))

        def pair(name):
            return [sem(f"{name}{s}") for s in range(2)]

        raw = at("raw", [P, RAW, D], F32, 0)
        w_hi = at("w_hi", [P, 2, D], F32R, 8)
        w_lo = at("w_lo", [P, 2, D], F32R, 16)
        a_hi = at("a_hi", [P, KB, S], F32R, 24)
        a_lo = at("a_lo", [P, KB, S], F32R, 56)
        T = at("T", [P, 4, S], F32, 88)
        mats = {name: at(name, [P, P], F32, 104 + 0.5 * n) for n, name in enumerate(MATRICES)}
        ident, ones = mats["ident"], mats["ones"]
        small = at("small", [P, SMALL_N], F32, 109.5)
        tiny = at("tiny", [P, 256], F32, 110.75)
        bias_now = tiny[:, 224:225]
        zero = at("zero", [P, 8], F32, 111.75)
        Y0 = 112
        k_f = at("k_f", [P, S], F32, Y0)
        q_f = at("q_f", [P, 3, S], F32, Y0 + 4)
        v_f = at("v_f", [P, TB, P], F32, Y0 + 16)
        score = at("score", [P, score_at(TB)], F32, Y0 + 20)
        rope_tab = at("rope_tab", [P, 4, S], F32, Y0 + 20)
        x_in = at("x_in", [P, KB, S], F32, Y0 + 38)
        qi_f = at("qi_f", [P, 2, S], F32, Y0 + 38)
        ki_f = at("ki_f", [P, S], F32, Y0 + 46)
        qc_f = at("qc_f", [P, 2, S], F32, Y0 + 98)
        m_hi = at("m_hi", [P, KB, MEM], F32R, Y0 + 74)
        m_lo = at("m_lo", [P, KB, MEM], F32R, Y0 + 82)
        ym_f = at("ym_f", [P, 2, S], F32, Y0 + 74)
        ym_hi = at("ym_hi", [P, 2, S], F32R, Y0 + 58)
        ym_lo = at("ym_lo", [P, 2, S], F32R, Y0 + 66)
        km_f = at("km_f", [P, 2, MEM], F32, Y0 + 90)
        vm_f = at("vm_f", [P, 2, MEM], F32, Y0 + 92)
        vm_t = at("vm_t", [P, 2, MEM], F32, Y0 + 94)
        m_in = at("m_in", [P, KB, MEM], F32, Y0 + 98)
        qi_hi, qi_lo = (at(n, [P, 2, IDX_S], F32R, 88 + 6 * m) for m, n in enumerate(("qi_hi", "qi_lo")))
        ki_hi, ki_lo = (at(n, [P, S], F32R, Y0 + 98 + 4 * m) for m, n in enumerate(("ki_hi", "ki_lo")))
        stack_in = at("stack_in", [P, 4 * STACK], F32, Y0 + 36)
        stack_mats = at("stack_mats", [P, 4, STACK], F32R, Y0 + 106)
        ki_stack = at("ki_stack", [P, S], F32R, Y0 + 46)
        qi_stack = at("qi_stack", [P, IDX_H, IDX_S], F32R, Y0 + 50)
        yc_hi = at("yc_hi", [P, 3, S], F32R, Y0 + 74)
        yc_lo = at("yc_lo", [P, 3, S], F32R, Y0 + 86)
        gates = at("gates", [P, 4, S], F32, Y0 + 38)
        ya_f = at("ya_f", [P, 3, S], F32, Y0 + 38)
        ya_hi = at("ya_hi", [P, 3, S], F32R, Y0 + 50)
        ya_lo = at("ya_lo", [P, 3, S], F32R, Y0 + 62)
        back = at("back", [P, 4, S], F32, Y0 + 74)
        x_res = at("x_res", [P, KB, S], F32, Y0)
        b_hi = at("b_hi", [P, FG, S], F32R, Y0 + 38)
        b_lo = at("b_lo", [P, FG, S], F32R, Y0 + 54)
        qc2_f = at("qc2_f", [P, 2, S], F32, Y0 + 38)
        y2_f = at("y2_f", [P, KB, S], F32, Y0 + 38)
        sq_hi, sq_lo, sk_hi, sk_lo = (at(n, [P, 2, S], F32R, Y0 + 8 * m) for m, n in enumerate(("sq_hi", "sq_lo", "sk_hi",
                                                                                               "sk_lo")))
        sv_t = at("sv_t", [P, S], F32, Y0 + 32)
        stick_mats = at("stick_mats", [P, 4, P], F32R, Y0 + 36)
        ident_r, strict_r, later_r, earlier_r = (stick_mats[:, n, :] for n in range(4))
        sv_hi, sv_lo = (at(n, [P, 2, TB, P], F32R, Y0 + 70 + 8 * m) for m, n in enumerate(("sv_hi", "sv_lo")))
        z_ring = at("z_ring", [P, 6, 512], F32, Y0 + 86)
        sp_hi, sp_lo = (at(n, [P, 3, 512], F32R, Y0 + 98 + 6 * m) for m, n in enumerate(("sp_hi", "sp_lo")))
        sp_ring = at("sp_ring", [P, 4, 512], F32, 88)
        stick_hi, stick_lo = (at(n, [P, 2, 512], F32R, 96 + 4 * m) for m, n in enumerate(("stick_hi", "stick_lo")))

        def par(name, k=0):
            return small[:, SMALL[name] + k:SMALL[name] + k + 1]

        row_max, neg_max = tiny[:, 0:8], tiny[:, 8:16]
        row_sum, inv_sum = tiny[:, 16:24], tiny[:, 24:32]
        std, rstd = tiny[:, 32:40], tiny[:, 40:48]
        best = tiny[:, 48:96].rearrange("p (b e) -> p b e", e=8)
        taps_act, taps_dve = tiny[:, 96:96 + 6 * FG], tiny[:, 128:128 + 6 * FG]
        wi_f = tiny[:, 160:160 + TB * IDX_H].rearrange("p (i h) -> p i h", h=IDX_H)

        dense = ctx.enter_context(nc.psum_tensor("dense", [P, 2, S], F32))
        side = ctx.enter_context(nc.psum_tensor("side", [P, 2, S], F32))

        weights_loaded = [sem(f"weights_loaded{r}") for r in range(RAW)]
        weights_rounded, weights_split = sem("weights_rounded"), sem("weights_split")
        tile_done, first_done = sem("tile_done"), sem("first_of_two_done")
        sums_free = pair("sums_free")
        consts_in, tables_in, x_back, out_stored = sem("consts_in"), sem("tables_in"), sem("x_back"), sem("out_stored")
        x_loaded = [sem(f"x_loaded{c}") for c in range(4)]
        mem_loaded, mem2_loaded = sem("mem_loaded"), sem("mem2_loaded")
        met = {e: sem(f"met_{e}") for e in ("pe", "act", "dve")}
        squares, squares_used = sem("squares_ready"), sem("squares_used")
        mean_ready, std_ready, diag_ready, spread_ready = (sem("mean_ready"), sem("std_ready"), sem("diagonals_ready"),
                                                           sem("spread_ready"))
        scaled, shifted = sem("scaled_ready"), sem("shifted_ready")
        centred = sem("centred_ready")
        parts = {n: (sem(n + "_rounded"), sem(n + "_split")) for n in (
            "h", "mem", "ym", "yc", "ya", "merged", "h2", "hidden", "x2", "mem2", "y2", "x3", "hidden2")}
        yc_ready = sem("conv_out_ready")
        turned, roped, turn_free = sem("proj_turned"), sem("proj_rotated"), pair("turn_free")
        idx_round, idx_split, stacked, stack_copied = (sem("index_rounded"), sem("index_split"), sem("index_stacked"),
                                                       sem("index_stack_copied"))
        idx_ready, rel_ready, rel_used = sem("index_products"), sem("relu_ready"), sem("relu_used")
        mturned = sem("mem_values_turned")
        lg_ready, lg_max, lg_exp, lg_p = sem("logits_ready"), sem("row_max_ready"), sem("exp_ready"), sem("probs_ready")
        lg_t, lg_tc, lg_o, lg_oc = (sem("probs_turned"), sem("probs_copied"), sem("heads_ready"), sem("heads_copied"))
        conv_used = sem("conv_gate_used")
        part_ready, branch_free = sem("partial_ready"), pair("branch_free")
        gate_spilled, part_spilled, fetched = pair("gate_spilled"), pair("partial_spilled"), pair("fetched")
        att_sums, att_free, merged_sum = sem("att_out_ready"), pair("att_out_free"), sem("merged_ready")
        tap_ready, taps_done, acted = sem("first_tap_ready"), sem("taps_done"), sem("hidden_gate_ready")
        product_ready, squared = sem("hidden_product_ready"), sem("hidden_squared")
        v_copied, v_turned, v_rounded, v_split = (sem("stick_values_copied"), sem("stick_values_turned"),
                                                  sem("stick_values_rounded"), sem("stick_values_split"))
        qk_rounded, qk_split = sem("stick_qk_rounded"), sem("stick_qk_split")
        z_copied = sem("z_copied")
        z_ready, e_ready, e_clip, ln_ready, sp_ready = (sem("z_ready"), sem("exp_z_ready"), sem("exp_z_clipped"),
                                                        sem("log_ready"), sem("softplus_ready"))
        sp_round, sp_split = sem("softplus_rounded"), sem("softplus_split")
        later_ready, carried, arg_ready = sem("later_sums_ready"), sem("carried"), sem("exponent_ready")
        w_ready, w_round, w_split = sem("stick_weights_ready"), sem("stick_weights_rounded"), sem("stick_weights_split")
        pv_done, y_copied = sem("stick_pv_done"), sem("stick_heads_copied")
        x_spilled, x_returned = sem("x_spilled"), [sem(f"x_returned{n}") for n in range(2)]

        spill_gate = nc.dram_tensor("spill_gate", [KB, P, S], F32).ap()
        spill_x = nc.dram_tensor("spill_x", [P, KB, S], F32).ap()
        spill_part = nc.dram_tensor("spill_part", [KB, P, S], F32).ap()

        block = ctx.enter_context(nc.Block())

        def out_bank(hh, c0=0):
            return dense[:, 1, 512 * hh + c0:512 * hh + 512]

        def sum_bank(hh, c0=0):
            return side[:, 0, 512 * hh + c0:512 * hh + 512]

        def z_bank(n, c0=0):
            return side[:, 1, 512 * (n % 2) + c0:512 * (n % 2) + 512]

        def sp_strip(n):
            return sp_ring[:, n % 4, PLAN[n % NS][3]:512]

        def z_strip(n):
            return z_ring[:, n % 6, PLAN[n % NS][3]:512]

        def group_end(n):
            hh, th, a, _ = PLAN[n % NS]
            return 2 * (n // NS) + th if hh == 1 and a == 0 else None

        def emptied(eng, u, i=0, per=0):
            eng.wait_ge(sums_free[u % 2], i * (per // 2) + (u // 2 + 1))

        def meet(eng, me, count):
            count[0] += 1
            eng.drain().then_inc(met[me], 1)
            for other in met:
                if other != me:
                    eng.wait_ge(met[other], count[0])

        @block.sync
        def _(sp):
            sp.dma_start(m_in[:, :, :], io["mem_t"]).then_inc(mem_loaded, 16)
            sp.dma_start(small[:, :], io["small"]).then_inc(consts_in, 16)
            for name in MATRICES:
                sp.dma_start(mats[name][:, :], io[name]).then_inc(consts_in, 16)
            for c in range(4):
                sp.dma_start(x_in[:, 2 * c:2 * c + 2, :], io["x_t"][:, 2 * c:2 * c + 2, :]).then_inc(x_loaded[c], 16)
            for r in range(RAW):
                sp.dma_start(raw[:, r, :], io["w_stream"][r]).then_inc(weights_loaded[r], 16)
            sp.dma_start(rope_tab[:, :, :], io["rope_tab"]).then_inc(tables_in, 16)
            sp.dma_start(stack_in[:, :], io["stack_mats"]).then_inc(tables_in, 16)
            with sp.Fori(1, TILES // RAW) as i:
                for r in range(RAW):
                    sp.wait_ge(weights_split, i * RAW + (r - RAW + 1))
                    sp.dma_start(raw[:, r, :], io["w_stream"][bass.ds(i * RAW + r, 1)].rearrange("a p k -> p (a k)")
                                 ).then_inc(weights_loaded[r], 16)
            for r in range(TILES % RAW):
                t = TILES // RAW * RAW + r
                sp.wait_ge(weights_split, t - RAW + 1)
                sp.dma_start(raw[:, r, :], io["w_stream"][t]).then_inc(weights_loaded[r], 16)

        CONSTS = 16 * (len(MATRICES) + 1)

        @block.gpsimd
        def _(pool):
            def split(t, r, loads):
                pool.wait_ge(weights_loaded[r], loads)
                pool.tensor_tensor(w_hi[:, r % 2, :], raw[:, r, :], zero[:, 0:1].broadcast_to([P, D]), ALU.add).then_inc(weights_rounded, 1)
                pool.wait_ge(weights_rounded, t + 1)
                pool.tensor_tensor(w_lo[:, r % 2, :], raw[:, r, :], w_hi[:, r % 2, :].bitcast(F32), ALU.subtract
                                   ).then_inc(weights_split, 1)

            pool.memset(zero[:, :], 0.0)
            pool.drain()
            for r in range(RAW):
                if r >= 2:
                    pool.wait_ge(tile_done, r - 1)
                split(r, r, 16)
            def split_tiles(begin, end):
                def one(t):
                    pool.wait_ge(tile_done, t - 1)
                    split(t, t % RAW, 16 * (t // RAW) + 16)

                if begin % RAW:
                    one(begin)
                with pool.Fori(-(-begin // RAW), end // RAW) as i:
                    for r in range(RAW):
                        pool.wait_ge(tile_done, i * RAW + (r - 1))
                        split(i * RAW + r, r, i * 16 + 16)
                if end % RAW:
                    one(end - 1)

            def split_quarter(t, i, q):
                half = slice(q % 2 * 512, q % 2 * 512 + 512)
                raw_t, hi, lo = raw[:, t % RAW, half], w_hi[:, t % 2, half], w_lo[:, t % 2, half]
                if q == 0:
                    pool.wait_ge(weights_loaded[t % RAW], i * (6 // RAW * 16) + 16 * (t // RAW + 1))
                    pool.wait_ge(tile_done, i * 6 + (t - 1))
                if q == 2:
                    pool.wait_ge(weights_rounded, i * 6 + (t + 1))
                done = None
                if q < 2:
                    done = pool.tensor_tensor(hi, raw_t, zero[:, 0:1].broadcast_to([P, 512]), ALU.add)
                else:
                    done = pool.tensor_tensor(lo, raw_t, hi.bitcast(F32), ALU.subtract)
                if q % 2:
                    done.then_inc(weights_rounded if q == 1 else weights_split, 1)

            def stick_pairs(i, end=False):
                for n in range(BODY + SUM_LAG + 1):
                    if 2 <= n < BODY + 2:
                        m, c0 = n - 2, PLAN[(n - 2) % NS][3]
                        pool.wait_ge(sp_round, i * BODY + (m + 1))
                        pool.tensor_tensor(sp_lo[:, m % 3, c0:512], sp_strip(m), sp_hi[:, m % 3, c0:512].bitcast(F32),
                                           ALU.subtract).then_inc(sp_split, 1)
                    if n > SUM_LAG:
                        m, c0 = n - SUM_LAG - 1, PLAN[(n - SUM_LAG - 1) % NS][3]
                        pool.wait_ge(w_round, i * BODY + (m + 1))
                        pool.tensor_tensor(stick_lo[:, m % 2, c0:512], z_strip(m), stick_hi[:, m % 2, c0:512].bitcast(F32),
                                           ALU.subtract).then_inc(w_split, 1)
                    if n < BODY:
                        for c, at_step in enumerate(SPLIT_STEPS):
                            if 0 <= n % NS - at_step < 4 and not (end and n >= NS and c):
                                split_quarter(T_SB + 3 * (n // NS + 1) + c + 1, i, n % NS - at_step)

            split_tiles(RAW, T_SB + 4)
            with pool.Fori(0, SB_H // 4 - 1) as i:
                stick_pairs(i)
            stick_pairs(SB_H // 4 - 1, end=True)
            split_tiles(T_OUT2 + 2, TILES)

        @block.tensor
        def _(pe):
            met_n, norm_n = [0], {"sq": 0, "mean": 0, "diag": 0}

            def halves(psum, s, width=S):
                return [psum[:, s, c:min(c + 512, width)] for c in range(0, width, 512)]

            def product(slot, outs, hi, lo, blocks, at_block=0, ready=None, begin=0, end=True):
                for b in range(begin, blocks):
                    w = slice(P * (at_block + b), P * (at_block + b) + P)
                    stop = end and b == blocks - 1
                    if ready is not None:
                        pe.wait_ge(ready, b + 1)
                    for c, o in enumerate(outs):
                        x = slice(c * 512, c * 512 + o.shape[-1])
                        pe.matmul(o, w_hi[:, slot, w], hi[:, b, x], start=b == 0, stop=False)
                        pe.matmul(o, w_hi[:, slot, w], lo[:, b, x], start=False, stop=False)
                    for c, o in enumerate(outs):
                        x = slice(c * 512, c * 512 + o.shape[-1])
                        last = pe.matmul(o, w_lo[:, slot, w], hi[:, b, x], start=False, stop=stop)
                return last

            def tile(t, u, hi=a_hi, lo=a_lo, blocks=KB, width=S, at_block=0, ready=None, i=0, per=(0, 0),
                     done=tile_done):
                s = u % 2
                if u >= 2:
                    pe.wait_ge(sums_free[s], i * (per[1] // 2) + u // 2)
                pe.wait_ge(weights_split, i * per[0] + (t + 1))
                product(t % 2, halves(dense, s, width), hi, lo, blocks, at_block, ready).then_inc(done, 1)

            def two_tiles(t, u, ready):
                for m in range(2):
                    if u + m >= 2:
                        pe.wait_ge(sums_free[(u + m) % 2], (u + m) // 2)
                pe.wait_ge(weights_split, t + 2)
                for b in range(KB):
                    pe.wait_ge(ready, b + 1)
                    for m in range(2):
                        last = product((t + m) % 2, halves(dense, (u + m) % 2), a_hi, a_lo, b + 1, begin=b, end=b == KB - 1)
                        if b == KB - 1:
                            last.then_inc(tile_done, 1)

            def mean_part(k, src, blocks):
                for b in range(blocks):
                    last = pe.matmul(side[:, 0, b:b + 1], src[:, b * P:b * P + P], par("inv_d"), start=k == 0 and b == 0,
                                     stop=k == KB - 1, skip_group_check=True)
                return last

            def squares_part(k, blocks=TB):
                pe.wait_ge(squares, norm_n["sq"] + k + 1)
                mean_part(k, T[:, k % 2, :], blocks).then_inc(squares_used if k < KB - 1 else mean_ready, 1)

            def spread(blocks):
                pe.wait_ge(diag_ready, norm_n["diag"] + 1)
                norm_n["diag"] += 1
                for b in range(blocks):
                    last = pe.matmul(side[:, 1, b * P:b * P + P], ones[:, :], T[:, 2, b * P:b * P + P], start=True,
                                     stop=True, skip_group_check=True)
                last.then_inc(spread_ready, 1)

            def rms(blocks, begin=0):
                for k in range(begin, KB):
                    squares_part(k, blocks)
                norm_n["sq"] += KB
                spread(blocks)

            def residual_mean(k, u):
                emptied(pe, u + k)
                last = mean_part(k, x_res[:, k, :], TB)
                if k == KB - 1:
                    last.then_inc(mean_ready, 1)

            def layer_norm():
                spread(TB)
                rms(TB)

            pe.wait_ge(consts_in, CONSTS)
            rms(MEM // P)
            rms(TB)

            def turn(n, src, matrices):
                for m, (v, matrix) in enumerate(matrices):
                    if m == 0:
                        emptied(pe, n)
                    if v >= 2:
                        pe.wait_ge(turn_free[v % 2], v // 2)
                    for c in range(0, S, 512):
                        last = pe.matmul(side[:, v % 2, c:c + 512], matrix[:, :], src[:, c:c + 512], start=True, stop=True)
                    last.then_inc(turned, 1)

            for t in range(T_KI, T_MEM):
                if t == 0:
                    two_tiles(t, t, parts["h"][1])
                elif t >= 2:
                    tile(t, t)
                if t == 1:
                    turn(0, T[:, 0, :], [(0, mats["rep_ki"]), (1, mats["rep_swap_ki"])])
                    pe.wait_ge(turn_free[0], 1)
                    for b in range(TB):
                        last = pe.matmul(side[:, 0, b * IDX_H:b * IDX_H + IDX_H], T[:, 0, b * P:b * P + P],
                                         small[:, SMALL["pick_wi"]:SMALL["pick_wi"] + IDX_H], start=True, stop=True,
                                         skip_group_check=True)
                    last.then_inc(turned, 1)
                elif t >= 2:
                    turn(t - 1, T[:, (t - 1) % 2, :], [(t + 1, mats["swap_idx" if t - 1 < T_K else "swap_att"])])
            emptied(pe, T_V)
            pe.wait_ge(turn_free[1], 4)
            for b in range(TB):
                last = pe.transpose(side[:, 1, b * P:b * P + P], T[:, T_V % 2, b * P:b * P + P], ident[:, :])
            last.then_inc(turned, 1)
            meet(pe, "pe", met_n)

            for n in range(IDX_H + 1):
                width, head = (S, 0) if n == 0 else (IDX_S, n - 1)
                hi, lo = (ki_hi, ki_lo) if n == 0 else (qi_hi[:, head // 4, :], qi_lo[:, head // 4, :])
                r = slice(IDX_D * (head % 4), IDX_D * (head % 4) + IDX_D)
                pe.wait_ge(idx_split, 1 if n == 0 else head // 4 + 2)
                if n >= 2:
                    pe.wait_ge(stack_copied, n - 1)
                for c in range(0, width, 512):
                    e = min(width, c + 512)
                    m = 0 if n == 0 else 2
                    pe.matmul(side[0:STACK, n % 2, c:e], stack_mats[r, m, :], hi[r, c:e], start=True, stop=False)
                    last = pe.matmul(side[0:STACK, n % 2, c:e], stack_mats[r, m + 1, :], lo[r, c:e], start=False, stop=True)
                last.then_inc(stacked, 1)
            pe.wait_ge(stack_copied, IDX_H + 1)

            def memory_block(t, b):
                if b == 0:
                    pe.wait_ge(sums_free[t % 2], t // 2)
                    pe.wait_ge(weights_split, t + 1)
                own = t < T_MEM + 4
                last = product(t % 2, halves(dense, t % 2, MEM if own else S), m_hi if own else a_hi, m_lo if own else a_lo,
                               b + 1, begin=b, end=b == KB - 1)
                if b == KB - 1:
                    last.then_inc(tile_done, 1)

            pe.wait_ge(parts["mem"][1], KB)
            for n in range(IDX_STEPS):
                i, h = TOPK // P + n // IDX_H, n % IDX_H
                q = slice(i * P - TOPK, i * P - TOPK + P)
                if n >= 2:
                    pe.wait_ge(rel_ready, n - 1)
                for c in range(0, P * (i + 1), 512):
                    e = min(P * (i + 1), c + 512)
                    last = pe.matmul(side[:, n % 2, c:e], qi_stack[0:STACK, h, q], ki_stack[0:STACK, c:e], start=True, stop=True)
                last.then_inc(idx_ready, 1)
                memory_block(T_MEM + n // KB, n % KB)
            pe.wait_ge(rel_ready, IDX_STEPS)

            def probs_turn(n, n0, blocks):
                pe.wait_ge(lg_p, n0 + n + 1)
                if n >= 2:
                    pe.wait_ge(lg_oc, n0 + n - 1)
                for b in range(blocks):
                    last = pe.transpose(dense[:, n % 2, b * P:b * P + P], T[:, n % 2, b * P:b * P + P], ident[:, :])
                last.then_inc(lg_t, 1)

            def memory(u_kv, qc, n0):
                emptied(pe, u_kv + 2)
                emptied(pe, u_kv + 3)
                for mt in range(2):
                    for j in range(2):
                        last = pe.transpose(side[:, 0, mt * MEM + j * P:mt * MEM + j * P + P],
                                            vm_t[:, j, mt * P:mt * P + P], ident[:, :])
                last.then_inc(mturned, 1)
                meet(pe, "pe", met_n)
                for n in range(TB + 2):
                    if n < TB:
                        if n >= 2:
                            pe.wait_ge(lg_exp, n0 + n - 1)
                        for h in range(4):
                            o = 512 * (h % 2) + MEM * (h // 2)
                            r = slice(HD * (h % 2), HD * (h % 2) + HD)
                            last = pe.matmul(side[:, n % 2, o:o + MEM], qc[r, h // 2, n * P:n * P + P], km_f[r, h // 2, :],
                                             start=h < 2, stop=True, skip_group_check=True)
                        last.then_inc(lg_ready, 1)
                    if 1 <= n <= TB:
                        probs_turn(n - 1, n0, KB)
                    if n >= 2:
                        b = n - 2
                        pe.wait_ge(lg_tc, n0 + b + 1)
                        for h in range(4):
                            q = 2 * (h % 2) + h // 2
                            for mt in range(2):
                                last = pe.matmul(dense[:, b % 2, h * P:h * P + P], vm_f[:, mt, h // 2 * P:h // 2 * P + P],
                                                 T[:, 2 + b % 2, (2 * q + mt) * P:(2 * q + mt) * P + P],
                                                 start=h == 0 and mt == 0, stop=mt == 1, skip_group_check=True)
                        last.then_inc(lg_o, 1)
                meet(pe, "pe", met_n)

            memory(T_MEM, qc_f, 0)

            for t in range(T_CONV, T_GATE):
                tile(t, t)

            pe.wait_ge(parts["yc"][1], 3)
            pe.wait_ge(parts["ym"][1], 2)

            def gate_blocks(i):
                for j in range(2):
                    for c in range(4):
                        t = T_GATE + 4 * j + c
                        if c < 3:
                            tile(t, t, i=i, per=(8, 8))
                        else:
                            tile(t, t, hi=yc_hi, lo=yc_lo, blocks=3, i=i, per=(8, 8), done=first_done)
                            if not isinstance(i, int):
                                pe.wait_ge(branch_free[j], i)
                            product(t % 2, halves(side, j), ym_hi, ym_lo, 2, at_block=3).then_inc(tile_done, 1)

            repeat(pe, 4, gate_blocks)
            meet(pe, "pe", met_n)

            for n in range(DSA_STEPS + 2):
                if n < DSA_STEPS:
                    i, h = divmod(n, ATT_H)
                    r = slice(HD * (h // 3), HD * (h // 3) + HD)
                    if n >= 2:
                        pe.wait_ge(lg_max, TB + n - 1)
                    for c in range(0, P * (i + 1), 512):
                        e = min(P * (i + 1), c + 512)
                        last = pe.matmul(side[:, n % 2, c:e], q_f[r, h % 3, i * P:i * P + P], k_f[r, c:e], start=True,
                                         stop=True)
                    last.then_inc(lg_ready, 1)
                if 1 <= n <= DSA_STEPS:
                    probs_turn(n - 1, TB, (n - 1) // ATT_H + 1)
                if n >= 2:
                    b = n - 2
                    i = b // ATT_H
                    pe.wait_ge(lg_tc, TB + b + 1)
                    for kb in range(i + 1):
                        last = pe.matmul(dense[:, b % 2, 0:P], v_f[:, kb, :], T[:, 2 + b % 2, kb * P:kb * P + P],
                                         start=kb == 0, stop=kb == i)
                    last.then_inc(lg_o, 1)
            meet(pe, "pe", met_n)

            for n in range(KB // 2):
                t = T_ATT + n
                tile(t, t, hi=ya_hi, lo=ya_lo, blocks=3, ready=parts["ya"][1] if n == 0 else None, done=first_done)
                if n >= 2:
                    pe.wait_ge(att_free[n % 2], n // 2)
                product(t % 2, halves(side, n % 2), ya_hi, ya_lo, 3, at_block=3).then_inc(tile_done, 1)
            for n in range(KB):
                if n == 0:
                    two_tiles(T_WO, T_WO, parts["merged"][1])
                elif n >= 2:
                    tile(T_WO + n, T_WO + n)
                    squares_part(n - 2)
            rms(TB, begin=KB - 2)

            def feed(t0, u0, ups, hidden, blocks, per, ready, n0):
                def group(i, behind=None):
                    for c in range(ups):
                        if isinstance(i, int) and i == 0 and ready is not None and c < 2:
                            if c == 0:
                                two_tiles(t0, u0, ready)
                        else:
                            tile(t0 + c, u0 + c, i=i, per=per)
                    t = t0 + ups
                    pe.wait_ge(weights_split, i * per[0] + (t + 1))
                    for m in range(2):
                        u = u0 + ups + m
                        pe.wait_ge(sums_free[u % 2], i * (per[1] // 2) + u // 2)
                        if m == 0:
                            pe.wait_ge(hidden, i * blocks + (n0 + blocks - 1))
                        product(t % 2, halves(dense, u % 2), b_hi, b_lo, blocks - 1, m * blocks, end=False)
                    pe.wait_ge(hidden, i * blocks + (n0 + blocks))
                    for m in range(2):
                        product(t % 2, halves(dense, (u0 + ups + m) % 2), b_hi, b_lo, blocks, m * blocks, begin=blocks - 1
                                ).then_inc(tile_done if m else first_done, 1)
                    for c in range(1, KB // 2):
                        for m in range(2):
                            tile(t + c, u0 + ups + 2 * c + m, hi=b_hi, lo=b_lo, blocks=blocks, at_block=m * blocks, i=i,
                                 per=per, done=tile_done if m else first_done)
                            if behind is not None:
                                behind(2 * c + m - 2)
                return group

            h2 = parts["h2"][1]
            hidden = parts["hidden"][1]
            repeat(pe, FULL, feed(T_FF, T_FF, 2 * FG, hidden, FG, (FF_TILES, FF_USES), h2, 0))
            for n in range(4):
                tile(T_KV2 + n, U_KV2 + n, hi=m_hi, lo=m_lo, width=MEM, ready=parts["mem2"][1] if n == 0 else None)
            feed(T_REST, U_REST, 2 * REST, hidden, REST, (0, 0), None, FULL * FG)(0, behind=squares_part)
            rms(TB, begin=KB - 2)

            two_tiles(T_MEM2, U_MEM2, parts["x2"][1])
            emptied(pe, U_MEM2)
            emptied(pe, U_MEM2 + 1)
            memory(U_KV2, qc2_f, TB + DSA_STEPS)

            def project(i, p, c, begin, end, sums=dense[:, 0, :]):
                t = T_SB + 3 * p + c
                if begin == 0:
                    if c == 0 and p:
                        pe.wait_ge(qk_split, i * 4 + 2 * p)
                    if c == 1 and p:
                        pe.wait_ge(v_split, i * 2 + (p + 1))
                    if c == 2 and p:
                        pe.wait_ge(qk_split, i * 4 + (2 * p + 1))
                    pe.wait_ge(weights_split, i * 6 + (t + 1))
                last = product(t % 2, [sums[:, 0:512], sums[:, 512:S]], a_hi, a_lo, end, begin=begin, end=end == KB)
                if end == KB:
                    last.then_inc(tile_done, 1)

            def turn_values(i, p, sums=dense[:, 0, :]):
                pe.wait_ge(v_copied, i * 2 + (p + 1))
                for b in range(TB):
                    last = pe.transpose(sums[:, b * P:b * P + P], sv_t[:, b * P:b * P + P], ident[:, :])
                last.then_inc(v_turned, 1)

            def stick_pairs(i, end=False):
                for n in range(BODY + PV_LAG):
                    if n < BODY:
                        pr, (hh, th, a, c0) = n // NS, PLAN[n % NS]
                        r = slice(HD * hh, HD * hh + HD)
                        kb, tk = slice(a * P, a * P + P), slice(512 * th + c0, 512 * th + 512)
                        if n % NS == 0:
                            pe.wait_ge(qk_split, i * 4 + (2 * pr + 2))
                        if n >= 2:
                            pe.wait_ge(z_copied, i * BODY + (n - 1))
                        z = z_bank(n, c0)
                        if a >= 4 * th:
                            pe.matmul(z[:, 0:P], ident_r, strict_r, start=True, stop=False, skip_group_check=True)
                        pe.matmul(z, sk_hi[r, pr, kb], sq_hi[r, pr, tk], start=a < 4 * th, stop=False, skip_group_check=True)
                        pe.matmul(z, sk_hi[r, pr, kb], sq_lo[r, pr, tk], start=False, stop=False, skip_group_check=True)
                        pe.matmul(z, sk_lo[r, pr, kb], sq_hi[r, pr, tk], start=False, stop=True, skip_group_check=True
                                  ).then_inc(z_ready, 1)
                    if SUM_LAG < n <= BODY + SUM_LAG and PLAN[(n - SUM_LAG - 1) % NS][2] > 0:
                        m = n - SUM_LAG - 1
                        hh, th, a, c0 = PLAN[m % NS]
                        pe.wait_ge(arg_ready, i * BODY + (m + 1))
                        pe.matmul(sum_bank(hh, c0), earlier_r, sp_hi[:, m % 3, c0:512], start=False, stop=False,
                                  skip_group_check=True)
                        pe.matmul(sum_bank(hh, c0), earlier_r, sp_lo[:, m % 3, c0:512], start=False, stop=True,
                                  skip_group_check=True).then_inc(carried, 1)
                    if SUM_LAG <= n < BODY + SUM_LAG:
                        m = n - SUM_LAG
                        hh, th, a, c0 = PLAN[m % NS]
                        pe.wait_ge(sp_split, i * BODY + (m + 1))
                        pe.matmul(sum_bank(hh, c0), later_r, sp_hi[:, m % 3, c0:512], start=a == 4 * th + 3, stop=False,
                                  skip_group_check=True)
                        pe.matmul(sum_bank(hh, c0), later_r, sp_lo[:, m % 3, c0:512], start=False, stop=True,
                                  skip_group_check=True).then_inc(later_ready, 1)
                    if n >= PV_LAG:
                        m = n - PV_LAG
                        pr, (hh, th, a, c0) = m // NS, PLAN[m % NS]
                        first = a == 4 * th + 3
                        if first and m >= 2:
                            pe.wait_ge(y_copied, i * 8 + 2 * (2 * pr + th))
                        pe.wait_ge(w_split, i * BODY + (m + 1))
                        w_hi_m, w_lo_m = stick_hi[:, m % 2, c0:512], stick_lo[:, m % 2, c0:512]
                        o = out_bank(hh, c0)
                        pe.matmul(o, sv_hi[:, pr, a, :], w_hi_m, start=first, stop=False, skip_group_check=True)
                        pe.matmul(o, sv_hi[:, pr, a, :], w_lo_m, start=False, stop=False, skip_group_check=True)
                        pe.matmul(o, sv_lo[:, pr, a, :], w_hi_m, start=False, stop=a == 0, skip_group_check=True
                                  ).then_inc(pv_done, 1)
                    if n < BODY and not (end and n >= NS):
                        if n % NS in BETWEEN:
                            project(i, n // NS + 1, *BETWEEN[n % NS])
                        elif n % NS == TURN_V:
                            turn_values(i, n // NS + 1)
                pe.wait_ge(y_copied, i * 8 + 8)

            project(0, 0, 0, 0, KB)
            project(0, 0, 1, 0, KB, sums=dense[:, 1, :])
            turn_values(0, 0, sums=side[:, 0, :])
            project(0, 0, 2, 0, KB)
            pe.wait_ge(v_split, 1)
            with pe.Fori(0, SB_H // 4 - 1) as i:
                stick_pairs(i)
            stick_pairs(SB_H // 4 - 1, end=True)
            meet(pe, "pe", met_n)

            for n in range(KB):
                if n == 0:
                    two_tiles(T_OUT2, U_OUT2, parts["y2"][1])
                elif n >= 2:
                    tile(T_OUT2 + n, U_OUT2 + n)
                    residual_mean(n - 2, U_OUT2)
            for k in (KB - 2, KB - 1):
                residual_mean(k, U_OUT2)
            layer_norm()
            group = feed(T_FF2, U_FF2, FG, parts["hidden2"][1], FG, (FF2_TILES, FF2_USES), parts["x3"][1], 0)
            repeat(pe, FF2_GROUPS - 1, group)
            u_last = U_FF2 + (FF2_GROUPS - 1) * FF2_USES + FG
            group(FF2_GROUPS - 1, behind=lambda k: residual_mean(k, u_last))
            for k in (KB - 2, KB - 1):
                residual_mean(k, u_last)
            layer_norm()
            meet(pe, "pe", met_n)

        @block.scalar
        def _(act):
            met_n, norm_n = [0], {"sq": 0, "used": 0, "mean": 0, "scaled": 0}

            def rms_squares(src, width, ready):
                for k in range(KB):
                    ready(k)
                    if k >= 2:
                        act.wait_ge(squares_used, norm_n["used"] + k - 1)
                    act.activation(T[:, k % 2, 0:width], src(k), ACT.Square).then_inc(squares, 1)
                norm_n["used"] += KB - 1
                norm_n["mean"] += 1

            def root(blocks, eps):
                act.wait_ge(mean_ready, norm_n["mean"])
                act.activation(std[:, 0:blocks], side[:, 0, 0:blocks], ACT.Sqrt, bias=eps).then_inc(std_ready, 1)

            def round_scaled(dst, src, which, shift=None):
                for k in range(KB):
                    act.wait_ge(scaled, norm_n["scaled"] + k + 1)
                    if shift is not None:
                        act.activation(x_res[:, k, :], src(k), ACT.Identity, bias=par(shift, k)).then_inc(shifted, 1)
                        act.drain()
                        if dst is not None:
                            act.activation(dst[:, k, :], x_res[:, k, :], ACT.Copy).then_inc(parts[which][0], 1)
                    else:
                        act.activation(dst[:, k, :], src(k), ACT.Copy).then_inc(parts[which][0], 1)
                norm_n["scaled"] += KB

            act.wait_ge(consts_in, CONSTS)
            rms_squares(lambda k: m_in[:, k, :], MEM, lambda k: act.wait_ge(mem_loaded, 16))
            root(MEM // P, EPS_RMS)
            round_scaled(m_hi, lambda k: m_in[:, k, :], "mem")
            rms_squares(lambda k: x_in[:, k, :], S, lambda k: act.wait_ge(x_loaded[k // 2], 16))
            root(TB, EPS_RMS)
            round_scaled(a_hi, lambda k: x_in[:, k, :], "h")

            for t in range(T_KI, T_MEM):
                act.wait_ge(tile_done, t + 1)
                if t >= 2:
                    act.wait_ge(roped, t - 1)
                act.activation(T[:, t % 2, :], dense[:, t % 2, :], ACT.Copy).then_inc(sums_free[t % 2], 1)
            meet(act, "act", met_n)

            def memory_copy(t, u, n, qc):
                act.wait_ge(tile_done, t + 1)
                dst, width = (km_f[:, n, :], MEM) if n < 2 else (vm_t[:, n - 2, :], MEM) if n < 4 else (qc[:, n - 4, :], S)
                act.activation(dst, dense[:, u % 2, 0:width], ACT.Copy).then_inc(sums_free[u % 2], 1)

            act.activation(ki_hi[:, :], ki_f[:, :], ACT.Copy).then_inc(idx_round, 1)
            for t in range(2):
                act.activation(qi_hi[:, t, :], qi_f[:, t, TOPK:S], ACT.Copy).then_inc(idx_round, 1)
            for n in range(IDX_H + 1):
                act.wait_ge(stacked, n + 1)
                act.activation(ki_stack[0:STACK, :] if n == 0 else qi_stack[0:STACK, n - 1, :],
                               side[0:STACK, n % 2, 0:S if n == 0 else IDX_S], ACT.Copy).then_inc(stack_copied, 1)
            for n in range(IDX_STEPS):
                i = TOPK // P + n // IDX_H
                act.wait_ge(idx_ready, n + 1)
                if n >= 2:
                    act.wait_ge(rel_used, n - 1)
                act.activation(T[:, n % 2, 0:P * (i + 1)], side[:, n % 2, 0:P * (i + 1)], ACT.Relu).then_inc(rel_ready, 1)
                if n and n % KB == 0:
                    memory_copy(T_MEM + n // KB - 1, T_MEM + n // KB - 1, n // KB - 1, qc_f)
            memory_copy(T_MEM + 5, T_MEM + 5, 5, qc_f)

            def memory(yf, y0, n0):
                meet(act, "act", met_n)
                for n in range(TB + 2):
                    if n < TB:
                        act.wait_ge(lg_max, n0 + n + 1)
                        if n >= 2:
                            act.wait_ge(lg_t, n0 + n - 1)
                        for q in range(4):
                            e = 4 * (n % 2) + q
                            last = act.activation(T[:, n % 2, q * MEM:q * MEM + MEM], side[:, n % 2, q * MEM:q * MEM + MEM],
                                                  ACT.Exp, bias=neg_max[:, e:e + 1], scale=SCALE,
                                                  accum_out=row_sum[:, e:e + 1])
                        last.then_inc(lg_exp, 1)
                    if 1 <= n <= TB:
                        copy_turned(n - 1, n0, S)
                    if n >= 2:
                        b = n - 2
                        act.wait_ge(lg_o, n0 + b + 1)
                        heads = dense[:, b % 2, 0:512].rearrange("p (j e q) -> p j e q", j=2, e=2)
                        for e in range(2):
                            r = slice(HD * e, HD * e + HD)
                            last = act.activation(yf[r, y0:y0 + 2, b * P:b * P + P], heads[r, :, e, :], ACT.Copy)
                        last.then_inc(lg_oc, 1)

            def copy_turned(n, n0, width):
                act.wait_ge(lg_t, n0 + n + 1)
                if n >= 2:
                    act.wait_ge(lg_o, n0 + n - 1)
                act.activation(T[:, 2 + n % 2, 0:width], dense[:, n % 2, 0:width], ACT.Copy).then_inc(lg_tc, 1)

            memory(ym_f, 0, 0)
            act.drain()
            for k in range(2):
                act.activation(ym_hi[:, k, :], ym_f[:, k, :], ACT.Copy).then_inc(parts["ym"][0], 1)
            meet(act, "act", met_n)

            for j in range(3):
                t = T_CONV + 3 * j
                act.wait_ge(tile_done, t + 1)
                if j:
                    act.wait_ge(conv_used, j)
                act.activation(T[:, 0, :], dense[:, t % 2, :], ACT.Copy).then_inc(sums_free[t % 2], 1)
                act.wait_ge(yc_ready, j + 1)
                act.activation(yc_hi[:, j, :], T[:, 2, :], ACT.Copy).then_inc(parts["yc"][0], 1)

            def gate_blocks(i):
                first = isinstance(i, int)
                for j in range(2):
                    t = T_GATE + 4 * j
                    for c in range(3):
                        b = SMALL["b_gate"] + 3 * j + c
                        act.activation(bias_now[:, :], small[:, b:b + 1] if first else small[:, bass.ds(i * 6 + b, 1)], ACT.Copy)
                        act.drain()
                        act.wait_ge(tile_done, i * 8 + (t + c + 1))
                        dst = T[:, j, :] if c == 0 else gates[:, 2 * j + c - 1, :]
                        if not first and c == 0:
                            act.wait_ge(gate_spilled[j], i * 16)
                        if not first and c == 1:
                            act.wait_ge(part_spilled[j], i * 16)
                        act.activation(dst, dense[:, (t + c) % 2, :], ACT.Sigmoid, bias=bias_now[:, :]
                                       ).then_inc(sums_free[(t + c) % 2], 1)
                        act.drain()
                        if c == 0:
                            act.dma_start(spill_gate[bass.ds(i * 2 + j, 1)].rearrange("a p s -> p (a s)")
                                          if not first else spill_gate[j], T[:, j, :]).then_inc(gate_spilled[j], 16)
                    act.wait_ge(part_ready, i * 2 + (j + 1))
                    act.dma_start(spill_part[bass.ds(i * 2 + j, 1)].rearrange("a p s -> p (a s)")
                                  if not first else spill_part[j], gates[:, 2 * j, :]).then_inc(part_spilled[j], 16)

            repeat(act, 4, gate_blocks)
            for j in range(2):
                act.wait_ge(gate_spilled[j], 64)
                act.wait_ge(part_spilled[j], 64)
            meet(act, "act", met_n)

            for n in range(DSA_STEPS + 2):
                if n < DSA_STEPS:
                    w, e = P * (n // ATT_H + 1), n % 8
                    act.wait_ge(lg_max, TB + n + 1)
                    act.activation(T[:, n % 2, 0:w], T[:, n % 2, 0:w], ACT.Exp, bias=neg_max[:, e:e + 1], scale=SCALE,
                                   accum_out=row_sum[:, e:e + 1]).then_inc(lg_exp, 1)
                if 1 <= n <= DSA_STEPS:
                    copy_turned(n - 1, TB, P * ((n - 1) // ATT_H + 1))
                if n >= 2:
                    i, h = divmod(n - 2, ATT_H)
                    r = slice(HD * (h // 3), HD * (h // 3) + HD)
                    act.wait_ge(lg_o, TB + n - 1)
                    act.activation(ya_f[r, h % 3, i * P:i * P + P], dense[r, n % 2, 0:P], ACT.Copy).then_inc(lg_oc, 1)
            meet(act, "act", met_n)

            act.dma_start(x_res[:, :, :], io["x_t"]).then_inc(x_back, 16)

            def fetch(j):
                act.dma_start(back[:, 2 * (j % 2), :], spill_gate[j]).then_inc(fetched[j % 2], 16)
                act.dma_start(back[:, 2 * (j % 2) + 1, :], spill_part[j]).then_inc(fetched[j % 2], 16)

            fetch(0)
            fetch(1)
            act.dma_start(m_in[:, :, :], io["mem2_t"]).then_inc(mem2_loaded, 16)
            for k in range(3):
                act.activation(ya_hi[:, k, :], ya_f[:, k, :], ACT.Copy).then_inc(parts["ya"][0], 1)
            for j in range(KB):
                act.wait_ge(merged_sum, j + 1)
                act.activation(a_hi[:, j, :], T[:, j % 2, :], ACT.Copy).then_inc(parts["merged"][0], 1)
                if j + 2 < KB:
                    fetch(j + 2)

            rms_squares(lambda k: x_res[:, k, :], S, lambda k: emptied(act, T_WO + k))
            root(TB, EPS_RMS)
            round_scaled(a_hi, lambda k: T[:, (0, 1, 3)[k % 3], :], "h2")
            act.wait_ge(mem2_loaded, 16)
            act.activation(m_hi[:, :, :], m_in[:, :, :], ACT.Copy).then_inc(parts["mem2"][0], 1)

            def gated(i, t0, n_f, f0, per):
                cols = SMALL["taps_ff"] + 6 * f0
                act.drain()
                act.activation(taps_act[:, 0:6 * n_f], small[:, bass.ds(i * (6 * FG) + cols, 6 * n_f)]
                               if not isinstance(i, int) else small[:, cols:cols + 6 * n_f], ACT.Copy)
                act.drain()
                for f in range(n_f):
                    for c in range(2):
                        t = t0 + 2 * f + c
                        u = gu[0] + 2 * f + c
                        act.wait_ge(tile_done, i * per + (t + 1))
                        slot = 2 * (f % 2) + c
                        if f >= 2 or not isinstance(i, int) or f0:
                            act.wait_ge(parts["hidden"][1] if c == 0 else product_ready, i * FG + (f0 + f - 1))
                        act.activation(T[:, slot, :], dense[:, u % 2, :], ACT.Copy,
                                       scale=taps_act[:, 6 * f + 3 * c + 2:6 * f + 3 * c + 3]).then_inc(tap_ready, 1)
                    act.wait_ge(taps_done, i * (2 * FG) + (2 * (f0 + f) + 1))
                    act.activation(T[:, 2 * (f % 2), :], T[:, 2 * (f % 2), :], ACT.Silu).then_inc(acted, 1)
                    act.wait_ge(product_ready, i * FG + (f0 + f + 1))
                    act.activation(b_hi[:, f, :], T[:, 2 * (f % 2), :], ACT.Copy).then_inc(parts["hidden"][0], 1)

            gu = [T_FF]
            repeat(act, FULL, lambda i: gated(i, T_FF, FG, 0, FF_TILES))
            for n in range(4):
                memory_copy(T_KV2 + n, U_KV2 + n, n, None)
            gu[0] = U_REST
            gated(0, T_REST, REST, FULL * FG, 0)
            rms_squares(lambda k: x_res[:, k, :], S, lambda k: emptied(act, U_REST + 2 * REST + k))
            root(TB, EPS_RMS)
            round_scaled(a_hi, lambda k: x_res[:, k, :], "x2")

            for n in range(2):
                memory_copy(T_MEM2 + n, U_MEM2 + n, 4 + n, qc2_f)
            act.wait_ge(parts["x2"][1], KB)
            act.dma_start(spill_x, x_res[:, :, :]).then_inc(x_spilled, 16)
            memory(y2_f, 6, TB + DSA_STEPS)
            act.wait_ge(x_spilled, 16)
            meet(act, "act", met_n)

            def take(i, p, c, sums=dense[:, 0, :]):
                act.wait_ge(tile_done, i * 6 + (T_SB + 3 * p + c + 1))
                if c == 0:
                    act.activation(sv_t[:, :], sums, ACT.Copy).then_inc(v_copied, 1)
                elif c == 1:
                    act.activation(sk_hi[:, p % 2, :], sums, ACT.Copy).then_inc(qk_rounded, 1)
                else:
                    act.activation(sq_hi[:, p % 2, :], sums, ACT.Copy, scale=SCALE).then_inc(qk_rounded, 1)

            def stick_pairs(i, end=False):
                for n in range(BODY + SUM_LAG):
                    if 2 <= n < BODY + 2:
                        m = n - 2
                        if m >= 3:
                            if PLAN[(m - 3) % NS][2] > 0:
                                act.wait_ge(carried, i * CARRIES[-1] + CARRIES[m - 3])
                            else:
                                act.wait_ge(later_ready, i * BODY + (m - 2))
                        act.wait_ge(sp_ready, i * BODY + (m + 1))
                        act.activation(sp_hi[:, m % 3, PLAN[m % NS][3]:512], sp_strip(m), ACT.Copy).then_inc(sp_round, 1)
                    if n < BODY:
                        act.wait_ge(z_ready, i * BODY + (n + 1))
                        act.activation(sp_strip(n), z_bank(n, PLAN[n % NS][3]), ACT.Exp).then_inc(e_ready, 1)
                    if 1 <= n <= BODY:
                        m = n - 1
                        act.wait_ge(e_clip, i * BODY + (m + 1))
                        act.activation(sp_strip(m), sp_strip(m), ACT.Ln, bias=1.0).then_inc(ln_ready, 1)
                    if n < BODY:
                        if n >= 6:
                            act.wait_ge(w_split, i * BODY + (n - 5))
                        act.activation(z_strip(n), z_bank(n, PLAN[n % NS][3]), ACT.Copy).then_inc(z_copied, 1)
                    if n >= SUM_LAG:
                        m = n - SUM_LAG
                        act.wait_ge(arg_ready, i * BODY + (m + 1))
                        act.activation(z_strip(m), z_strip(m), ACT.Exp).then_inc(w_ready, 1)
                    if n < BODY and not (end and n >= NS) and n % NS in (COPY_V, COPY_K, COPY_Q):
                        take(i, n // NS + 1, (COPY_V, COPY_K, COPY_Q).index(n % NS))

            for c in range(3):
                take(0, 0, c, sums=dense[:, c % 2, :])
            act.preload_act_table_set("natural_log_exp_and_others")
            with act.Fori(0, SB_H // 4 - 1) as i:
                stick_pairs(i)
            stick_pairs(SB_H // 4 - 1, end=True)
            meet(act, "act", met_n)
            act.dma_start(x_res[:, 0:2, :], spill_x[:, 0:2, :]).then_inc(x_returned[0], 16)
            act.dma_start(x_res[:, 2:KB, :], spill_x[:, 2:KB, :]).then_inc(x_returned[1], 16)

            for k in range(KB):
                act.activation(a_hi[:, k, :], y2_f[:, k, :], ACT.Copy).then_inc(parts["y2"][0], 1)

            def layer_norm(dst, which, shift):
                norm_n["mean"] += 1
                act.wait_ge(mean_ready, norm_n["mean"])
                for k in range(KB):
                    act.wait_ge(centred, cen[0] + k + 1)
                    if k >= 2:
                        act.wait_ge(squares_used, norm_n["used"] + k - 1)
                    act.activation(T[:, k % 2, :], x_res[:, k, :], ACT.Square).then_inc(squares, 1)
                cen[0] += KB
                norm_n["used"] += KB - 1
                norm_n["mean"] += 1
                root(TB, EPS_LN)
                round_scaled(dst, lambda k: T[:, (0, 1, 3)[k % 3], :], which, shift)

            cen = [0]
            layer_norm(a_hi, "x3", "ln1_b")

            def squared_relu(i):
                for f in range(FG):
                    act.wait_ge(squared, i * FG + (f + 1))
                    act.activation(b_hi[:, f, :], T[:, f, :], ACT.Copy).then_inc(parts["hidden2"][0], 1)

            repeat(act, FF2_GROUPS, squared_relu)
            layer_norm(None, None, "ln2_b")
            act.drain()
            act.dma_start(out, x_res[:, :, :]).then_inc(out_stored, 16)
            act.wait_ge(out_stored, 16)
            meet(act, "act", met_n)

        @block.vector
        def _(dve):
            met_n, norm_n = [0], {"mean": 0, "std": 0, "spread": 0, "parts": 0, "shift": 0}

            def diagonals(values, blocks):
                for b in range(blocks):
                    last = dve.tensor_scalar(T[:, 2, b * P:b * P + P], ident[:, :], values[:, b:b + 1], None, ALU.mult)
                last.then_inc(diag_ready, 1)
                norm_n["spread"] += 1
                dve.wait_ge(spread_ready, norm_n["spread"])

            def inverse_std(blocks):
                norm_n["std"] += 1
                dve.wait_ge(std_ready, norm_n["std"])
                dve.reciprocal(rstd[:, 0:blocks], std[:, 0:blocks])
                dve.drain()
                diagonals(rstd, blocks)

            def low(dst, k, src, which, n):
                dve.wait_ge(parts[which][0], n)
                dve.tensor_tensor(dst[1], src, dst[0].bitcast(F32), ALU.subtract).then_inc(parts[which][1], 1)

            def scale_all(src, dst, gain, which, hi, lo, width, ring=0, lag=1):
                for k in range(KB + lag):
                    if k < KB:
                        if ring and k >= ring:
                            dve.wait_ge(parts[which][1], k - ring + 1)
                        dve.scalar_tensor_tensor(dst(k), src(k), par(gain, k), side[:, 1, 0:width], ALU.mult, ALU.mult
                                                 ).then_inc(scaled, 1)
                    if k >= lag and which is not None:
                        m = k - lag
                        low((hi[:, m, :], lo[:, m, :]), m, dst(m), which, m + 1)

            dve.wait_ge(consts_in, CONSTS)
            dve.wait_ge(mem_loaded, 16)
            inverse_std(MEM // P)
            scale_all(lambda k: m_in[:, k, :], lambda k: m_in[:, k, :], "g_mem", "mem", m_hi, m_lo, MEM)
            for c in range(4):
                dve.wait_ge(x_loaded[c], 16)
            inverse_std(TB)
            scale_all(lambda k: x_in[:, k, :], lambda k: x_in[:, k, :], "g_mix", "h", a_hi, a_lo, S)
            dve.wait_ge(tables_in, 32)

            def rotate(t, tab, dst, n_turned, v):
                dve.wait_ge(turned, n_turned)
                dve.tensor_tensor(T[:, 2 + t % 2, :], side[:, v % 2, :], rope_tab[:, tab + 1, :], ALU.mult
                                  ).then_inc(turn_free[v % 2], 1)
                dve.tensor_tensor(T[:, t % 2, :], T[:, t % 2, :], rope_tab[:, tab, :], ALU.mult)
                dve.drain()
                dve.tensor_tensor(dst, T[:, t % 2, :], T[:, 2 + t % 2, :], ALU.add).then_inc(roped, 1)

            dve.wait_ge(turned, 1)
            dve.tensor_tensor(T[:, 3, :], side[:, 0, :], rope_tab[:, 0, :], ALU.mult).then_inc(turn_free[0], 1)
            dve.wait_ge(turned, 2)
            dve.tensor_tensor(T[:, 2, :], side[:, 1, :], rope_tab[:, 1, :], ALU.mult).then_inc(turn_free[1], 1)
            dve.drain()
            dve.tensor_tensor(ki_f[:, :], T[:, 2, :], T[:, 3, :], ALU.add)
            dve.wait_ge(turned, 3)
            dve.tensor_copy(tiny[:, 160:160 + TB * IDX_H], side[:, 0, 0:TB * IDX_H]).then_inc(turn_free[0], 1)
            dve.drain().then_inc(roped, 1)
            for t in range(1, T_V):
                dst = qi_f[:, t - 1, :] if t < T_K else k_f[:, :] if t == T_K else q_f[:, t - T_Q, :]
                rotate(t, 0 if t < T_K else 2, dst, t + 3, t + 2)
            dve.tensor_copy(stack_mats[:, :, :], stack_in[:, :].rearrange("p (m c) -> p m c", m=4))
            dve.wait_ge(turned, 10)
            dve.tensor_copy(v_f[:, :, :], side[:, 1, :].rearrange("p (b d) -> p b d", d=P)).then_inc(turn_free[1], 1)
            meet(dve, "dve", met_n)

            dve.wait_ge(idx_round, 1)
            dve.tensor_tensor(ki_lo[:, :], ki_f[:, :], ki_hi[:, :].bitcast(F32), ALU.subtract).then_inc(idx_split, 1)
            for t in range(2):
                dve.wait_ge(idx_round, t + 2)
                dve.tensor_tensor(qi_lo[:, t, :], qi_f[:, t, TOPK:S], qi_hi[:, t, :].bitcast(F32), ALU.subtract
                                  ).then_inc(idx_split, 1)
            dve.memset(score[:, 0:score_at(2)], 0.0)
            for n in range(IDX_STEPS):
                i, h = TOPK // P + n // IDX_H, n % IDX_H
                w = P * (i + 1)
                sc = score[:, score_at(i):score_at(i) + w]
                dve.wait_ge(rel_ready, n + 1)
                if h == 0:
                    dve.tensor_scalar(sc, T[:, n % 2, 0:w], wi_f[:, i, h:h + 1], None, ALU.mult).then_inc(rel_used, 1)
                else:
                    dve.drain()
                    dve.scalar_tensor_tensor(sc, T[:, n % 2, 0:w], wi_f[:, i, h:h + 1], sc, ALU.mult, ALU.add
                                             ).then_inc(rel_used, 1)
            dve.drain()
            for i in range(TB):
                e = score_at(i + 1)
                dve.tensor_tensor(score[:, e - P:e], score[:, e - P:e], mats["causal_q"][:, :], ALU.add)
            dve.drain()

            def topk_round():
                for i in range(TOPK // P, TB):
                    dve.max(best[:, i - TOPK // P, :], score[:, score_at(i):score_at(i + 1)])
                dve.drain()
                for i in range(TOPK // P, TB):
                    sc = score[:, score_at(i):score_at(i + 1)]
                    dve.match_replace(sc, best[:, i - TOPK // P, :], sc, TAKEN)
                dve.drain()

            def memory(n0, layer):
                dve.wait_ge(mturned, layer + 1)
                dve.tensor_copy(vm_f[:, :, :], side[:, 0, 0:512].rearrange("p (m d) -> p m d", m=2))
                meet(dve, "dve", met_n)
                for n in range(TB):
                    e = 4 * (n % 2)
                    dve.wait_ge(lg_ready, n0 + n + 1)
                    dve.tensor_reduce(row_max[:, e:e + 4], side[:, n % 2, :].rearrange("p (q m) -> p q m", q=4), AX.X,
                                      ALU.max)
                    dve.drain()
                    dve.tensor_scalar(neg_max[:, e:e + 4], row_max[:, e:e + 4], -SCALE, None, ALU.mult
                                      ).then_inc(lg_max, 1)
                    dve.wait_ge(lg_exp, n0 + n + 1)
                    dve.reciprocal(inv_sum[:, e:e + 4], row_sum[:, e:e + 4])
                    dve.drain()
                    for q in range(4):
                        pq = T[:, n % 2, q * MEM:q * MEM + MEM]
                        last = dve.tensor_scalar(pq, pq, inv_sum[:, e + q:e + q + 1], None, ALU.mult)
                    last.then_inc(lg_p, 1)

            memory(0, 0)
            for k in range(2):
                low((ym_hi[:, k, :], ym_lo[:, k, :]), k, ym_f[:, k, :], "ym", k + 1)
            meet(dve, "dve", met_n)

            for j in range(3):
                t = T_CONV + 3 * j
                with dve.Fori(0, 2):
                    topk_round()
                emptied(dve, t)
                dve.wait_ge(tile_done, t + 2)
                dve.tensor_tensor(T[:, 1, :], dense[:, (t + 1) % 2, :], T[:, 0, :], ALU.mult
                                  ).then_inc(sums_free[(t + 1) % 2], 1)
                dve.drain().then_inc(conv_used, 1)
                dve.tensor_scalar(T[:, 2, :], T[:, 1, :], par("taps_short", 3 * j + 2), None, ALU.mult)
                for d in (1, 2):
                    dve.drain()
                    dve.scalar_tensor_tensor(T[:, 2, d:S], T[:, 1, 0:S - d], par("taps_short", 3 * j + 2 - d), T[:, 2, d:S],
                                             ALU.mult, ALU.add)
                dve.drain()
                dve.wait_ge(tile_done, t + 3)
                dve.tensor_tensor(T[:, 2, :], dense[:, (t + 2) % 2, :], T[:, 2, :], ALU.mult
                                  ).then_inc(sums_free[(t + 2) % 2], 1)
                dve.drain().then_inc(yc_ready, 1)
                low((yc_hi[:, j, :], yc_lo[:, j, :]), j, T[:, 2, :], "yc", j + 1)

            def gate_blocks(i):
                for j in range(2):
                    t = T_GATE + 4 * j
                    for _ in range(3):
                        topk_round()
                    g1, g2 = gates[:, 2 * j, :], gates[:, 2 * j + 1, :]
                    dve.wait_ge(sums_free[(t + 2) % 2], i * 4 + ((t + 2) // 2 + 1))
                    dve.wait_ge(sums_free[(t + 1) % 2], i * 4 + ((t + 1) // 2 + 1))
                    dve.wait_ge(first_done, i * 2 + (j + 1))
                    dve.tensor_tensor(g1, dense[:, (t + 3) % 2, :], g1, ALU.mult).then_inc(sums_free[(t + 3) % 2], 1)
                    dve.wait_ge(tile_done, i * 8 + (t + 4))
                    dve.tensor_tensor(g2, side[:, j, :], g2, ALU.mult).then_inc(branch_free[j], 1)
                    dve.drain()
                    dve.tensor_tensor(g1, g1, g2, ALU.add).then_inc(part_ready, 1)

            repeat(dve, 4, gate_blocks)
            with dve.Fori(0, ROUNDS - 30):
                topk_round()
            sc = score[:, score_at(2):score_at(TB)]
            dve.tensor_scalar(sc, sc, TAKEN / 2, NEG, ALU.is_gt, ALU.mult)
            meet(dve, "dve", met_n)

            for n in range(DSA_STEPS):
                i, e = n // ATT_H, n % 8
                w = P * (i + 1)
                dve.wait_ge(lg_ready, TB + n + 1)
                if n >= 2:
                    dve.wait_ge(lg_t, TB + n - 1)
                dve.tensor_tensor_reduce(out=T[:, n % 2, 0:w], in0=side[:, n % 2, 0:w],
                                         in1=score[:, score_at(i):score_at(i) + w], scale=1.0, scalar=TAKEN, op0=ALU.add,
                                         op1=ALU.max, accum_out=row_max[:, e:e + 1])
                dve.drain()
                dve.tensor_scalar(neg_max[:, e:e + 1], row_max[:, e:e + 1], -SCALE, None, ALU.mult).then_inc(lg_max, 1)
                dve.wait_ge(lg_exp, TB + n + 1)
                dve.reciprocal(inv_sum[:, e:e + 1], row_sum[:, e:e + 1])
                dve.drain()
                dve.tensor_scalar(T[:, n % 2, 0:w], T[:, n % 2, 0:w], inv_sum[:, e:e + 1], None, ALU.mult
                                  ).then_inc(lg_p, 1)
            meet(dve, "dve", met_n)

            for k in range(3):
                low((ya_hi[:, k, :], ya_lo[:, k, :]), k, ya_f[:, k, :], "ya", k + 1)
            for j in range(KB):
                t, m = T_ATT + j // 2, j // 2
                src = dense[:, t % 2, :] if j % 2 == 0 else side[:, m % 2, :]
                dve.wait_ge(fetched[j % 2], 32 * (j // 2 + 1))
                if j % 2 == 0:
                    dve.wait_ge(first_done, 8 + m + 1)
                else:
                    dve.wait_ge(tile_done, t + 1)
                dve.tensor_tensor(T[:, j % 2, :], src, back[:, 2 * (j % 2), :], ALU.mult
                                  ).then_inc(sums_free[t % 2] if j % 2 == 0 else att_free[m % 2], 1)
                dve.drain()
                dve.tensor_tensor(T[:, j % 2, :], T[:, j % 2, :], back[:, 2 * (j % 2) + 1, :], ALU.add
                                  ).then_inc(merged_sum, 1)
                low((a_hi[:, j, :], a_lo[:, j, :]), j, T[:, j % 2, :], "merged", j + 1)
            dve.wait_ge(x_back, 16)
            for n in range(KB):
                u = T_WO + n
                dve.wait_ge(tile_done, T_WO + n + 1)
                dve.tensor_tensor(x_res[:, n, :], x_res[:, n, :], dense[:, u % 2, :], ALU.add
                                  ).then_inc(sums_free[u % 2], 1)

            def third(k):
                return T[:, (0, 1, 3)[k % 3], :]

            inverse_std(TB)
            scale_all(lambda k: x_res[:, k, :], third, "g_ffn", "h2", a_hi, a_lo, S, ring=3)
            dve.wait_ge(parts["mem2"][0], 1)
            for k in range(KB):
                dve.tensor_tensor(m_lo[:, k, :], m_in[:, k, :], m_hi[:, k, :].bitcast(F32), ALU.subtract
                                  ).then_inc(parts["mem2"][1], 1)

            def down(i, t0, u0, per, n0):
                for n in range(KB):
                    u = u0 + n
                    if n % 2 == 0:
                        dve.wait_ge(first_done, i * (KB // 2) + (n0 + n // 2 + 1))
                    else:
                        dve.wait_ge(tile_done, i * per + (t0 + n // 2 + 1))
                    dve.tensor_tensor(x_res[:, n, :], x_res[:, n, :], dense[:, u % 2, :], ALU.add
                                      ).then_inc(sums_free[u % 2], 1)

            def gated(i, t0, u0, n_f, f0, per, n0):
                cols = SMALL["taps_ff"] + 6 * f0
                dve.drain()
                dve.tensor_copy(taps_dve[:, 0:6 * n_f], small[:, bass.ds(i * (6 * FG) + cols, 6 * n_f)]
                                if not isinstance(i, int) else small[:, cols:cols + 6 * n_f])
                dve.drain()
                for f in range(n_f):
                    for c in range(2):
                        u, slot = u0 + 2 * f + c, 2 * (f % 2) + c
                        dve.wait_ge(tap_ready, i * (2 * FG) + (2 * (f0 + f) + c + 1))
                        for d in (1, 2):
                            tap = taps_dve[:, 6 * f + 3 * c + 2 - d:6 * f + 3 * c + 3 - d]
                            last = dve.scalar_tensor_tensor(T[:, slot, d:S], dense[:, u % 2, 0:S - d], tap, T[:, slot, d:S],
                                                            ALU.mult, ALU.add)
                            if d == 1:
                                dve.drain()
                        last.then_inc(sums_free[u % 2], 1)
                        dve.drain().then_inc(taps_done, 1)
                    g, v = T[:, 2 * (f % 2), :], T[:, 2 * (f % 2) + 1, :]
                    dve.wait_ge(acted, i * FG + (f0 + f + 1))
                    dve.tensor_tensor(g, g, v, ALU.mult).then_inc(product_ready, 1)
                    dve.wait_ge(parts["hidden"][0], i * FG + (f0 + f + 1))
                    dve.tensor_tensor(b_lo[:, f, :], g, b_hi[:, f, :].bitcast(F32), ALU.subtract
                                      ).then_inc(parts["hidden"][1], 1)
                down(i, t0 + 2 * n_f, u0 + 2 * n_f, per, n0)

            repeat(dve, FULL, lambda i: gated(i, T_FF, T_FF, FG, 0, FF_TILES, 12))
            gated(0, T_REST, U_REST, REST, FULL * FG, 0, 12 + FULL * KB // 2)

            inverse_std(TB)
            scale_all(lambda k: x_res[:, k, :], lambda k: x_res[:, k, :], "g_final", "x2", a_hi, a_lo, S)
            memory(TB + DSA_STEPS, 1)
            meet(dve, "dve", met_n)

            for n, name in enumerate(("ident", "strict_add", "neg_later", "neg_earlier")):
                dve.tensor_copy(stick_mats[:, n, :], mats[name][:, :])
            dve.drain()

            def take_values(i, p, sums=dense[:, 0, :]):
                values = sums.rearrange("p (b d) -> p b d", b=TB)
                hi, lo = sv_hi[:, p % 2, :, :], sv_lo[:, p % 2, :, :]
                dve.wait_ge(v_turned, i * 2 + (p + 1))
                dve.tensor_copy(hi, values).then_inc(v_rounded, 1)
                dve.wait_ge(v_rounded, i * 2 + (p + 1))
                dve.tensor_tensor(lo, values, hi.bitcast(F32), ALU.subtract).then_inc(v_split, 1)

            def take(i, p, c, sums=dense[:, 0, :]):
                dve.wait_ge(qk_rounded, i * 4 + (2 * p + c))
                if c == 1:
                    dve.tensor_tensor(sk_lo[:, p % 2, :], sums, sk_hi[:, p % 2, :].bitcast(F32), ALU.subtract
                                      ).then_inc(qk_split, 1)
                else:
                    dve.scalar_tensor_tensor(sq_lo[:, p % 2, :], sums, SCALE, sq_hi[:, p % 2, :].bitcast(F32),
                                             ALU.mult, ALU.subtract).then_inc(qk_split, 1)

            def stick_pairs(i, end=False):
                for n in range(BODY + PV_LAG + 1):
                    e = n - PV_LAG - 1
                    if e >= 0 and group_end(e) is not None:
                        pr, th = divmod(group_end(e), 2)
                        tk = slice(512 * th, 512 * th + 512)
                        dve.wait_ge(pv_done, i * BODY + (e + 1))
                        for hh in range(2):
                            r = slice(HD * hh, HD * hh + HD)
                            dst = (y2_f[r, bass.ds(i * 2 + pr, 1), tk].rearrange("p a s -> p (a s)")
                                   if not isinstance(i, int) else y2_f[r, 2 * i + pr, tk])
                            dve.tensor_scalar(dst, out_bank(hh)[r, :], 1.0, None, ALU.mult).then_inc(y_copied, 1)
                    if SUM_LAG < n <= BODY + SUM_LAG:
                        w = n - SUM_LAG - 1
                        if w >= 2:
                            dve.wait_ge(pv_done, i * BODY + (w - 1))
                        dve.wait_ge(w_ready, i * BODY + (w + 1))
                        dve.tensor_copy(stick_hi[:, w % 2, PLAN[w % NS][3]:512], z_strip(w)).then_inc(w_round, 1)
                    if SUM_LAG <= n < BODY + SUM_LAG:
                        m = n - SUM_LAG
                        hh, th, a, c0 = PLAN[m % NS]
                        dve.wait_ge(later_ready, i * BODY + (m + 1))
                        dve.tensor_tensor(z_strip(m), z_strip(m), sum_bank(hh, c0), ALU.add).then_inc(arg_ready, 1)
                    if n < BODY:
                        dve.wait_ge(e_ready, i * BODY + (n + 1))
                        dve.tensor_scalar(sp_strip(n), sp_strip(n), BIG_E, None, ALU.min).then_inc(e_clip, 1)
                    if 1 <= n <= BODY:
                        m = n - 1
                        dve.wait_ge(z_copied, i * BODY + (m + 1))
                        dve.wait_ge(ln_ready, i * BODY + (m + 1))
                        dve.tensor_tensor(sp_strip(m), sp_strip(m), z_strip(m), ALU.max).then_inc(sp_ready, 1)
                    if n < BODY and not (end and n >= NS):
                        if n % NS == SPLIT_V:
                            take_values(i, n // NS + 1)
                        if n % NS in (COPY_K, COPY_Q):
                            take(i, n // NS + 1, (COPY_K, COPY_Q).index(n % NS) + 1)

            take(0, 0, 1, sums=dense[:, 1, :])
            take_values(0, 0, sums=side[:, 0, :])
            take(0, 0, 2)
            with dve.Fori(0, SB_H // 4 - 1) as i:
                stick_pairs(i)
            stick_pairs(SB_H // 4 - 1, end=True)
            meet(dve, "dve", met_n)

            for k in range(KB):
                low((a_hi[:, k, :], a_lo[:, k, :]), k, y2_f[:, k, :], "y2", k + 1)
            for n in range(KB):
                u = U_OUT2 + n
                if n in (0, 2):
                    dve.wait_ge(x_returned[n // 2], 16)
                dve.wait_ge(tile_done, T_OUT2 + n + 1)
                dve.scalar_tensor_tensor(x_res[:, n, :], x_res[:, n, :], ALPHA, dense[:, u % 2, :], ALU.mult, ALU.add
                                         ).then_inc(sums_free[u % 2], 1)

            def layer_norm(gain, which):
                norm_n["mean"] += 1
                dve.wait_ge(mean_ready, mean_at[norm_n["mean"] - 1])
                diagonals(side[:, 0, :], TB)
                for k in range(KB):
                    dve.tensor_tensor(x_res[:, k, :], x_res[:, k, :], side[:, 1, :], ALU.subtract).then_inc(centred, 1)
                inverse_std(TB)
                for k in range(KB + 1):
                    if k < KB:
                        if k >= 3:
                            dve.wait_ge(shifted, norm_n["shift"] + k - 2)
                        dve.scalar_tensor_tensor(third(k), x_res[:, k, :], par(gain, k), side[:, 1, :], ALU.mult, ALU.mult
                                                 ).then_inc(scaled, 1)
                    if k and which is not None:
                        m = k - 1
                        low((a_hi[:, m, :], a_lo[:, m, :]), m, x_res[:, m, :], which, m + 1)
                        dve.drain()
                        dve.tensor_scalar(x_res[:, m, :], x_res[:, m, :], ALPHA, None, ALU.mult)
                norm_n["shift"] += KB

            mean_at = [5, 7]
            layer_norm("ln1_g", "x3")

            def squared_relu(i):
                for f in range(FG):
                    u = U_FF2 + f
                    dve.wait_ge(tile_done, i * FF2_TILES + (T_FF2 + f + 1))
                    dve.tensor_scalar(T[:, f, :], dense[:, u % 2, :], 0.0, None, ALU.max)
                    dve.drain()
                    dve.tensor_tensor(T[:, f, :], dense[:, u % 2, :], T[:, f, :], ALU.mult).then_inc(squared, 1)
                    dve.drain().then_inc(sums_free[u % 2], 1)
                    dve.wait_ge(parts["hidden2"][0], i * FG + (f + 1))
                    dve.tensor_tensor(b_lo[:, f, :], T[:, f, :], b_hi[:, f, :].bitcast(F32), ALU.subtract
                                      ).then_inc(parts["hidden2"][1], 1)
                down(i, T_FF2 + FG, U_FF2 + FG, FF2_TILES, 12 + FULL * KB // 2 + KB // 2)

            repeat(dve, FF2_GROUPS, squared_relu)
            layer_norm("ln2_g", None)
            meet(dve, "dve", met_n)


def blocks_of(w, rows, cols):
    return np.stack([w[r][:, cols] for r in rows], axis=1)


def pack(x):
    tiles = np.zeros((TILES, P, KB, P), np.float32)
    n = [0]

    def put(*parts):
        at = 0
        for w, rows, cols in parts:
            b = blocks_of(w, rows, cols)
            tiles[n[0], :, at:at + b.shape[1], :b.shape[2]] = b
            at += b.shape[1]
        n[0] += 1

    def rows(*ks):
        return [slice(P * k, P * k + P) for k in ks]

    full = rows(*range(KB))
    w = x["w_in"][0]
    off = np.cumsum([0, 384, 128, 128, 256, 32, 8, CONV, CONV, CONV, 256])
    o_q, o_k, o_v, o_qi, o_ki, _, o_bg, o_cg, o_u, o_qc, o_gate = off

    def cols(o, j=0):
        return slice(o + P * j, o + P * j + P)

    put((w, full, slice(o_ki, o_ki + IDX_D + IDX_H)))
    for j in range(2):
        put((w, full, cols(o_qi, j)))
    put((w, full, cols(o_k)))
    two = [np.r_[HD * j:HD * j + HD, HD * (j + 3):HD * (j + 3) + HD] for j in range(3)]
    for j in range(3):
        put((w, full, o_q + two[j]))
    put((w, full, cols(o_v)))
    for j in range(4):
        put((x["w_mem_kv"][0], full, cols(0, j)))
    for j in range(2):
        put((w, full, cols(o_qc, j)))
    for j in range(3):
        for o in (o_cg, o_u, o_bg):
            put((w, full, cols(o, j)))
    for j in range(KB):
        for b in range(3):
            put((w, full, cols(o_gate + D * b, j)))
        put((x["w_conv_out"][0], rows(0, 1, 2), cols(0, j)), (x["w_mem_out"][0], rows(0, 1), cols(0, j)))
    for j in range(0, KB, 2):
        put((x["w_att_out"][0], two, cols(0, j)), (x["w_att_out"][0], two, cols(0, j + 1)))
    for j in range(KB):
        put((x["w_o"][0], full, cols(0, j)))
    for f0 in range(0, FB, FG):
        if f0 == FULL * FG:
            for j in range(4):
                put((x["w_mem_kv_2"][0], full, cols(0, j)))
        group = range(f0, min(FB, f0 + FG))
        for f in group:
            put((x["w_up"][0], full, cols(0, f)))
            put((x["w_up"][0], full, cols(FF, f)))
        for j in range(0, KB, 2):
            put((x["w_down"][0], rows(*group), cols(0, j)), (x["w_down"][0], rows(*group), cols(0, j + 1)))
    w = x["w_in_sb_2"][0]
    o_k, o_v, o_qc = SB_H * HD, 2 * SB_H * HD, 3 * SB_H * HD
    for j in range(2):
        put((w, full, cols(o_qc, j)))
    for j in range(SB_H // 2):
        for o in (o_v, o_k, 0):
            put((w, full, cols(o, j)))
    for j in range(KB):
        put((x["w_out_2"][0], full, cols(0, j)))
    for f0 in range(0, FB2, FG):
        group = range(f0, f0 + FG)
        for f in group:
            put((x["w_up_2"][0], full, cols(0, f)))
        for j in range(0, KB, 2):
            put((x["w_down_2"][0], rows(*group), cols(0, j)), (x["w_down_2"][0], rows(*group), cols(0, j + 1)))
    assert n[0] == TILES
    return tiles.reshape(TILES, P, D)


def constants():
    r = np.arange(P)
    c = {"ident": np.eye(P), "ones": np.ones((P, P))}

    def partner(d, half):
        return np.where(d % (8 * half) < half, d + half, d - half)

    def swap(half):
        m = np.zeros((P, P))
        turn = r[r % (8 * half) < 2 * half]
        m[partner(turn, half), turn] = 1
        return m

    c["swap_att"], c["swap_idx"] = swap(8), swap(4)
    c["rep_ki"] = (r[:, None] == r[None, :] % IDX_D).astype(float)
    c["rep_swap_ki"] = c["swap_idx"][:, r % IDX_D] * (r[:, None] < IDX_D)
    c["causal_q"] = np.where(r[None, :] <= r[:, None], 0.0, NEG)
    c["strict_add"] = np.where(r[:, None] < r[None, :], 0.0, NEG)
    c["neg_later"] = -(r[:, None] >= r[None, :]).astype(float)
    c["neg_earlier"] = -(r[:, None] < r[None, :]).astype(float)
    same, to = r[:, None] % IDX_D == np.arange(STACK)[None, :] % IDX_D, np.arange(STACK)[None, :] // IDX_D
    c["stack_mats"] = np.concatenate([same * np.isin(to, g) for g in ((0, 1), (2,), (0, 2), (1,))], axis=1)
    tab = np.zeros((P, 4, S), np.float32)
    for n, half in ((0, 4), (2, 8)):
        freq = np.float32(500000.0) ** (-np.arange(half, dtype=np.float32) / np.float32(half))
        ang = np.arange(S, dtype=np.float32)[:, None] * freq.astype(np.float32)[None, :]
        d = r % (8 * half)
        on = d < 2 * half
        tab[:, n] = np.where(on[:, None], np.cos(ang).T[d % half], 1.0)
        tab[:, n + 1] = np.where(on[:, None], np.where(d < half, -1.0, 1.0)[:, None] * np.sin(ang).T[d % half], 0.0)
    c = {k: np.ascontiguousarray(v, np.float32) for k, v in c.items()}
    c["rope_tab"] = tab
    return c


def small_params(x):
    s = np.zeros((P, SMALL_N), np.float32)

    def put(name, a):
        s[:, SMALL[name]:SMALL[name] + a.shape[1]] = a

    def by_block(v):
        return v.reshape(-1, P).T

    s[:, SMALL["inv_d"]] = 1.0 / D
    for name, src in (("g_mix", "g_mix"), ("g_mem", "g_mem"), ("g_ffn", "g_ffn"), ("ln1_g", "ln_mix_g_2"),
                      ("ln1_b", "ln_mix_b_2"), ("ln2_g", "ln_ffn_g_2"), ("ln2_b", "ln_ffn_b_2")):
        put(name, by_block(x[src][0]))
    put("g_final", by_block(x["g_final"]))
    put("b_gate", x["b_gate"][0].reshape(3, KB, P).transpose(2, 1, 0).reshape(P, 3 * KB))
    put("taps_short", x["conv_w_short"][0].reshape(3, 3, P).transpose(2, 1, 0).reshape(P, 9))
    put("taps_ff", x["conv_w_ffn"][0].reshape(3, 2, FB, P).transpose(3, 2, 1, 0).reshape(P, 6 * FB))
    for h in range(IDX_H):
        s[IDX_D + h, SMALL["pick_wi"] + h] = IDX_SCALE
    return s


def kernel(**inputs):
    import concourse.bacc as bacc
    from concourse.bass_utils import run_bass_kernel_spmd

    x = {k: np.asarray(v) for k, v in inputs.items()}

    def turned(a):
        return np.ascontiguousarray(a[0].reshape(-1, KB, P).transpose(2, 1, 0))

    arrays = {"x_t": turned(x["x"]), "mem_t": turned(x["mem"]), "mem2_t": turned(x["mem_2"]), "w_stream": pack(x),
              "small": small_params(x), **constants()}
    nc = bacc.Bacc("TRN2", target_bir_lowering=False, num_devices=1, dynamic_dma_scratch_size=1024)
    io = {k: nc.dram_tensor("in_" + k, a.shape, F32, kind="ExternalInput").ap() for k, a in arrays.items()}
    out = nc.dram_tensor("out_t", (P, KB, S), F32, kind="ExternalOutput").ap()
    build(nc, io, out)
    r = run_bass_kernel_spmd(nc, [{"in_" + k: a for k, a in arrays.items()}], core_ids=[0])
    y = r.results[0]["out_t"]
    return np.ascontiguousarray(y.transpose(2, 1, 0).reshape(1, S, D))
```

```python
from contextlib import ExitStack

import numpy as np

import concourse.bass as bass
from concourse import mybir

F32 = mybir.dt.float32
F32R = mybir.dt.float32r
ACT = mybir.ActivationFunctionType
ALU = mybir.AluOpType
AX = mybir.AxisListType

P = 128
S = 1024
D = 1024
KB = D // P
TB = S // P
MEM = 256
HD = 64
ATT_H, GROUPS = 6, 2
IDX_H, IDX_D = 8, 32
TOPK = 256
CONV = 384
FF, FF2 = 2816, 4096
SB_H = 12
FB, FB2 = FF // P, FF2 // P
FG = 4
EPS_RMS, EPS_LN = 1e-6, 1e-5
ALPHA = 2.0 ** 0.25
SCALE = HD ** -0.5
IDX_SCALE = (IDX_H * IDX_D) ** -0.5
NEG = -1e30
TAKEN = -3e38
BIG_E = 2.0 ** 60
RAW = 2

T_KI = 0
T_QI = 1
T_K = 3
T_Q = 4
T_V = 7
T_MEM = 8
T_CONV = 14
T_GATE = 23
T_ATT = T_GATE + 4 * KB
T_WO = T_ATT + KB // 2
T_FF = T_WO + KB
FULL, REST = FB // FG, FB % FG
FF_TILES = 2 * FG + KB // 2
T_KV2 = T_FF + FULL * FF_TILES
T_REST = T_KV2 + 4
T_MEM2 = T_REST + 2 * REST + KB // 2
T_SB = T_MEM2 + 2
T_OUT2 = T_SB + 3 * SB_H // 2
T_FF2 = T_OUT2 + KB
FF2_GROUPS = FB2 // FG
FF2_TILES = FG + KB // 2
TILES = T_FF2 + FF2_GROUPS * FF2_TILES
FF_USES = 2 * FG + KB
U_KV2 = T_FF + FULL * FF_USES
U_REST = U_KV2 + 4
U_MEM2 = U_REST + 2 * REST + KB
U_SB = U_MEM2 + 2
U_OUT2 = U_SB
U_FF2 = U_OUT2 + KB
FF2_USES = FG + KB

SMALL, _at = {}, 0
for _name, _n in (("g_mix", KB), ("g_mem", KB), ("g_ffn", KB), ("g_final", KB), ("ln1_g", KB),
                  ("ln1_b", KB), ("ln2_g", KB), ("ln2_b", KB), ("b_gate", 3 * KB), ("taps_short", 9),
                  ("pick_wi", IDX_H), ("taps_ff", 6 * FB)):
    SMALL[_name] = _at
    _at += _n
SMALL_N = _at
IDX_STEPS = (TB - TOPK // P) * IDX_H
DSA_PLAN = [(i, h) for i in range(TB) for h in range(ATT_H)]
DSA_STEPS = len(DSA_PLAN)
IDX_S = S - TOPK
STACK = 3 * IDX_D
MATRICES = ("ident", "ones", "swap_att", "swap_idx", "rep_ki", "rep_swap_ki", "causal_q", "strict_add", "neg_later",
            "neg_earlier")


def stick_plan():
    return [(hh, th, a, max(0, a * P - 512 * th)) for th in range(2) for a in range(4 * th + 3, -1, -1)
            for hh in range(2)]


PLAN = stick_plan()
NS = len(PLAN)
BODY = 2 * NS
CARRIES = np.cumsum([PLAN[n % NS][2] > 0 for n in range(BODY + NS)]).tolist()
BETWEEN = {3: (0, 0, 2), 4: (0, 2, 4), 5: (0, 4, 6), 6: (0, 6, 7), 7: (0, 7, 8),
           9: (1, 0, 1), 10: (1, 1, 3), 11: (1, 3, 5), 12: (1, 5, 6), 13: (1, 6, 7), 14: (1, 7, 8),
           **{16 + k: (2, k, k + 1) for k in range(KB)}}
SPLIT_STEPS = (1, 9, 17)
SUM_LAG, PV_LAG = 3, 5
LEAD = PV_LAG + 2
COPY_Q, COPY_K = 8, 15
COPY_V, TURN_V, SPLIT_V = 0, 1, 2
EARLY = 2


def active(n, lag, end):
    return n >= lag and (not end or n < BODY + lag)


def score_at(i):
    return P * (i * (i + 1) // 2)


def repeat(eng, n, body):
    body(0)
    with eng.Fori(1, n) as i:
        body(i)


def build(nc, io, out):
    with ExitStack() as ctx:
        base = (nc.sbuf_base + 31) // 32 * 32

        def at(name, shape, dtype, kib):
            return nc.alloc_sbuf_tensor_at(name, shape, dtype, offset=base + int(kib * 1024))

        def sem(name):
            return ctx.enter_context(nc.semaphore(name))

        def pair(name):
            return [sem(f"{name}{s}") for s in range(2)]

        raw = at("raw", [P, RAW, D], F32, 0)
        w_hi = at("w_hi", [P, 2, D], F32R, 8)
        w_lo = at("w_lo", [P, 2, D], F32R, 16)
        a_hi = at("a_hi", [P, KB, S], F32R, 24)
        a_lo = at("a_lo", [P, KB, S], F32R, 56)
        T = at("T", [P, 4, S], F32, 88)
        mats = {name: at(name, [P, P], F32, 104 + 0.5 * n) for n, name in enumerate(MATRICES)}
        ident, ones = mats["ident"], mats["ones"]
        small = at("small", [P, SMALL_N], F32, 109.5)
        tiny = at("tiny", [P, 256], F32, 110.75)
        bias_now = tiny[:, 224:225]
        zero = at("zero", [P, 8], F32, 111.75)
        Y0 = 112
        k_f = at("k_f", [P, S], F32, Y0)
        q_f = at("q_f", [P, 3, S], F32, Y0 + 4)
        v_f = at("v_f", [P, TB, P], F32, Y0 + 16)
        score = at("score", [P, score_at(TB)], F32, Y0 + 20)
        rope_tab = at("rope_tab", [P, 4, S], F32, Y0 + 20)
        x_in = at("x_in", [P, KB, S], F32, Y0 + 38)
        qi_f = at("qi_f", [P, 2, S], F32, Y0 + 38)
        ki_f = at("ki_f", [P, S], F32, Y0 + 46)
        qc_f = at("qc_f", [P, 2, S], F32, Y0 + 98)
        mem_squares = at("mem_squares", [P, KB, MEM], F32, Y0 + 90)
        m_hi = at("m_hi", [P, KB, MEM], F32R, Y0 + 74)
        m_lo = at("m_lo", [P, KB, MEM], F32R, Y0 + 82)
        ym_f = at("ym_f", [P, 2, S], F32, Y0 + 74)
        ym_hi = at("ym_hi", [P, 2, S], F32R, Y0 + 58)
        ym_lo = at("ym_lo", [P, 2, S], F32R, Y0 + 66)
        km_f = at("km_f", [P, 2, MEM], F32, Y0 + 90)
        vm_f = at("vm_f", [P, 2, MEM], F32, Y0 + 92)
        vm_t = at("vm_t", [P, 2, MEM], F32, Y0 + 94)
        m_in = at("m_in", [P, KB, MEM], F32, Y0 + 98)
        qi_hi, qi_lo = (at(n, [P, 2, IDX_S], F32R, 88 + 6 * m) for m, n in enumerate(("qi_hi", "qi_lo")))
        ki_hi, ki_lo = (at(n, [P, S], F32R, Y0 + 98 + 4 * m) for m, n in enumerate(("ki_hi", "ki_lo")))
        stack_in = at("stack_in", [P, 4 * STACK], F32, Y0 + 36)
        stack_mats = at("stack_mats", [P, 4, STACK], F32R, Y0 + 106)
        ki_stack = at("ki_stack", [P, S], F32R, Y0 + 46)
        qi_stack = at("qi_stack", [P, IDX_H, IDX_S], F32R, Y0 + 50)
        yc_hi = at("yc_hi", [P, 3, S], F32R, Y0 + 74)
        yc_lo = at("yc_lo", [P, 3, S], F32R, Y0 + 86)
        gates = at("gates", [P, 4, S], F32, Y0 + 38)
        ya_f = at("ya_f", [P, 3, S], F32, Y0 + 38)
        ya_hi = at("ya_hi", [P, 3, S], F32R, Y0 + 50)
        ya_lo = at("ya_lo", [P, 3, S], F32R, Y0 + 62)
        back = at("back", [P, 4, S], F32, Y0 + 74)
        x_res = at("x_res", [P, KB, S], F32, Y0)
        b_hi = at("b_hi", [P, FG, S], F32R, Y0 + 38)
        b_lo = at("b_lo", [P, FG, S], F32R, Y0 + 54)
        qc2_f = at("qc2_f", [P, 2, S], F32, Y0 + 38)
        y2_f = at("y2_f", [P, KB, S], F32, Y0 + 38)
        sq_hi, sq_lo, sk_hi, sk_lo = (at(n, [P, 2, S], F32R, Y0 + 8 * m) for m, n in enumerate(("sq_hi", "sq_lo", "sk_hi",
                                                                                               "sk_lo")))
        sv_t = at("sv_t", [P, S], F32, Y0 + 32)
        stick_mats = at("stick_mats", [P, 4, P], F32R, Y0 + 36)
        ident_r, strict_r, later_r, earlier_r = (stick_mats[:, n, :] for n in range(4))
        sv = at("sv", [P, 2, TB, 2, P], F32R, Y0 + 70)
        out_low = at("out_low", [HD, 2, 512], F32, Y0 + 32)
        z_ring = at("z_ring", [P, 6, 512], F32, Y0 + 86)
        sp_hi, sp_lo = (at(n, [P, 3, 512], F32R, Y0 + 98 + 6 * m) for m, n in enumerate(("sp_hi", "sp_lo")))
        sp_ring = at("sp_ring", [P, 4, 512], F32, 88)
        stick_hi, stick_lo = (at(n, [P, 2, 512], F32R, 96 + 4 * m) for m, n in enumerate(("stick_hi", "stick_lo")))

        def par(name, k=0):
            return small[:, SMALL[name] + k:SMALL[name] + k + 1]

        own_sum = tiny[:, 232:240]
        row_max, neg_max = tiny[:, 0:8], tiny[:, 8:16]
        row_sum, inv_sum = tiny[:, 16:24], tiny[:, 24:32]
        std, rstd = tiny[:, 32:40], tiny[:, 40:48]
        best = tiny[:, 48:96].rearrange("p (b e) -> p b e", e=8)
        taps_act, taps_dve = tiny[:, 96:96 + 6 * FG], tiny[:, 128:128 + 6 * FG]
        wi_f = tiny[:, 160:160 + TB * IDX_H].rearrange("p (i h) -> p i h", h=IDX_H)

        dense = ctx.enter_context(nc.psum_tensor("dense", [P, 2, S], F32))
        side = ctx.enter_context(nc.psum_tensor("side", [P, 2, S], F32))

        weights_loaded = [sem(f"weights_loaded{r}") for r in range(RAW)]
        weights_rounded, weights_split = sem("weights_rounded"), sem("weights_split")
        tile_done, first_done = sem("tile_done"), sem("first_of_two_done")
        sums_free = pair("sums_free")
        consts_in, tables_in, x_back, out_stored = sem("consts_in"), sem("tables_in"), sem("x_back"), sem("out_stored")
        x_loaded = [sem(f"x_loaded{c}") for c in range(4)]
        mem_loaded, mem2_loaded = sem("mem_loaded"), sem("mem2_loaded")
        met = {e: sem(f"met_{e}") for e in ("pe", "act", "dve")}
        squares, squares_used = sem("squares_ready"), sem("squares_used")
        sum_ready, own_ready = sem("sum_ready"), sem("own_sums_ready")
        std_ready, diag_ready, spread_ready = sem("std_ready"), sem("diagonals_ready"), sem("spread_ready")
        scaled, shifted = sem("scaled_ready"), sem("shifted_ready")
        centred = sem("centred_ready")
        parts = {n: (sem(n + "_rounded"), sem(n + "_split")) for n in (
            "h", "mem", "ym", "yc", "ya", "merged", "h2", "hidden", "x2", "mem2", "y2", "x3", "hidden2")}
        yc_ready = sem("conv_out_ready")
        turned, roped, turn_free = sem("proj_turned"), sem("proj_rotated"), pair("turn_free")
        idx_round, idx_split, stacked, stack_copied = (sem("index_rounded"), sem("index_split"), sem("index_stacked"),
                                                       sem("index_stack_copied"))
        idx_ready, rel_ready, rel_used = sem("index_products"), sem("relu_ready"), sem("relu_used")
        mturned = sem("mem_values_turned")
        lg_ready, lg_max, lg_exp, lg_p = sem("logits_ready"), sem("row_max_ready"), sem("exp_ready"), sem("probs_ready")
        lg_t, lg_tc, lg_o, lg_oc = (sem("probs_turned"), sem("probs_copied"), sem("heads_ready"), sem("heads_copied"))
        conv_used = sem("conv_gate_used")
        part_ready, branch_free = sem("partial_ready"), pair("branch_free")
        gate_spilled, part_spilled, fetched = pair("gate_spilled"), pair("partial_spilled"), pair("fetched")
        att_sums, att_free, merged_sum = sem("att_out_ready"), pair("att_out_free"), sem("merged_ready")
        tap_ready, taps_done, acted = sem("first_tap_ready"), sem("taps_done"), sem("hidden_gate_ready")
        product_ready, squared = sem("hidden_product_ready"), sem("hidden_squared")
        v_copied, v_turned, v_rounded, v_split = (sem("stick_values_copied"), sem("stick_values_turned"),
                                                  sem("stick_values_rounded"), sem("stick_values_split"))
        qk_rounded, qk_split = sem("stick_qk_rounded"), sem("stick_qk_split")
        z_copied = sem("z_copied")
        z_ready, e_ready, e_clip, ln_ready, sp_ready = (sem("z_ready"), sem("exp_z_ready"), sem("exp_z_clipped"),
                                                        sem("log_ready"), sem("softplus_ready"))
        sp_round, sp_split = sem("softplus_rounded"), sem("softplus_split")
        later_ready, carried, arg_ready = sem("later_sums_ready"), sem("carried"), sem("exponent_ready")
        w_ready, w_round, w_split = sem("stick_weights_ready"), sem("stick_weights_rounded"), sem("stick_weights_split")
        pv_done, low_ready, y_copied = sem("stick_pv_done"), sem("stick_low_parts_ready"), sem("stick_heads_copied")
        x_spilled, x_returned = sem("x_spilled"), [sem(f"x_returned{n}") for n in range(2)]

        spill_gate = nc.dram_tensor("spill_gate", [KB, P, S], F32).ap()
        spill_x = nc.dram_tensor("spill_x", [P, KB, S], F32).ap()
        spill_part = nc.dram_tensor("spill_part", [KB, P, S], F32).ap()

        block = ctx.enter_context(nc.Block())

        def out_bank(hh, c0=0):
            return dense[:, 1, 512 * hh + c0:512 * hh + 512]

        def sum_bank(hh, c0=0):
            return side[:, 0, 512 * hh + c0:512 * hh + 512]

        def z_bank(n, c0=0):
            return side[:, 1, 512 * (n % 2) + c0:512 * (n % 2) + 512]

        def sp_strip(n):
            return sp_ring[:, n % 4, PLAN[n % NS][3]:512]

        def z_strip(n):
            return z_ring[:, n % 6, PLAN[n % NS][3]:512]

        def group_end(n):
            hh, th, a, _ = PLAN[n % NS]
            return 4 * (n // NS) + 2 * th + hh if a == 0 else None

        def emptied(eng, u, i=0, per=0):
            eng.wait_ge(sums_free[u % 2], i * (per // 2) + (u // 2 + 1))

        def meet(eng, me, count):
            count[0] += 1
            eng.drain().then_inc(met[me], 1)
            for other in met:
                if other != me:
                    eng.wait_ge(met[other], count[0])

        @block.sync
        def _(sp):
            sp.dma_start(small[:, :], io["small"]).then_inc(consts_in, 16)
            for name in MATRICES[:2]:
                sp.dma_start(mats[name][:, :], io[name]).then_inc(consts_in, 16)
            for c in range(4):
                sp.dma_start(x_in[:, 2 * c:2 * c + 2, :], io["x_t"][:, 2 * c:2 * c + 2, :]).then_inc(x_loaded[c], 16)
            for r in range(RAW):
                sp.dma_start(raw[:, r, :], io["w_stream"][r]).then_inc(weights_loaded[r], 16)
            sp.dma_start(m_in[:, :, :], io["mem_t"]).then_inc(mem_loaded, 16)
            for name in MATRICES[2:]:
                sp.dma_start(mats[name][:, :], io[name]).then_inc(tables_in, 16)
            sp.dma_start(rope_tab[:, :, :], io["rope_tab"]).then_inc(tables_in, 16)
            sp.dma_start(stack_in[:, :], io["stack_mats"]).then_inc(tables_in, 16)
            with sp.Fori(1, TILES // RAW) as i:
                for r in range(RAW):
                    sp.wait_ge(weights_split, i * RAW + (r - RAW + 1))
                    sp.dma_start(raw[:, r, :], io["w_stream"][bass.ds(i * RAW + r, 1)].rearrange("a p k -> p (a k)")
                                 ).then_inc(weights_loaded[r], 16)
            for r in range(TILES % RAW):
                t = TILES // RAW * RAW + r
                sp.wait_ge(weights_split, t - RAW + 1)
                sp.dma_start(raw[:, r, :], io["w_stream"][t]).then_inc(weights_loaded[r], 16)

        CONSTS, TABLES = 16 * 3, 16 * len(MATRICES)

        @block.gpsimd
        def _(pool):
            def split(t, r, loads):
                pool.wait_ge(weights_loaded[r], loads)
                pool.tensor_tensor(w_hi[:, r % 2, :], raw[:, r, :], zero[:, 0:1].broadcast_to([P, D]), ALU.add).then_inc(weights_rounded, 1)
                pool.wait_ge(weights_rounded, t + 1)
                pool.tensor_tensor(w_lo[:, r % 2, :], raw[:, r, :], w_hi[:, r % 2, :].bitcast(F32), ALU.subtract
                                   ).then_inc(weights_split, 1)

            pool.memset(zero[:, :], 0.0)
            pool.drain()
            for r in range(RAW):
                if r >= 2:
                    pool.wait_ge(tile_done, r - 1)
                split(r, r, 16)
            def split_tiles(begin, end):
                def one(t):
                    pool.wait_ge(tile_done, t - 1)
                    split(t, t % RAW, 16 * (t // RAW) + 16)

                if begin % RAW:
                    one(begin)
                with pool.Fori(-(-begin // RAW), end // RAW) as i:
                    for r in range(RAW):
                        pool.wait_ge(tile_done, i * RAW + (r - 1))
                        split(i * RAW + r, r, i * 16 + 16)
                if end % RAW:
                    one(end - 1)

            def split_half(t, i, c):
                half = slice(512 * c, 512 * c + 512)
                if c == 0:
                    pool.wait_ge(weights_rounded, i * 6 + (t + 1))
                done = pool.tensor_tensor(w_lo[:, t % 2, half], raw[:, t % RAW, half], w_hi[:, t % 2, half].bitcast(F32),
                                          ALU.subtract)
                if c == 1:
                    done.then_inc(weights_split, 1)

            def stick_steps(i, begin, stop, end=False):
                for n in range(begin, stop):
                    if active(n, 2, end):
                        m, c0 = n - 2, PLAN[(n - 2) % NS][3]
                        pool.wait_ge(sp_round, i * BODY + (m + 1))
                        pool.tensor_tensor(sp_lo[:, m % 3, c0:512], sp_strip(m), sp_hi[:, m % 3, c0:512].bitcast(F32),
                                           ALU.subtract).then_inc(sp_split, 1)
                    if active(n, SUM_LAG + 1, end):
                        m, c0 = n - SUM_LAG - 1, PLAN[(n - SUM_LAG - 1) % NS][3]
                        pool.wait_ge(w_round, i * BODY + (m + 1))
                        pool.tensor_tensor(stick_lo[:, m % 2, c0:512], z_strip(m), stick_hi[:, m % 2, c0:512].bitcast(F32),
                                           ALU.subtract).then_inc(w_split, 1)
                    if active(n, 0, end):
                        for c, at_step in enumerate(SPLIT_STEPS):
                            if 1 <= n % NS - at_step <= 2 and not (end and n >= NS and c):
                                split_half(T_SB + 3 * (n // NS + 1) + c + 1, i, n % NS - at_step - 1)

            split_tiles(RAW, T_ATT + 2)
            for i in range(TB):
                cols = slice(i * P, i * P + P)
                pool.wait_ge(parts["ya"][0], i + 1)
                pool.tensor_tensor(ya_lo[:, :, cols], ya_f[:, :, cols], ya_hi[:, :, cols].bitcast(F32), ALU.subtract
                                   ).then_inc(parts["ya"][1], 1)
            split_tiles(T_ATT + 2, T_KV2)
            for t in range(T_KV2, T_KV2 + 4):
                pool.wait_ge(weights_rounded, t + 1)
                pool.tensor_tensor(w_lo[:, t % 2, :], raw[:, t % RAW, :], w_hi[:, t % 2, :].bitcast(F32), ALU.subtract
                                   ).then_inc(weights_split, 1)
            split_tiles(T_KV2 + 4, T_SB + 4)
            stick_steps(0, 0, LEAD)
            with pool.Fori(0, SB_H // 4 - 1) as i:
                stick_steps(i, LEAD, BODY + LEAD)
            stick_steps(SB_H // 4 - 1, LEAD, BODY + LEAD, end=True)
            split_tiles(T_OUT2 + 2, TILES)

        @block.tensor
        def _(pe):
            met_n, norm_n = [0], {"sq": 0, "mean": 0, "diag": 0}

            def halves(psum, s, width=S):
                return [psum[:, s, c:min(c + 512, width)] for c in range(0, width, 512)]

            def product(slot, outs, hi, lo, blocks, at_block=0, ready=None, begin=0, end=True):
                for b in range(begin, blocks):
                    w = slice(P * (at_block + b), P * (at_block + b) + P)
                    stop = end and b == blocks - 1
                    if ready is not None:
                        pe.wait_ge(ready, b + 1)
                    for c, o in enumerate(outs):
                        x = slice(c * 512, c * 512 + o.shape[-1])
                        pe.matmul(o, w_hi[:, slot, w], hi[:, b, x], start=b == 0, stop=False)
                        pe.matmul(o, w_hi[:, slot, w], lo[:, b, x], start=False, stop=False)
                    for c, o in enumerate(outs):
                        x = slice(c * 512, c * 512 + o.shape[-1])
                        last = pe.matmul(o, w_lo[:, slot, w], hi[:, b, x], start=False, stop=stop)
                return last

            def tile(t, u, hi=a_hi, lo=a_lo, blocks=KB, width=S, at_block=0, ready=None, i=0, per=(0, 0),
                     done=tile_done):
                s = u % 2
                if u >= 2:
                    pe.wait_ge(sums_free[s], i * (per[1] // 2) + u // 2)
                pe.wait_ge(weights_split, i * per[0] + (t + 1))
                product(t % 2, halves(dense, s, width), hi, lo, blocks, at_block, ready).then_inc(done, 1)

            def two_tiles(t, u, ready, lag=0):
                for n in range(KB + lag):
                    for m in range(2):
                        b = n - lag * m
                        if not 0 <= b < KB:
                            continue
                        if b == 0:
                            if u + m >= 2:
                                pe.wait_ge(sums_free[(u + m) % 2], (u + m) // 2)
                            pe.wait_ge(weights_split, t + m + 1)
                        if m == 0:
                            pe.wait_ge(ready, b + 1)
                        last = product((t + m) % 2, halves(dense, (u + m) % 2), a_hi, a_lo, b + 1, begin=b, end=b == KB - 1)
                        if b == KB - 1:
                            last.then_inc(tile_done, 1)

            def sum_part(k, src, width, at=0):
                for c in range(0, width, 512):
                    e = min(width, c + 512)
                    last = pe.matmul(side[:, at, c:e], ones[:, :], src[:, c:e], start=k == 0, stop=k == KB - 1,
                                     skip_group_check=True)
                return last

            def squares_part(k, width=S, src=None):
                pe.wait_ge(squares, norm_n["sq"] + k + 1)
                sum_part(k, T[:, k % 2, :] if src is None else src[:, k, :], width
                         ).then_inc(squares_used if k < KB - 1 else sum_ready, 1)

            def rms(width, begin=0):
                for k in range(begin, KB):
                    squares_part(k, width)
                norm_n["sq"] += KB
                pe.wait_ge(diag_ready, norm_n["diag"] + 1)
                norm_n["diag"] += 1
                for c in range(0, width, 512):
                    e = min(width, c + 512)
                    last = pe.matmul(side[:, 1, c:e], ones[:, :], T[:, 2, c:e], start=True, stop=True)
                last.then_inc(spread_ready, 1)

            def residual_sum(k, u):
                emptied(pe, u + k)
                last = sum_part(k, x_res[:, k, :], S, at=1)
                if k == KB - 1:
                    last.then_inc(sum_ready, 1)

            pe.wait_ge(consts_in, CONSTS)
            rms(S)

            def turn(n, src, matrices):
                for m, (v, matrix) in enumerate(matrices):
                    if m == 0:
                        emptied(pe, n)
                    if v >= 2:
                        pe.wait_ge(turn_free[v % 2], v // 2)
                    for c in range(0, S, 512):
                        last = pe.matmul(side[:, v % 2, c:c + 512], matrix[:, :], src[:, c:c + 512], start=True, stop=True)
                    last.then_inc(turned, 1)

            for t in range(T_KI, T_MEM):
                if t == 0:
                    two_tiles(t, t, parts["h"][1])
                    pe.wait_ge(tables_in, TABLES)
                    for k in range(KB):
                        squares_part(k, MEM, mem_squares)
                elif t > 2:
                    tile(t, t)
                if t == 2:
                    pe.wait_ge(sums_free[0], 1)
                    pe.wait_ge(weights_split, t + 1)
                    product(0, halves(dense, 0), a_hi, a_lo, KB // 2, end=False)
                    rms(MEM, begin=KB)
                    product(0, halves(dense, 0), a_hi, a_lo, KB, begin=KB // 2).then_inc(tile_done, 1)
                    pe.wait_ge(scaled, 2 * KB)
                    turn(0, T[:, 0, :], [(0, mats["rep_ki"]), (1, mats["rep_swap_ki"])])
                    pe.wait_ge(turn_free[0], 1)
                    for b in range(TB):
                        last = pe.matmul(side[:, 0, b * IDX_H:b * IDX_H + IDX_H], T[:, 0, b * P:b * P + P],
                                         small[:, SMALL["pick_wi"]:SMALL["pick_wi"] + IDX_H], start=True, stop=True,
                                         skip_group_check=True)
                    last.then_inc(turned, 1)
                if t >= 2:
                    turn(t - 1, T[:, (t - 1) % 2, :], [(t + 1, mats["swap_idx" if t - 1 < T_K else "swap_att"])])
            emptied(pe, T_V)
            pe.wait_ge(turn_free[1], 4)
            for b in range(TB):
                last = pe.transpose(side[:, 1, b * P:b * P + P], T[:, T_V % 2, b * P:b * P + P], ident[:, :])
            last.then_inc(turned, 1)
            meet(pe, "pe", met_n)

            for n in range(IDX_H + 1):
                width, head = (S, 0) if n == 0 else (IDX_S, n - 1)
                hi, lo = (ki_hi, ki_lo) if n == 0 else (qi_hi[:, head // 4, :], qi_lo[:, head // 4, :])
                r = slice(IDX_D * (head % 4), IDX_D * (head % 4) + IDX_D)
                pe.wait_ge(idx_split, 1 if n == 0 else head // 4 + 2)
                if n >= 2:
                    pe.wait_ge(stack_copied, n - 1)
                for c in range(0, width, 512):
                    e = min(width, c + 512)
                    m = 0 if n == 0 else 2
                    pe.matmul(side[0:STACK, n % 2, c:e], stack_mats[r, m, :], hi[r, c:e], start=True, stop=False)
                    last = pe.matmul(side[0:STACK, n % 2, c:e], stack_mats[r, m + 1, :], lo[r, c:e], start=False, stop=True)
                last.then_inc(stacked, 1)
            pe.wait_ge(stack_copied, IDX_H + 1)

            def memory_block(t, b):
                if b == 0:
                    pe.wait_ge(sums_free[t % 2], t // 2)
                    pe.wait_ge(weights_split, t + 1)
                own = t < T_MEM + 4
                last = product(t % 2, halves(dense, t % 2, MEM if own else S), m_hi if own else a_hi, m_lo if own else a_lo,
                               b + 1, begin=b, end=b == KB - 1)
                if b == KB - 1:
                    last.then_inc(tile_done, 1)

            pe.wait_ge(parts["mem"][1], KB)
            for n in range(IDX_STEPS):
                i, h = TOPK // P + n // IDX_H, n % IDX_H
                q = slice(i * P - TOPK, i * P - TOPK + P)
                if n >= 2:
                    pe.wait_ge(rel_ready, n - 1)
                for c in range(0, P * (i + 1), 512):
                    e = min(P * (i + 1), c + 512)
                    last = pe.matmul(side[:, n % 2, c:e], qi_stack[0:STACK, h, q], ki_stack[0:STACK, c:e], start=True, stop=True)
                last.then_inc(idx_ready, 1)
                memory_block(T_MEM + n // KB, n % KB)
            pe.wait_ge(rel_ready, IDX_STEPS)

            def probs_turn(n, n0, blocks):
                pe.wait_ge(lg_p, n0 + n + 1)
                if n >= 2:
                    pe.wait_ge(lg_oc, n0 + n - 1)
                for b in range(blocks):
                    last = pe.transpose(dense[:, n % 2, b * P:b * P + P], T[:, n % 2, b * P:b * P + P], ident[:, :])
                last.then_inc(lg_t, 1)

            def memory(u_kv, qc, n0):
                emptied(pe, u_kv + 2)
                emptied(pe, u_kv + 3)
                for mt in range(2):
                    for j in range(2):
                        last = pe.transpose(side[:, 0, mt * MEM + j * P:mt * MEM + j * P + P],
                                            vm_t[:, j, mt * P:mt * P + P], ident[:, :])
                last.then_inc(mturned, 1)
                meet(pe, "pe", met_n)
                for n in range(TB + 2):
                    if n < TB:
                        if n >= 2:
                            pe.wait_ge(lg_exp, n0 + n - 1)
                        for h in range(4):
                            o = 512 * (h % 2) + MEM * (h // 2)
                            r = slice(HD * (h % 2), HD * (h % 2) + HD)
                            last = pe.matmul(side[:, n % 2, o:o + MEM], qc[r, h // 2, n * P:n * P + P], km_f[r, h // 2, :],
                                             start=h < 2, stop=True, skip_group_check=True)
                        last.then_inc(lg_ready, 1)
                    if 1 <= n <= TB:
                        probs_turn(n - 1, n0, KB)
                    if n >= 2:
                        b = n - 2
                        pe.wait_ge(lg_tc, n0 + b + 1)
                        for h in range(4):
                            q = 2 * (h % 2) + h // 2
                            for mt in range(2):
                                last = pe.matmul(dense[:, b % 2, h * P:h * P + P], vm_f[:, mt, h // 2 * P:h // 2 * P + P],
                                                 T[:, 2 + b % 2, (2 * q + mt) * P:(2 * q + mt) * P + P],
                                                 start=h == 0 and mt == 0, stop=mt == 1, skip_group_check=True)
                        last.then_inc(lg_o, 1)
                meet(pe, "pe", met_n)

            memory(T_MEM, qc_f, 0)

            for t in range(T_CONV, T_GATE):
                tile(t, t)

            def gate_blocks(i):
                for j in range(2):
                    for c in range(4):
                        t = T_GATE + 4 * j + c
                        if c < 3:
                            tile(t, t, i=i, per=(8, 8))
                        else:
                            if isinstance(i, int) and j == 0:
                                pe.wait_ge(parts["yc"][1], 3)
                                pe.wait_ge(parts["ym"][1], 2)
                            tile(t, t, hi=yc_hi, lo=yc_lo, blocks=3, i=i, per=(8, 8), done=first_done)
                            if not isinstance(i, int):
                                pe.wait_ge(branch_free[j], i)
                            product(t % 2, halves(side, j), ym_hi, ym_lo, 2, at_block=3).then_inc(tile_done, 1)

            repeat(pe, 4, gate_blocks)
            meet(pe, "pe", met_n)

            for n in range(DSA_STEPS + 2):
                if n < DSA_STEPS:
                    i, h = DSA_PLAN[n]
                    r = slice(HD * (h // 3), HD * (h // 3) + HD)
                    if n >= 2:
                        pe.wait_ge(lg_max, TB + n - 1)
                    for c in range(0, P * (i + 1), 512):
                        e = min(P * (i + 1), c + 512)
                        last = pe.matmul(side[:, n % 2, c:e], q_f[r, h % 3, i * P:i * P + P], k_f[r, c:e], start=True,
                                         stop=True)
                    last.then_inc(lg_ready, 1)
                if 1 <= n <= DSA_STEPS:
                    probs_turn(n - 1, TB, DSA_PLAN[n - 1][0] + 1)
                if n >= 2:
                    b = n - 2
                    i = DSA_PLAN[b][0]
                    pe.wait_ge(lg_tc, TB + b + 1)
                    for kb in range(i + 1):
                        last = pe.matmul(dense[:, b % 2, 0:P], v_f[:, kb, :], T[:, 2 + b % 2, kb * P:kb * P + P],
                                         start=kb == 0, stop=kb == i)
                    last.then_inc(lg_o, 1)
            meet(pe, "pe", met_n)

            pe.wait_ge(parts["ya"][1], TB)
            for n in range(KB // 2):
                t = T_ATT + n
                tile(t, t, hi=ya_hi, lo=ya_lo, blocks=3, done=first_done)
                if n >= 2:
                    pe.wait_ge(att_free[n % 2], n // 2)
                product(t % 2, halves(side, n % 2), ya_hi, ya_lo, 3, at_block=3).then_inc(tile_done, 1)
            for n in range(KB):
                if n == 0:
                    two_tiles(T_WO, T_WO, parts["merged"][1], lag=4)
                elif n >= 2:
                    tile(T_WO + n, T_WO + n)
                    squares_part(n - 2)
            rms(S, begin=KB - 2)

            def feed(t0, u0, ups, hidden, blocks, per, ready, n0):
                def group(i, behind=None):
                    for c in range(ups):
                        if isinstance(i, int) and i == 0 and ready is not None and c < 2:
                            if c == 0:
                                two_tiles(t0, u0, ready)
                        else:
                            tile(t0 + c, u0 + c, i=i, per=per)
                    t = t0 + ups
                    pe.wait_ge(weights_split, i * per[0] + (t + 1))
                    for m in range(2):
                        u = u0 + ups + m
                        pe.wait_ge(sums_free[u % 2], i * (per[1] // 2) + u // 2)
                        if m == 0:
                            pe.wait_ge(hidden, i * blocks + (n0 + blocks - 1))
                        product(t % 2, halves(dense, u % 2), b_hi, b_lo, blocks - 1, m * blocks, end=False)
                    pe.wait_ge(hidden, i * blocks + (n0 + blocks))
                    for m in range(2):
                        product(t % 2, halves(dense, (u0 + ups + m) % 2), b_hi, b_lo, blocks, m * blocks, begin=blocks - 1
                                ).then_inc(tile_done if m else first_done, 1)
                    for c in range(1, KB // 2):
                        for m in range(2):
                            tile(t + c, u0 + ups + 2 * c + m, hi=b_hi, lo=b_lo, blocks=blocks, at_block=m * blocks, i=i,
                                 per=per, done=tile_done if m else first_done)
                            if behind is not None:
                                behind(2 * c + m - 2)
                return group

            h2 = parts["h2"][1]
            hidden = parts["hidden"][1]
            repeat(pe, FULL, feed(T_FF, T_FF, 2 * FG, hidden, FG, (FF_TILES, FF_USES), h2, 0))
            for n in range(4):
                tile(T_KV2 + n, U_KV2 + n, hi=m_hi, lo=m_lo, width=MEM, ready=parts["mem2"][1] if n == 0 else None)
            feed(T_REST, U_REST, 2 * REST, hidden, REST, (0, 0), None, FULL * FG)(0, behind=squares_part)
            rms(S, begin=KB - 2)

            two_tiles(T_MEM2, U_MEM2, parts["x2"][1])
            emptied(pe, U_MEM2)
            emptied(pe, U_MEM2 + 1)
            memory(U_KV2, qc2_f, TB + DSA_STEPS)

            def project(i, p, c, begin, end, sums=dense[:, 0, :]):
                t = T_SB + 3 * p + c
                if begin == 0:
                    if c == 0 and p:
                        pe.wait_ge(v_split, i * 2 + p)
                    if c == 1 and p:
                        pe.wait_ge(qk_split, i * 4 + (2 * p + 1))
                    if c == 2:
                        pe.wait_ge(qk_split, i * 4 + (2 * p + (2 if p else 1)))
                    pe.wait_ge(weights_split, i * 6 + (t + 1))
                last = product(t % 2, [sums[:, 0:512], sums[:, 512:S]], a_hi, a_lo, end, begin=begin, end=end == KB)
                if end == KB:
                    last.then_inc(tile_done, 1)

            def turn_values(i, p, sums=dense[:, 0, :]):
                pe.wait_ge(v_copied, i * 2 + (p + 1))
                for b in range(TB):
                    last = pe.transpose(sums[:, b * P:b * P + P], sv_t[:, b * P:b * P + P], ident[:, :])
                last.then_inc(v_turned, 1)

            def stick_steps(i, begin, stop, end=False):
                for n in range(begin, stop):
                    if active(n, 0, end):
                        pr, (hh, th, a, c0) = n // NS, PLAN[n % NS]
                        r = slice(HD * hh, HD * hh + HD)
                        kb, tk = slice(a * P, a * P + P), slice(512 * th + c0, 512 * th + 512)
                        if n % NS == 0:
                            pe.wait_ge(qk_split, i * 4 + (2 * pr + 2))
                        if n >= 2:
                            pe.wait_ge(z_copied, i * BODY + (n - 1))
                        z = z_bank(n, c0)
                        if a >= 4 * th:
                            pe.matmul(z[:, 0:P], ident_r, strict_r, start=True, stop=False, skip_group_check=True)
                        pe.matmul(z, sk_hi[r, pr % 2, kb], sq_hi[r, pr % 2, tk], start=a < 4 * th, stop=False, skip_group_check=True)
                        pe.matmul(z, sk_hi[r, pr % 2, kb], sq_lo[r, pr % 2, tk], start=False, stop=False, skip_group_check=True)
                        pe.matmul(z, sk_lo[r, pr % 2, kb], sq_hi[r, pr % 2, tk], start=False, stop=True, skip_group_check=True
                                  ).then_inc(z_ready, 1)
                    if active(n, SUM_LAG + 1, end) and PLAN[(n - SUM_LAG - 1) % NS][2] > 0:
                        m = n - SUM_LAG - 1
                        hh, th, a, c0 = PLAN[m % NS]
                        pe.wait_ge(arg_ready, i * BODY + (m + 1))
                        pe.matmul(sum_bank(hh, c0), earlier_r, sp_hi[:, m % 3, c0:512], start=False, stop=False,
                                  skip_group_check=True)
                        pe.matmul(sum_bank(hh, c0), earlier_r, sp_lo[:, m % 3, c0:512], start=False, stop=True,
                                  skip_group_check=True).then_inc(carried, 1)
                    if active(n, SUM_LAG, end):
                        m = n - SUM_LAG
                        hh, th, a, c0 = PLAN[m % NS]
                        pe.wait_ge(sp_split, i * BODY + (m + 1))
                        pe.matmul(sum_bank(hh, c0), later_r, sp_hi[:, m % 3, c0:512], start=a == 4 * th + 3, stop=False,
                                  skip_group_check=True)
                        pe.matmul(sum_bank(hh, c0), later_r, sp_lo[:, m % 3, c0:512], start=False, stop=True,
                                  skip_group_check=True).then_inc(later_ready, 1)
                    if active(n, PV_LAG, end):
                        m = n - PV_LAG
                        pr, (hh, th, a, c0) = m // NS, PLAN[m % NS]
                        first = a == 4 * th + 3
                        if first and m >= 2:
                            pe.wait_ge(y_copied, i * 8 + (4 * pr + 2 * th + hh - 1))
                        pe.wait_ge(w_split, i * BODY + (m + 1))
                        o = out_bank(hh, c0)
                        pe.matmul(o, sv[:, pr % 2, a, hh, :], stick_hi[:, m % 2, c0:512], start=first, stop=False,
                                  skip_group_check=True)
                        pe.matmul(o, sv[:, pr % 2, a, hh, :], stick_lo[:, m % 2, c0:512], start=False, stop=a == 0,
                                  skip_group_check=True).then_inc(pv_done, 1)
                    if active(n, 0, end) and n % NS == TURN_V:
                        turn_values(i, n // NS)
                    if active(n, 0, end) and n % NS == SPLIT_V + 1:
                        pe.wait_ge(v_split, i * 2 + (n // NS + 1))
                    if (not end or n < NS) and n % NS in BETWEEN:
                        project(i, n // NS + 1, *BETWEEN[n % NS])

            project(0, 0, 0, 0, KB)
            project(0, 0, 1, 0, KB, sums=dense[:, 1, :])
            project(0, 0, 2, 0, KB)
            stick_steps(0, 0, LEAD)
            with pe.Fori(0, SB_H // 4 - 1) as i:
                stick_steps(i, LEAD, BODY + LEAD)
            stick_steps(SB_H // 4 - 1, LEAD, BODY + LEAD, end=True)
            meet(pe, "pe", met_n)

            for n in range(KB):
                if n == 0:
                    two_tiles(T_OUT2, U_OUT2, parts["y2"][1], lag=4)
                elif n >= 2:
                    tile(T_OUT2 + n, U_OUT2 + n)
                    residual_sum(n - 2, U_OUT2)
            for k in (KB - 2, KB - 1):
                residual_sum(k, U_OUT2)
            rms(S)
            group = feed(T_FF2, U_FF2, FG, parts["hidden2"][1], FG, (FF2_TILES, FF2_USES), parts["x3"][1], 0)
            repeat(pe, FF2_GROUPS - 1, group)
            u_last = U_FF2 + (FF2_GROUPS - 1) * FF2_USES + FG
            group(FF2_GROUPS - 1, behind=lambda k: residual_sum(k, u_last))
            for k in (KB - 2, KB - 1):
                residual_sum(k, u_last)
            rms(S)
            meet(pe, "pe", met_n)

        @block.scalar
        def _(act):
            met_n, norm_n = [0], {"used": 0, "own": 0, "scaled": 0}

            def rms_squares(src, width, ready, dst=None):
                for k in range(KB):
                    ready(k)
                    if dst is not None:
                        act.activation(dst[:, k, :], src(k), ACT.Square).then_inc(squares, 1)
                        continue
                    if k >= 2:
                        act.wait_ge(squares_used, norm_n["used"] + k - 1)
                    act.activation(T[:, k % 2, 0:width], src(k), ACT.Square).then_inc(squares, 1)
                norm_n["used"] += KB - 1

            def root(blocks, eps):
                norm_n["own"] += 1
                act.wait_ge(own_ready, norm_n["own"])
                act.activation(std[:, 0:blocks], own_sum[:, 0:blocks], ACT.Sqrt, bias=eps, scale=1.0 / D).then_inc(std_ready, 1)

            def round_scaled(dst, src, which, shift=None):
                for k in range(KB):
                    act.wait_ge(scaled, norm_n["scaled"] + k + 1)
                    if shift is not None:
                        act.activation(x_res[:, k, :], src(k), ACT.Identity, bias=par(shift, k)).then_inc(shifted, 1)
                        act.drain()
                        if dst is None:
                            act.dma_start(out[:, k, :], x_res[:, k, :]).then_inc(out_stored, 16)
                        else:
                            act.activation(dst[:, k, :], x_res[:, k, :], ACT.Copy).then_inc(parts[which][0], 1)
                    else:
                        act.activation(dst[:, k, :], src(k), ACT.Copy).then_inc(parts[which][0], 1)
                norm_n["scaled"] += KB

            act.wait_ge(consts_in, CONSTS)
            rms_squares(lambda k: x_in[:, k, :], S, lambda k: act.wait_ge(x_loaded[k // 2], 16))
            root(TB, EPS_RMS)
            round_scaled(a_hi, lambda k: x_in[:, k, :], "h")
            rms_squares(lambda k: m_in[:, k, :], MEM, lambda k: act.wait_ge(mem_loaded, 16), mem_squares)

            for t in range(T_KI, T_MEM):
                act.wait_ge(tile_done, t + 1)
                if t >= 2:
                    act.wait_ge(roped, t - 1)
                act.activation(T[:, t % 2, :], dense[:, t % 2, :], ACT.Copy).then_inc(sums_free[t % 2], 1)
                if t == 1:
                    root(MEM // P, EPS_RMS)
                    round_scaled(m_hi, lambda k: m_in[:, k, :], "mem")
            meet(act, "act", met_n)

            def memory_copy(t, u, n, qc):
                act.wait_ge(tile_done, t + 1)
                dst, width = (km_f[:, n, :], MEM) if n < 2 else (vm_t[:, n - 2, :], MEM) if n < 4 else (qc[:, n - 4, :], S)
                act.activation(dst, dense[:, u % 2, 0:width], ACT.Copy).then_inc(sums_free[u % 2], 1)

            act.activation(ki_hi[:, :], ki_f[:, :], ACT.Copy).then_inc(idx_round, 1)
            for t in range(2):
                act.activation(qi_hi[:, t, :], qi_f[:, t, TOPK:S], ACT.Copy).then_inc(idx_round, 1)
            for n in range(IDX_H + 1):
                act.wait_ge(stacked, n + 1)
                act.activation(ki_stack[0:STACK, :] if n == 0 else qi_stack[0:STACK, n - 1, :],
                               side[0:STACK, n % 2, 0:S if n == 0 else IDX_S], ACT.Copy).then_inc(stack_copied, 1)
            for n in range(IDX_STEPS):
                i = TOPK // P + n // IDX_H
                act.wait_ge(idx_ready, n + 1)
                if n >= 2:
                    act.wait_ge(rel_used, n - 1)
                act.activation(T[:, n % 2, 0:P * (i + 1)], side[:, n % 2, 0:P * (i + 1)], ACT.Relu).then_inc(rel_ready, 1)
                if n and n % KB == 0:
                    memory_copy(T_MEM + n // KB - 1, T_MEM + n // KB - 1, n // KB - 1, qc_f)
            memory_copy(T_MEM + 5, T_MEM + 5, 5, qc_f)

            def memory(yf, y0, n0):
                meet(act, "act", met_n)
                for n in range(TB + 2):
                    if n < TB:
                        act.wait_ge(lg_max, n0 + n + 1)
                        if n >= 2:
                            act.wait_ge(lg_t, n0 + n - 1)
                        for q in range(4):
                            e = 4 * (n % 2) + q
                            last = act.activation(T[:, n % 2, q * MEM:q * MEM + MEM], side[:, n % 2, q * MEM:q * MEM + MEM],
                                                  ACT.Exp, bias=neg_max[:, e:e + 1], scale=SCALE,
                                                  accum_out=row_sum[:, e:e + 1])
                        last.then_inc(lg_exp, 1)
                    if 1 <= n <= TB:
                        copy_turned(n - 1, n0, S)
                    if n >= 2:
                        b = n - 2
                        act.wait_ge(lg_o, n0 + b + 1)
                        heads = dense[:, b % 2, 0:512].rearrange("p (j e q) -> p j e q", j=2, e=2)
                        for e in range(2):
                            r = slice(HD * e, HD * e + HD)
                            last = act.activation(yf[r, y0:y0 + 2, b * P:b * P + P], heads[r, :, e, :], ACT.Copy)
                        last.then_inc(lg_oc, 1)

            def copy_turned(n, n0, width):
                act.wait_ge(lg_t, n0 + n + 1)
                if n >= 2:
                    act.wait_ge(lg_o, n0 + n - 1)
                act.activation(T[:, 2 + n % 2, 0:width], dense[:, n % 2, 0:width], ACT.Copy).then_inc(lg_tc, 1)

            memory(ym_f, 0, 0)
            act.drain()
            for k in range(2):
                act.activation(ym_hi[:, k, :], ym_f[:, k, :], ACT.Copy).then_inc(parts["ym"][0], 1)
            meet(act, "act", met_n)

            for j in range(3):
                t = T_CONV + 3 * j
                act.wait_ge(tile_done, t + 1)
                if j:
                    act.wait_ge(conv_used, j)
                act.activation(T[:, 0, :], dense[:, t % 2, :], ACT.Copy).then_inc(sums_free[t % 2], 1)
                act.wait_ge(yc_ready, j + 1)
                act.activation(yc_hi[:, j, :], T[:, 2, :], ACT.Copy).then_inc(parts["yc"][0], 1)

            def gate_blocks(i):
                first = isinstance(i, int)
                for j in range(2):
                    t = T_GATE + 4 * j
                    for c in range(3):
                        b = SMALL["b_gate"] + 3 * j + c
                        act.activation(bias_now[:, :], small[:, b:b + 1] if first else small[:, bass.ds(i * 6 + b, 1)], ACT.Copy)
                        act.drain()
                        act.wait_ge(tile_done, i * 8 + (t + c + 1))
                        dst = T[:, j, :] if c == 0 else gates[:, 2 * j + c - 1, :]
                        if not first and c == 0:
                            act.wait_ge(gate_spilled[j], i * 16)
                        if not first and c == 1:
                            act.wait_ge(part_spilled[j], i * 16)
                        act.activation(dst, dense[:, (t + c) % 2, :], ACT.Sigmoid, bias=bias_now[:, :]
                                       ).then_inc(sums_free[(t + c) % 2], 1)
                        act.drain()
                        if c == 0:
                            act.dma_start(spill_gate[bass.ds(i * 2 + j, 1)].rearrange("a p s -> p (a s)")
                                          if not first else spill_gate[j], T[:, j, :]).then_inc(gate_spilled[j], 16)
                    act.wait_ge(part_ready, i * 2 + (j + 1))
                    act.dma_start(spill_part[bass.ds(i * 2 + j, 1)].rearrange("a p s -> p (a s)")
                                  if not first else spill_part[j], gates[:, 2 * j, :]).then_inc(part_spilled[j], 16)

            repeat(act, 4, gate_blocks)
            for j in range(2):
                act.wait_ge(gate_spilled[j], 64)
                act.wait_ge(part_spilled[j], 64)
            meet(act, "act", met_n)

            def fetch(j):
                act.dma_start(back[:, 2 * (j % 2), :], spill_gate[j]).then_inc(fetched[j % 2], 16)
                act.dma_start(back[:, 2 * (j % 2) + 1, :], spill_part[j]).then_inc(fetched[j % 2], 16)

            fetch(0)
            fetch(1)
            act.dma_start(m_in[:, :, :], io["mem2_t"]).then_inc(mem2_loaded, 16)
            for n in range(DSA_STEPS + 2):
                if n < DSA_STEPS:
                    w, e = P * (DSA_PLAN[n][0] + 1), n % 8
                    act.wait_ge(lg_max, TB + n + 1)
                    act.activation(T[:, n % 2, 0:w], T[:, n % 2, 0:w], ACT.Exp, bias=neg_max[:, e:e + 1], scale=SCALE,
                                   accum_out=row_sum[:, e:e + 1]).then_inc(lg_exp, 1)
                if 1 <= n <= DSA_STEPS:
                    copy_turned(n - 1, TB, P * (DSA_PLAN[n - 1][0] + 1))
                if n >= 2:
                    i, h = DSA_PLAN[n - 2]
                    r = slice(HD * (h // 3), HD * (h // 3) + HD)
                    act.wait_ge(lg_o, TB + n - 1)
                    act.activation(ya_f[r, h % 3, i * P:i * P + P], dense[r, n % 2, 0:P], ACT.Copy).then_inc(lg_oc, 1)
                    if h == ATT_H - 1:
                        act.wait_ge(lg_oc, TB + n - 1)
                        act.activation(ya_hi[:, :, i * P:i * P + P], ya_f[:, :, i * P:i * P + P], ACT.Copy
                                       ).then_inc(parts["ya"][0], 1)
            meet(act, "act", met_n)


            for j in range(KB):
                act.wait_ge(merged_sum, j + 1)
                if j + 2 < KB:
                    fetch(j + 2)
                act.activation(a_hi[:, j, :], T[:, j % 2, :], ACT.Copy).then_inc(parts["merged"][0], 1)
                if j in (KB // 2 - 2, KB - 2):
                    half = slice(0, KB // 2) if j < KB // 2 else slice(KB // 2, KB)
                    act.dma_start(x_res[:, half, :], io["x_t"][:, half, :]).then_inc(x_back, 16)

            rms_squares(lambda k: x_res[:, k, :], S, lambda k: emptied(act, T_WO + k))
            root(TB, EPS_RMS)
            round_scaled(a_hi, lambda k: T[:, (0, 1, 3)[k % 3], :], "h2")
            act.wait_ge(mem2_loaded, 16)
            act.activation(m_hi[:, :, :], m_in[:, :, :], ACT.Copy).then_inc(parts["mem2"][0], 1)

            def gated(i, t0, n_f, f0, per):
                cols = SMALL["taps_ff"] + 6 * f0
                act.drain()
                act.activation(taps_act[:, 0:6 * n_f], small[:, bass.ds(i * (6 * FG) + cols, 6 * n_f)]
                               if not isinstance(i, int) else small[:, cols:cols + 6 * n_f], ACT.Copy)
                act.drain()
                for f in range(n_f):
                    for c in range(2):
                        t = t0 + 2 * f + c
                        u = gu[0] + 2 * f + c
                        act.wait_ge(tile_done, i * per + (t + 1))
                        slot = 2 * (f % 2) + c
                        if f >= 2 or not isinstance(i, int) or f0:
                            act.wait_ge(parts["hidden"][1] if c == 0 else product_ready, i * FG + (f0 + f - 1))
                        act.activation(T[:, slot, :], dense[:, u % 2, :], ACT.Copy,
                                       scale=taps_act[:, 6 * f + 3 * c + 2:6 * f + 3 * c + 3]).then_inc(tap_ready, 1)
                    act.wait_ge(taps_done, i * (2 * FG) + (2 * (f0 + f) + 1))
                    act.activation(T[:, 2 * (f % 2), :], T[:, 2 * (f % 2), :], ACT.Silu).then_inc(acted, 1)
                    act.wait_ge(product_ready, i * FG + (f0 + f + 1))
                    act.activation(b_hi[:, f, :], T[:, 2 * (f % 2), :], ACT.Copy).then_inc(parts["hidden"][0], 1)

            gu = [T_FF]
            repeat(act, FULL, lambda i: gated(i, T_FF, FG, 0, FF_TILES))
            for n in range(5):
                if n < 4:
                    t = T_KV2 + n
                    act.wait_ge(tile_done, t - 1)
                    act.wait_ge(weights_split, t)
                    act.wait_ge(weights_loaded[t % RAW], 16 * (t // RAW) + 16)
                    act.activation(w_hi[:, t % 2, :], raw[:, t % RAW, :], ACT.Copy).then_inc(weights_rounded, 1)
                if n:
                    memory_copy(T_KV2 + n - 1, U_KV2 + n - 1, n - 1, None)
            gu[0] = U_REST
            gated(0, T_REST, REST, FULL * FG, 0)
            rms_squares(lambda k: x_res[:, k, :], S, lambda k: emptied(act, U_REST + 2 * REST + k))
            root(TB, EPS_RMS)
            round_scaled(a_hi, lambda k: x_res[:, k, :], "x2")

            for n in range(2):
                memory_copy(T_MEM2 + n, U_MEM2 + n, 4 + n, qc2_f)
            act.wait_ge(parts["x2"][1], KB)
            act.dma_start(spill_x, x_res[:, :, :]).then_inc(x_spilled, 16)
            memory(y2_f, 6, TB + DSA_STEPS)
            act.wait_ge(x_spilled, 16)
            meet(act, "act", met_n)

            def take(i, p, c, sums=dense[:, 0, :]):
                act.wait_ge(tile_done, i * 6 + (T_SB + 3 * p + c + 1))
                if c == 0:
                    act.activation(sq_hi[:, p % 2, :], sums, ACT.Copy, scale=SCALE).then_inc(qk_rounded, 1)
                elif c == 1:
                    act.activation(sk_hi[:, p % 2, :], sums, ACT.Copy).then_inc(qk_rounded, 1)
                else:
                    act.activation(sv_t[:, :], sums, ACT.Copy).then_inc(v_copied, 1)

            def round_tile(t, i):
                act.wait_ge(weights_loaded[t % RAW], i * (6 // RAW * 16) + 16 * (t // RAW + 1))
                act.wait_ge(weights_split, i * 6 + t)
                act.wait_ge(tile_done, i * 6 + (t - 1))
                act.activation(w_hi[:, t % 2, :], raw[:, t % RAW, :], ACT.Copy).then_inc(weights_rounded, 1)

            def stick_steps(i, begin, stop, end=False):
                for n in range(begin, stop):
                    e = n - PV_LAG - 1
                    if active(n, PV_LAG + 1, end) and group_end(e) is not None:
                        act.wait_ge(pv_done, i * BODY + (e + 1))
                        hh = group_end(e) % 2
                        act.activation(out_low[:, hh, :], out_bank(hh)[HD:P, :], ACT.Copy).then_inc(low_ready, 1)
                    if active(n, 0, end):
                        act.wait_ge(z_ready, i * BODY + (n + 1))
                        act.activation(sp_strip(n), z_bank(n, PLAN[n % NS][3]), ACT.Exp).then_inc(e_ready, 1)
                    if active(n, 1, end):
                        m = n - 1
                        act.wait_ge(e_clip, i * BODY + (m + 1))
                        act.activation(sp_strip(m), sp_strip(m), ACT.Ln, bias=1.0).then_inc(ln_ready, 1)
                    if active(n, 0, end):
                        if n >= 6:
                            act.wait_ge(w_split, i * BODY + (n - 5))
                        act.activation(z_strip(n), z_bank(n, PLAN[n % NS][3]), ACT.Copy).then_inc(z_copied, 1)
                    if active(n, SUM_LAG, end):
                        m = n - SUM_LAG
                        act.wait_ge(arg_ready, i * BODY + (m + 1))
                        act.activation(z_strip(m), z_strip(m), ACT.Exp).then_inc(w_ready, 1)
                    if (not end or n < NS) and n % NS in (COPY_Q, COPY_K):
                        take(i, n // NS + 1, (COPY_Q, COPY_K).index(n % NS))
                    if active(n, 0, end) and n % NS == COPY_V:
                        if n:
                            act.wait_ge(y_copied, i * 8 + (4 * (n // NS) - 2))
                        take(i, n // NS, 2)
                    if active(n, 0, end) and n % NS in SPLIT_STEPS and not (end and n >= NS and n % NS != SPLIT_STEPS[0]):
                        round_tile(T_SB + 3 * (n // NS + 1) + SPLIT_STEPS.index(n % NS) + 1, i)

            for c in range(2):
                take(0, 0, c, sums=dense[:, c, :])
            act.preload_act_table_set("natural_log_exp_and_others")
            stick_steps(0, 0, LEAD)
            with act.Fori(0, SB_H // 4 - 1) as i:
                stick_steps(i, LEAD, BODY + LEAD)
            stick_steps(SB_H // 4 - 1, LEAD, BODY + SUM_LAG, end=True)
            act.wait_ge(y_copied, 4 * EARLY)
            for k in range(EARLY):
                act.activation(a_hi[:, k, :], y2_f[:, k, :], ACT.Copy).then_inc(parts["y2"][0], 1)
            stick_steps(SB_H // 4 - 1, BODY + SUM_LAG, BODY + LEAD, end=True)
            meet(act, "act", met_n)
            act.dma_start(x_res[:, 0:2, :], spill_x[:, 0:2, :]).then_inc(x_returned[0], 16)
            act.dma_start(x_res[:, 2:KB, :], spill_x[:, 2:KB, :]).then_inc(x_returned[1], 16)

            for k in range(EARLY, KB):
                act.activation(a_hi[:, k, :], y2_f[:, k, :], ACT.Copy).then_inc(parts["y2"][0], 1)

            def layer_norm(dst, which, shift):
                for k in range(KB):
                    act.wait_ge(centred, cen[0] + k + 1)
                    if k >= 2:
                        act.wait_ge(squares_used, norm_n["used"] + k - 1)
                    act.activation(T[:, k % 2, :], x_res[:, k, :], ACT.Square).then_inc(squares, 1)
                cen[0] += KB
                norm_n["used"] += KB - 1
                root(TB, EPS_LN)
                round_scaled(dst, lambda k: T[:, (0, 1, 3)[k % 3], :], which, shift)

            cen = [0]
            layer_norm(a_hi, "x3", "ln1_b")

            def squared_relu(i):
                for f in range(FG):
                    act.wait_ge(squared, i * FG + (f + 1))
                    act.activation(b_hi[:, f, :], T[:, f, :], ACT.Copy).then_inc(parts["hidden2"][0], 1)

            repeat(act, FF2_GROUPS, squared_relu)
            layer_norm(None, None, "ln2_b")
            act.wait_ge(out_stored, KB * 16)
            meet(act, "act", met_n)

        @block.vector
        def _(dve):
            met_n, norm_n = [0], {"sum": 0, "std": 0, "shift": 0}

            def inverse_std(blocks):
                norm_n["std"] += 1
                norm_n["sum"] += 1
                dve.wait_ge(sum_ready, norm_n["sum"])
                for b in range(blocks):
                    t = slice(b * P, b * P + P)
                    last = dve.tensor_tensor_reduce(out=T[:, 2, t], in0=side[:, 0, t], in1=ident[:, :], scale=1.0, scalar=0.0,
                                                    op0=ALU.mult, op1=ALU.add, accum_out=own_sum[:, b:b + 1])
                last.then_inc(own_ready, 1)
                dve.wait_ge(std_ready, norm_n["std"])
                dve.reciprocal(rstd[:, 0:blocks], std[:, 0:blocks])
                dve.drain()
                for b in range(blocks):
                    last = dve.tensor_scalar(T[:, 2, b * P:b * P + P], ident[:, :], rstd[:, b:b + 1], None, ALU.mult)
                last.then_inc(diag_ready, 1)
                dve.wait_ge(spread_ready, norm_n["std"])

            def low(dst, k, src, which, n):
                dve.wait_ge(parts[which][0], n)
                dve.tensor_tensor(dst[1], src, dst[0].bitcast(F32), ALU.subtract).then_inc(parts[which][1], 1)

            def scale_all(src, dst, gain, which, hi, lo, width, ring=0, lag=1):
                for k in range(KB + lag):
                    if k < KB:
                        if ring and k >= ring:
                            dve.wait_ge(parts[which][1], k - ring + 1)
                        dve.scalar_tensor_tensor(dst(k), src(k), par(gain, k), side[:, 1, 0:width], ALU.mult, ALU.mult
                                                 ).then_inc(scaled, 1)
                    if k >= lag and which is not None:
                        m = k - lag
                        low((hi[:, m, :], lo[:, m, :]), m, dst(m), which, m + 1)

            dve.wait_ge(consts_in, CONSTS)
            for c in range(4):
                dve.wait_ge(x_loaded[c], 16)
            inverse_std(TB)
            scale_all(lambda k: x_in[:, k, :], lambda k: x_in[:, k, :], "g_mix", "h", a_hi, a_lo, S)
            dve.wait_ge(mem_loaded, 16)
            inverse_std(MEM // P)
            scale_all(lambda k: m_in[:, k, :], lambda k: m_in[:, k, :], "g_mem", "mem", m_hi, m_lo, MEM)
            dve.wait_ge(tables_in, TABLES)

            def rotate(t, tab, dst, n_turned, v):
                dve.wait_ge(turned, n_turned)
                dve.tensor_tensor(T[:, 2 + t % 2, :], side[:, v % 2, :], rope_tab[:, tab + 1, :], ALU.mult
                                  ).then_inc(turn_free[v % 2], 1)
                dve.tensor_tensor(T[:, t % 2, :], T[:, t % 2, :], rope_tab[:, tab, :], ALU.mult)
                dve.drain()
                dve.tensor_tensor(dst, T[:, t % 2, :], T[:, 2 + t % 2, :], ALU.add).then_inc(roped, 1)

            dve.wait_ge(turned, 1)
            dve.tensor_tensor(T[:, 3, :], side[:, 0, :], rope_tab[:, 0, :], ALU.mult).then_inc(turn_free[0], 1)
            dve.wait_ge(turned, 2)
            dve.tensor_tensor(T[:, 2, :], side[:, 1, :], rope_tab[:, 1, :], ALU.mult).then_inc(turn_free[1], 1)
            dve.drain()
            dve.tensor_tensor(ki_f[:, :], T[:, 2, :], T[:, 3, :], ALU.add)
            dve.wait_ge(turned, 3)
            dve.tensor_copy(tiny[:, 160:160 + TB * IDX_H], side[:, 0, 0:TB * IDX_H]).then_inc(turn_free[0], 1)
            dve.drain().then_inc(roped, 1)
            for t in range(1, T_V):
                dst = qi_f[:, t - 1, :] if t < T_K else k_f[:, :] if t == T_K else q_f[:, t - T_Q, :]
                rotate(t, 0 if t < T_K else 2, dst, t + 3, t + 2)
            dve.tensor_copy(stack_mats[:, :, :], stack_in[:, :].rearrange("p (m c) -> p m c", m=4))
            dve.wait_ge(turned, 10)
            dve.tensor_copy(v_f[:, :, :], side[:, 1, :].rearrange("p (b d) -> p b d", d=P)).then_inc(turn_free[1], 1)
            meet(dve, "dve", met_n)

            dve.wait_ge(idx_round, 1)
            dve.tensor_tensor(ki_lo[:, :], ki_f[:, :], ki_hi[:, :].bitcast(F32), ALU.subtract).then_inc(idx_split, 1)
            for t in range(2):
                dve.wait_ge(idx_round, t + 2)
                dve.tensor_tensor(qi_lo[:, t, :], qi_f[:, t, TOPK:S], qi_hi[:, t, :].bitcast(F32), ALU.subtract
                                  ).then_inc(idx_split, 1)
            dve.memset(score[:, 0:score_at(2)], 0.0)
            for n in range(IDX_STEPS):
                i, h = TOPK // P + n // IDX_H, n % IDX_H
                w = P * (i + 1)
                sc = score[:, score_at(i):score_at(i) + w]
                dve.wait_ge(rel_ready, n + 1)
                if h == 0:
                    dve.tensor_scalar(sc, T[:, n % 2, 0:w], wi_f[:, i, h:h + 1], None, ALU.mult).then_inc(rel_used, 1)
                else:
                    dve.drain()
                    dve.scalar_tensor_tensor(sc, T[:, n % 2, 0:w], wi_f[:, i, h:h + 1], sc, ALU.mult, ALU.add
                                             ).then_inc(rel_used, 1)
            dve.drain()
            for i in range(TB):
                e = score_at(i + 1)
                dve.tensor_tensor(score[:, e - P:e], score[:, e - P:e], mats["causal_q"][:, :], ALU.add)
            dve.drain()

            def topk_round():
                for i in range(TOPK // P, TB):
                    dve.max(best[:, i - TOPK // P, :], score[:, score_at(i):score_at(i + 1)])
                dve.drain()
                for i in range(TOPK // P, TB):
                    sc = score[:, score_at(i):score_at(i + 1)]
                    dve.match_replace(sc, best[:, i - TOPK // P, :], sc, TAKEN)
                dve.drain()

            def memory(n0, layer):
                dve.wait_ge(mturned, layer + 1)
                dve.tensor_copy(vm_f[:, :, :], side[:, 0, 0:512].rearrange("p (m d) -> p m d", m=2))
                meet(dve, "dve", met_n)
                for n in range(TB):
                    e = 4 * (n % 2)
                    dve.wait_ge(lg_ready, n0 + n + 1)
                    dve.tensor_reduce(row_max[:, e:e + 4], side[:, n % 2, :].rearrange("p (q m) -> p q m", q=4), AX.X,
                                      ALU.max)
                    dve.drain()
                    dve.tensor_scalar(neg_max[:, e:e + 4], row_max[:, e:e + 4], -SCALE, None, ALU.mult
                                      ).then_inc(lg_max, 1)
                    dve.wait_ge(lg_exp, n0 + n + 1)
                    dve.reciprocal(inv_sum[:, e:e + 4], row_sum[:, e:e + 4])
                    dve.drain()
                    for q in range(4):
                        pq = T[:, n % 2, q * MEM:q * MEM + MEM]
                        last = dve.tensor_scalar(pq, pq, inv_sum[:, e + q:e + q + 1], None, ALU.mult)
                    last.then_inc(lg_p, 1)

            memory(0, 0)
            for k in range(2):
                low((ym_hi[:, k, :], ym_lo[:, k, :]), k, ym_f[:, k, :], "ym", k + 1)
            meet(dve, "dve", met_n)

            for j in range(3):
                t = T_CONV + 3 * j
                with dve.Fori(0, 3 if j == 2 else 2):
                    topk_round()
                emptied(dve, t)
                dve.wait_ge(tile_done, t + 2)
                dve.tensor_tensor(T[:, 1, :], dense[:, (t + 1) % 2, :], T[:, 0, :], ALU.mult
                                  ).then_inc(sums_free[(t + 1) % 2], 1)
                dve.drain().then_inc(conv_used, 1)
                dve.tensor_scalar(T[:, 2, :], T[:, 1, :], par("taps_short", 3 * j + 2), None, ALU.mult)
                for d in (1, 2):
                    dve.drain()
                    dve.scalar_tensor_tensor(T[:, 2, d:S], T[:, 1, 0:S - d], par("taps_short", 3 * j + 2 - d), T[:, 2, d:S],
                                             ALU.mult, ALU.add)
                dve.drain()
                dve.wait_ge(tile_done, t + 3)
                dve.tensor_tensor(T[:, 2, :], dense[:, (t + 2) % 2, :], T[:, 2, :], ALU.mult
                                  ).then_inc(sums_free[(t + 2) % 2], 1)
                dve.drain().then_inc(yc_ready, 1)
                low((yc_hi[:, j, :], yc_lo[:, j, :]), j, T[:, 2, :], "yc", j + 1)

            def gate_blocks(i):
                for j in range(2):
                    t = T_GATE + 4 * j
                    for _ in range(4 if isinstance(i, int) and j else 3):
                        topk_round()
                    g1, g2 = gates[:, 2 * j, :], gates[:, 2 * j + 1, :]
                    dve.wait_ge(sums_free[(t + 2) % 2], i * 4 + ((t + 2) // 2 + 1))
                    dve.wait_ge(sums_free[(t + 1) % 2], i * 4 + ((t + 1) // 2 + 1))
                    dve.wait_ge(first_done, i * 2 + (j + 1))
                    dve.tensor_tensor(g1, dense[:, (t + 3) % 2, :], g1, ALU.mult).then_inc(sums_free[(t + 3) % 2], 1)
                    dve.wait_ge(tile_done, i * 8 + (t + 4))
                    dve.tensor_tensor(g2, side[:, j, :], g2, ALU.mult).then_inc(branch_free[j], 1)
                    dve.drain()
                    dve.tensor_tensor(g1, g1, g2, ALU.add).then_inc(part_ready, 1)

            repeat(dve, 4, gate_blocks)
            sc = score[:, score_at(2):score_at(TB)]
            dve.tensor_scalar(sc, sc, TAKEN / 2, NEG, ALU.is_gt, ALU.mult)
            meet(dve, "dve", met_n)

            for n in range(DSA_STEPS):
                i, e = DSA_PLAN[n][0], n % 8
                w = P * (i + 1)
                dve.wait_ge(lg_ready, TB + n + 1)
                if n >= 2:
                    dve.wait_ge(lg_t, TB + n - 1)
                dve.tensor_tensor_reduce(out=T[:, n % 2, 0:w], in0=side[:, n % 2, 0:w],
                                         in1=score[:, score_at(i):score_at(i) + w], scale=1.0, scalar=TAKEN, op0=ALU.add,
                                         op1=ALU.max, accum_out=row_max[:, e:e + 1])
                dve.drain()
                dve.tensor_scalar(neg_max[:, e:e + 1], row_max[:, e:e + 1], -SCALE, None, ALU.mult).then_inc(lg_max, 1)
                dve.wait_ge(lg_exp, TB + n + 1)
                dve.reciprocal(inv_sum[:, e:e + 1], row_sum[:, e:e + 1])
                dve.drain()
                dve.tensor_scalar(T[:, n % 2, 0:w], T[:, n % 2, 0:w], inv_sum[:, e:e + 1], None, ALU.mult
                                  ).then_inc(lg_p, 1)
            meet(dve, "dve", met_n)

            for j in range(KB + 1):
                if j < KB:
                    t, m = T_ATT + j // 2, j // 2
                    src = dense[:, t % 2, :] if j % 2 == 0 else side[:, m % 2, :]
                    if j >= 2:
                        dve.wait_ge(parts["merged"][1], j - 1)
                    dve.wait_ge(fetched[j % 2], 32 * (j // 2 + 1))
                    if j % 2 == 0:
                        dve.wait_ge(first_done, 8 + m + 1)
                    else:
                        dve.wait_ge(tile_done, t + 1)
                    dve.tensor_tensor(T[:, j % 2, :], src, back[:, 2 * (j % 2), :], ALU.mult
                                      ).then_inc(sums_free[t % 2] if j % 2 == 0 else att_free[m % 2], 1)
                    dve.drain()
                    dve.tensor_tensor(T[:, j % 2, :], T[:, j % 2, :], back[:, 2 * (j % 2) + 1, :], ALU.add
                                      ).then_inc(merged_sum, 1)
                if j:
                    low((a_hi[:, j - 1, :], a_lo[:, j - 1, :]), j - 1, T[:, (j - 1) % 2, :], "merged", j)
            for n in range(KB):
                u = T_WO + n
                if n % (KB // 2) == 0:
                    dve.wait_ge(x_back, 32 if n else 16)
                dve.wait_ge(tile_done, T_WO + n + 1)
                dve.tensor_tensor(x_res[:, n, :], x_res[:, n, :], dense[:, u % 2, :], ALU.add
                                  ).then_inc(sums_free[u % 2], 1)

            def third(k):
                return T[:, (0, 1, 3)[k % 3], :]

            inverse_std(TB)
            scale_all(lambda k: x_res[:, k, :], third, "g_ffn", "h2", a_hi, a_lo, S, ring=3)
            dve.wait_ge(parts["mem2"][0], 1)
            for k in range(KB):
                dve.tensor_tensor(m_lo[:, k, :], m_in[:, k, :], m_hi[:, k, :].bitcast(F32), ALU.subtract
                                  ).then_inc(parts["mem2"][1], 1)

            def down(i, t0, u0, per, n0):
                for n in range(KB):
                    u = u0 + n
                    if n % 2 == 0:
                        dve.wait_ge(first_done, i * (KB // 2) + (n0 + n // 2 + 1))
                    else:
                        dve.wait_ge(tile_done, i * per + (t0 + n // 2 + 1))
                    dve.tensor_tensor(x_res[:, n, :], x_res[:, n, :], dense[:, u % 2, :], ALU.add
                                      ).then_inc(sums_free[u % 2], 1)

            def gated(i, t0, u0, n_f, f0, per, n0):
                cols = SMALL["taps_ff"] + 6 * f0
                dve.drain()
                dve.tensor_copy(taps_dve[:, 0:6 * n_f], small[:, bass.ds(i * (6 * FG) + cols, 6 * n_f)]
                                if not isinstance(i, int) else small[:, cols:cols + 6 * n_f])
                dve.drain()
                for f in range(n_f):
                    for c in range(2):
                        u, slot = u0 + 2 * f + c, 2 * (f % 2) + c
                        dve.wait_ge(tap_ready, i * (2 * FG) + (2 * (f0 + f) + c + 1))
                        for d in (1, 2):
                            tap = taps_dve[:, 6 * f + 3 * c + 2 - d:6 * f + 3 * c + 3 - d]
                            last = dve.scalar_tensor_tensor(T[:, slot, d:S], dense[:, u % 2, 0:S - d], tap, T[:, slot, d:S],
                                                            ALU.mult, ALU.add)
                            if d == 1:
                                dve.drain()
                        last.then_inc(sums_free[u % 2], 1)
                        dve.drain().then_inc(taps_done, 1)
                    g, v = T[:, 2 * (f % 2), :], T[:, 2 * (f % 2) + 1, :]
                    dve.wait_ge(acted, i * FG + (f0 + f + 1))
                    dve.tensor_tensor(g, g, v, ALU.mult).then_inc(product_ready, 1)
                    dve.wait_ge(parts["hidden"][0], i * FG + (f0 + f + 1))
                    dve.tensor_tensor(b_lo[:, f, :], g, b_hi[:, f, :].bitcast(F32), ALU.subtract
                                      ).then_inc(parts["hidden"][1], 1)
                down(i, t0 + 2 * n_f, u0 + 2 * n_f, per, n0)

            repeat(dve, FULL, lambda i: gated(i, T_FF, T_FF, FG, 0, FF_TILES, 12))
            gated(0, T_REST, U_REST, REST, FULL * FG, 0, 12 + FULL * KB // 2)

            inverse_std(TB)
            scale_all(lambda k: x_res[:, k, :], lambda k: x_res[:, k, :], "g_final", "x2", a_hi, a_lo, S)
            memory(TB + DSA_STEPS, 1)
            meet(dve, "dve", met_n)

            for n, name in enumerate(("ident", "strict_add", "neg_later", "neg_earlier")):
                dve.tensor_copy(stick_mats[:, n, :], mats[name][:, :])
            dve.drain()

            def take_values(i, p, sums=dense[:, 0, :]):
                values = sums.rearrange("p (b e d) -> p b e d", b=TB, e=2)
                hi, lo = sv[:, p % 2, :, :, 0:HD], sv[:, p % 2, :, :, HD:P]
                dve.wait_ge(v_turned, i * 2 + (p + 1))
                dve.tensor_copy(hi, values).then_inc(v_rounded, 1)
                dve.wait_ge(v_rounded, i * 2 + (p + 1))
                dve.tensor_tensor(lo, values, hi.bitcast(F32), ALU.subtract).then_inc(v_split, 1)

            def take(i, p, c, sums=dense[:, 0, :]):
                dve.wait_ge(qk_rounded, i * 4 + (2 * p + c + 1))
                if c == 1:
                    dve.tensor_tensor(sk_lo[:, p % 2, :], sums, sk_hi[:, p % 2, :].bitcast(F32), ALU.subtract
                                      ).then_inc(qk_split, 1)
                else:
                    dve.scalar_tensor_tensor(sq_lo[:, p % 2, :], sums, SCALE, sq_hi[:, p % 2, :].bitcast(F32),
                                             ALU.mult, ALU.subtract).then_inc(qk_split, 1)

            def stick_steps(i, begin, stop, end=False):
                for n in range(begin, stop):
                    if active(n, 2, end):
                        m = n - 2
                        if m >= 3:
                            if PLAN[(m - 3) % NS][2] > 0:
                                dve.wait_ge(carried, i * CARRIES[BODY - 1] + CARRIES[m - 3])
                            else:
                                dve.wait_ge(later_ready, i * BODY + (m - 2))
                        dve.wait_ge(sp_ready, i * BODY + (m + 1))
                        dve.tensor_copy(sp_hi[:, m % 3, PLAN[m % NS][3]:512], sp_strip(m)).then_inc(sp_round, 1)
                    if active(n, SUM_LAG + 1, end):
                        w = n - SUM_LAG - 1
                        if w >= 2:
                            dve.wait_ge(pv_done, i * BODY + (w - 1))
                        dve.wait_ge(w_ready, i * BODY + (w + 1))
                        dve.tensor_copy(stick_hi[:, w % 2, PLAN[w % NS][3]:512], z_strip(w)).then_inc(w_round, 1)
                    if active(n, SUM_LAG, end):
                        m = n - SUM_LAG
                        hh, th, a, c0 = PLAN[m % NS]
                        dve.wait_ge(later_ready, i * BODY + (m + 1))
                        dve.tensor_tensor(z_strip(m), z_strip(m), sum_bank(hh, c0), ALU.add).then_inc(arg_ready, 1)
                    e = n - PV_LAG - 1
                    if active(n, PV_LAG + 1, end) and group_end(e) is not None:
                        pr, th, hh = group_end(e) // 4, group_end(e) // 2 % 2, group_end(e) % 2
                        r, tk = slice(HD * hh, HD * hh + HD), slice(512 * th, 512 * th + 512)
                        dst = (y2_f[r, bass.ds(i * 2 + pr, 1), tk].rearrange("p a s -> p (a s)") if not isinstance(i, int)
                               else y2_f[r, 2 * i + pr, tk])
                        dve.wait_ge(low_ready, i * 8 + (group_end(e) + 1))
                        dve.tensor_tensor(dst, out_bank(hh)[0:HD, :], out_low[:, hh, :], ALU.add).then_inc(y_copied, 1)
                    if active(n, 0, end):
                        dve.wait_ge(e_ready, i * BODY + (n + 1))
                        dve.tensor_scalar(sp_strip(n), sp_strip(n), BIG_E, None, ALU.min).then_inc(e_clip, 1)
                    if active(n, 1, end):
                        m = n - 1
                        dve.wait_ge(z_copied, i * BODY + (m + 1))
                        dve.wait_ge(ln_ready, i * BODY + (m + 1))
                        dve.tensor_tensor(sp_strip(m), sp_strip(m), z_strip(m), ALU.max).then_inc(sp_ready, 1)
                    if active(n, 0, end) and n % NS == SPLIT_V:
                        take_values(i, n // NS)
                    if (not end or n < NS) and n % NS in (COPY_Q, COPY_K):
                        take(i, n // NS + 1, (COPY_Q, COPY_K).index(n % NS))

            for c in range(2):
                take(0, 0, c, sums=dense[:, c, :])
            stick_steps(0, 0, LEAD)
            with dve.Fori(0, SB_H // 4 - 1) as i:
                stick_steps(i, LEAD, BODY + LEAD)
            stick_steps(SB_H // 4 - 1, LEAD, BODY + PV_LAG, end=True)
            for k in range(EARLY):
                low((a_hi[:, k, :], a_lo[:, k, :]), k, y2_f[:, k, :], "y2", k + 1)
            stick_steps(SB_H // 4 - 1, BODY + PV_LAG, BODY + LEAD, end=True)
            meet(dve, "dve", met_n)

            for k in range(EARLY, KB):
                low((a_hi[:, k, :], a_lo[:, k, :]), k, y2_f[:, k, :], "y2", k + 1)
            for n in range(KB):
                u = U_OUT2 + n
                if n in (0, 2):
                    dve.wait_ge(x_returned[n // 2], 16)
                dve.wait_ge(tile_done, T_OUT2 + n + 1)
                dve.scalar_tensor_tensor(x_res[:, n, :], x_res[:, n, :], ALPHA, dense[:, u % 2, :], ALU.mult, ALU.add
                                         ).then_inc(sums_free[u % 2], 1)

            def layer_norm(gain, which):
                norm_n["sum"] += 1
                dve.wait_ge(sum_ready, norm_n["sum"])
                for k in range(KB):
                    dve.scalar_tensor_tensor(x_res[:, k, :], side[:, 1, :], -1.0 / D, x_res[:, k, :], ALU.mult, ALU.add
                                             ).then_inc(centred, 1)
                inverse_std(TB)
                for k in range(KB + 1):
                    if k < KB:
                        if k >= 3:
                            dve.wait_ge(shifted, norm_n["shift"] + k - 2)
                        dve.scalar_tensor_tensor(third(k), x_res[:, k, :], par(gain, k), side[:, 1, :], ALU.mult, ALU.mult
                                                 ).then_inc(scaled, 1)
                    if k and which is not None:
                        m = k - 1
                        low((a_hi[:, m, :], a_lo[:, m, :]), m, x_res[:, m, :], which, m + 1)
                        dve.drain()
                        dve.tensor_scalar(x_res[:, m, :], x_res[:, m, :], ALPHA, None, ALU.mult)
                norm_n["shift"] += KB

            layer_norm("ln1_g", "x3")

            def squared_relu(i):
                for f in range(FG):
                    u = U_FF2 + f
                    dve.wait_ge(tile_done, i * FF2_TILES + (T_FF2 + f + 1))
                    dve.tensor_scalar(T[:, f, :], dense[:, u % 2, :], 0.0, None, ALU.max)
                    dve.drain()
                    dve.tensor_tensor(T[:, f, :], dense[:, u % 2, :], T[:, f, :], ALU.mult).then_inc(squared, 1)
                    dve.drain().then_inc(sums_free[u % 2], 1)
                    dve.wait_ge(parts["hidden2"][0], i * FG + (f + 1))
                    dve.tensor_tensor(b_lo[:, f, :], T[:, f, :], b_hi[:, f, :].bitcast(F32), ALU.subtract
                                      ).then_inc(parts["hidden2"][1], 1)
                down(i, T_FF2 + FG, U_FF2 + FG, FF2_TILES, 12 + FULL * KB // 2 + KB // 2)

            repeat(dve, FF2_GROUPS, squared_relu)
            layer_norm("ln2_g", None)
            meet(dve, "dve", met_n)


def blocks_of(w, rows, cols):
    return np.stack([w[r][:, cols] for r in rows], axis=1)


def pack(x):
    tiles = np.zeros((TILES, P, KB, P), np.float32)
    n = [0]

    def put(*parts):
        at = 0
        for w, rows, cols in parts:
            b = blocks_of(w, rows, cols)
            tiles[n[0], :, at:at + b.shape[1], :b.shape[2]] = b
            at += b.shape[1]
        n[0] += 1

    def rows(*ks):
        return [slice(P * k, P * k + P) for k in ks]

    full = rows(*range(KB))
    w = x["w_in"][0]
    off = np.cumsum([0, 384, 128, 128, 256, 32, 8, CONV, CONV, CONV, 256])
    o_q, o_k, o_v, o_qi, o_ki, _, o_bg, o_cg, o_u, o_qc, o_gate = off

    def cols(o, j=0):
        return slice(o + P * j, o + P * j + P)

    put((w, full, slice(o_ki, o_ki + IDX_D + IDX_H)))
    for j in range(2):
        put((w, full, cols(o_qi, j)))
    put((w, full, cols(o_k)))
    two = [np.r_[HD * j:HD * j + HD, HD * (j + 3):HD * (j + 3) + HD] for j in range(3)]
    for j in range(3):
        put((w, full, o_q + two[j]))
    put((w, full, cols(o_v)))
    for j in range(4):
        put((x["w_mem_kv"][0], full, cols(0, j)))
    for j in range(2):
        put((w, full, cols(o_qc, j)))
    for j in range(3):
        for o in (o_cg, o_u, o_bg):
            put((w, full, cols(o, j)))
    for j in range(KB):
        for b in range(3):
            put((w, full, cols(o_gate + D * b, j)))
        put((x["w_conv_out"][0], rows(0, 1, 2), cols(0, j)), (x["w_mem_out"][0], rows(0, 1), cols(0, j)))
    for j in range(0, KB, 2):
        put((x["w_att_out"][0], two, cols(0, j)), (x["w_att_out"][0], two, cols(0, j + 1)))
    for j in range(KB):
        put((x["w_o"][0], full, cols(0, j)))
    for f0 in range(0, FB, FG):
        if f0 == FULL * FG:
            for j in range(4):
                put((x["w_mem_kv_2"][0], full, cols(0, j)))
        group = range(f0, min(FB, f0 + FG))
        for f in group:
            put((x["w_up"][0], full, cols(0, f)))
            put((x["w_up"][0], full, cols(FF, f)))
        for j in range(0, KB, 2):
            put((x["w_down"][0], rows(*group), cols(0, j)), (x["w_down"][0], rows(*group), cols(0, j + 1)))
    w = x["w_in_sb_2"][0]
    o_k, o_v, o_qc = SB_H * HD, 2 * SB_H * HD, 3 * SB_H * HD
    for j in range(2):
        put((w, full, cols(o_qc, j)))
    for j in range(SB_H // 2):
        for o in (0, o_k, o_v):
            put((w, full, cols(o, j)))
    for j in range(KB):
        put((x["w_out_2"][0], full, cols(0, j)))
    for f0 in range(0, FB2, FG):
        group = range(f0, f0 + FG)
        for f in group:
            put((x["w_up_2"][0], full, cols(0, f)))
        for j in range(0, KB, 2):
            put((x["w_down_2"][0], rows(*group), cols(0, j)), (x["w_down_2"][0], rows(*group), cols(0, j + 1)))
    assert n[0] == TILES
    return tiles.reshape(TILES, P, D)


def constants():
    r = np.arange(P)
    c = {"ident": np.eye(P), "ones": np.ones((P, P))}

    def partner(d, half):
        return np.where(d % (8 * half) < half, d + half, d - half)

    def swap(half):
        m = np.zeros((P, P))
        turn = r[r % (8 * half) < 2 * half]
        m[partner(turn, half), turn] = 1
        return m

    c["swap_att"], c["swap_idx"] = swap(8), swap(4)
    c["rep_ki"] = (r[:, None] == r[None, :] % IDX_D).astype(float)
    c["rep_swap_ki"] = c["swap_idx"][:, r % IDX_D] * (r[:, None] < IDX_D)
    c["causal_q"] = np.where(r[None, :] <= r[:, None], 0.0, NEG)
    c["strict_add"] = np.where(r[:, None] < r[None, :], 0.0, NEG)
    c["neg_later"] = -(r[:, None] >= r[None, :]).astype(float)
    c["neg_earlier"] = -(r[:, None] < r[None, :]).astype(float)
    same, to = r[:, None] % IDX_D == np.arange(STACK)[None, :] % IDX_D, np.arange(STACK)[None, :] // IDX_D
    c["stack_mats"] = np.concatenate([same * np.isin(to, g) for g in ((0, 1), (2,), (0, 2), (1,))], axis=1)
    tab = np.zeros((P, 4, S), np.float32)
    for n, half in ((0, 4), (2, 8)):
        freq = np.float32(500000.0) ** (-np.arange(half, dtype=np.float32) / np.float32(half))
        ang = np.arange(S, dtype=np.float32)[:, None] * freq.astype(np.float32)[None, :]
        d = r % (8 * half)
        on = d < 2 * half
        tab[:, n] = np.where(on[:, None], np.cos(ang).T[d % half], 1.0)
        tab[:, n + 1] = np.where(on[:, None], np.where(d < half, -1.0, 1.0)[:, None] * np.sin(ang).T[d % half], 0.0)
    c = {k: np.ascontiguousarray(v, np.float32) for k, v in c.items()}
    c["rope_tab"] = tab
    return c


def small_params(x):
    s = np.zeros((P, SMALL_N), np.float32)

    def put(name, a):
        s[:, SMALL[name]:SMALL[name] + a.shape[1]] = a

    def by_block(v):
        return v.reshape(-1, P).T

    for name, src in (("g_mix", "g_mix"), ("g_mem", "g_mem"), ("g_ffn", "g_ffn"), ("ln1_g", "ln_mix_g_2"),
                      ("ln1_b", "ln_mix_b_2"), ("ln2_g", "ln_ffn_g_2"), ("ln2_b", "ln_ffn_b_2")):
        put(name, by_block(x[src][0]))
    put("g_final", by_block(x["g_final"]))
    put("b_gate", x["b_gate"][0].reshape(3, KB, P).transpose(2, 1, 0).reshape(P, 3 * KB))
    put("taps_short", x["conv_w_short"][0].reshape(3, 3, P).transpose(2, 1, 0).reshape(P, 9))
    put("taps_ff", x["conv_w_ffn"][0].reshape(3, 2, FB, P).transpose(3, 2, 1, 0).reshape(P, 6 * FB))
    for h in range(IDX_H):
        s[IDX_D + h, SMALL["pick_wi"] + h] = IDX_SCALE
    return s


def kernel(**inputs):
    import concourse.bacc as bacc
    from concourse.bass_utils import run_bass_kernel_spmd

    x = {k: np.asarray(v) for k, v in inputs.items()}

    def turned(a):
        return np.ascontiguousarray(a[0].reshape(-1, KB, P).transpose(2, 1, 0))

    arrays = {"x_t": turned(x["x"]), "mem_t": turned(x["mem"]), "mem2_t": turned(x["mem_2"]), "w_stream": pack(x),
              "small": small_params(x), **constants()}
    nc = bacc.Bacc("TRN2", target_bir_lowering=False, num_devices=1, dynamic_dma_scratch_size=1024)
    io = {k: nc.dram_tensor("in_" + k, a.shape, F32, kind="ExternalInput").ap() for k, a in arrays.items()}
    out = nc.dram_tensor("out_t", (P, KB, S), F32, kind="ExternalOutput").ap()
    build(nc, io, out)
    r = run_bass_kernel_spmd(nc, [{"in_" + k: a for k, a in arrays.items()}], core_ids=[0])
    y = r.results[0]["out_t"]
    return np.ascontiguousarray(y.transpose(2, 1, 0).reshape(1, S, D))
```
